# Optimizing a Trainium2 kernel written in Bass

```python
import jax, jax.numpy as jnp
from jax import lax
import numpy as np

D_MODEL = 1024
BATCH = 1
SEQ = 256
DEPTH = 2

GRID_W = 64
CTX_LEN = 256
N_EVEN = (DEPTH + 1) // 2
N_ODD = DEPTH // 2
H_A = 4
DK_A = 128
DV_A = 128
H_B = 4
DK_B = 64
DV_B = 128
CONV_W = 3
CHUNK = 32
MIX_W = H_A * DV_A + H_B * DV_B
N_HEADS_C = 8
N_KV_C = 2
GROUP_C = N_HEADS_C // N_KV_C
HEAD_DIM = 128
AXIS_DIM = HEAD_DIM // 2
Q_BLOCK = 128
ROPE_THETA = 10000.0
D_QKV_C = (N_HEADS_C + 2 * N_KV_C) * HEAD_DIM
D_FF = ((8 * D_MODEL // 3 + 255) // 256) * 256
AB_SPLIT = (H_A * DK_A, H_A * DV_A, H_A * DV_A, H_A * DK_A, H_A * DK_A,
            2 * H_B * DK_B, H_B * DV_B, H_B * DV_B, 4 * H_B)
D_AB_IN = sum(AB_SPLIT)


def rmsnorm(x, g, eps=1e-6):
    xf = x.astype(jnp.float32)
    y = xf * lax.rsqrt(jnp.mean(xf * xf, axis=-1, keepdims=True) + eps)
    return (y * g.astype(jnp.float32)).astype(x.dtype)

def modulate(x, g, shift, scale):
    return rmsnorm(x, g) * (1 + scale) + shift

def ada_params(cvec, w, b):
    return jnp.split(jax.nn.silu(cvec) @ w + b, 6, axis=-1)

def swiglu(h, w_in, w_out):
    g, u = jnp.split(h @ w_in, 2, axis=-1)
    return (jax.nn.silu(g) * u) @ w_out

def conv_centred(x, w):
    return lax.conv_general_dilated(x, w[:, None, :], window_strides=(1,),
                                    padding=[(CONV_W // 2, CONV_W // 2)],
                                    dimension_numbers=('NWC', 'WIO', 'NWC'),
                                    feature_group_count=x.shape[-1])

def to_chunks(a):
    Bn, T = a.shape[:2]
    return jnp.moveaxis(a.reshape(Bn, T // CHUNK, CHUNK, *a.shape[2:]), 1, 0)

def from_chunks(a):
    nc, Bn, C = a.shape[:3]
    return jnp.moveaxis(a, 0, 1).reshape(Bn, nc * C, *a.shape[3:])

def hgrn2_chunk_scan(q, k, v, logf, state0):
    f32 = jnp.float32
    mask = jnp.tril(jnp.ones((CHUNK, CHUNK), bool))

    def step(S, xs):
        qc, kc, vc, fc = xs
        b = jnp.cumsum(fc, axis=1)
        b_mid = b[:, CHUNK // 2 - 1:CHUNK // 2]
        b_last = b[:, -1:]
        A = jnp.einsum('bthd,bshd->bhts', qc * jnp.exp(b - b_mid), kc * jnp.exp(b_mid - b))
        A = jnp.where(mask, A, 0.0)
        o = (jnp.einsum('bhts,bshe->bthe', A, vc)
             + jnp.einsum('bthd,bhde->bthe', qc * jnp.exp(b), S))
        S_new = (S * jnp.exp(b_last[:, 0])[..., None]
                 + jnp.einsum('bshd,bshe->bhde', kc * jnp.exp(b_last - b), vc))
        return S_new, o

    xs = tuple(to_chunks(a.astype(f32)) for a in (q, k, v, logf))
    S_fin, o = lax.scan(step, state0, xs)
    return from_chunks(o).astype(v.dtype), S_fin

def mlstm_chunk_scan(q, k, v, ig, logf, state0):
    f32 = jnp.float32
    mask = jnp.tril(jnp.ones((CHUNK, CHUNK), bool))

    def step(carry, xs):
        C, n, m = carry
        qc, kc, vc, igc, fc = xs
        bh = jnp.swapaxes(jnp.cumsum(fc, axis=1), 1, 2)
        igh = jnp.swapaxes(igc, 1, 2)
        D = jnp.where(mask, bh[..., :, None] - bh[..., None, :] + igh[..., None, :], -jnp.inf)
        m_inter = bh + m[..., None]
        m_t = jnp.maximum(D.max(-1), m_inter)
        S = jnp.einsum('bthd,bshd->bhts', qc, kc) * jnp.exp(D - m_t[..., None])
        w_inter = jnp.exp(m_inter - m_t)
        num = (jnp.einsum('bhts,bshe->bthe', S, vc)
               + jnp.swapaxes(w_inter, 1, 2)[..., None] * jnp.einsum('bthd,bhde->bthe', qc, C))
        den = S.sum(-1) + w_inter * jnp.einsum('bthd,bhd->bht', qc, n)
        h = num / jnp.swapaxes(jnp.maximum(jnp.abs(den), jnp.exp(-m_t)), 1, 2)[..., None]
        b_last = bh[..., -1]
        g = b_last[..., None] - bh + igh
        m_new = jnp.maximum(b_last + m, g.max(-1))
        wk = jnp.exp(g - m_new[..., None])
        decay = jnp.exp(b_last + m - m_new)
        C_new = decay[..., None, None] * C + jnp.einsum('bhs,bshd,bshe->bhde', wk, kc, vc)
        n_new = decay[..., None] * n + jnp.einsum('bhs,bshd->bhd', wk, kc)
        return (C_new, n_new, m_new), h

    xs = tuple(to_chunks(a.astype(f32)) for a in (q, k, v, ig, logf))
    state_fin, h = lax.scan(step, state0, xs)
    return from_chunks(h).astype(v.dtype), state_fin

def bidirectional_prefix(scan_fn, ctx_dirs, lat_dirs, state0):
    outs_c, outs_l = [], []
    for d, reverse in enumerate((False, True)):
        flip = (lambda a: jnp.flip(a, axis=1)) if reverse else (lambda a: a)
        o_c, st = scan_fn(*[flip(a) for a in ctx_dirs[d]], state0)
        o_l, _ = scan_fn(*[flip(a) for a in lat_dirs[d]], st)
        outs_c.append(flip(o_c))
        outs_l.append(flip(o_l))
    return outs_c[0] + outs_c[1], outs_l[0] + outs_l[1]

def mixer_ab(h_ctx, h_lat, w_in, conv_w, gate_b, lb, out_g, w_out, need_ctx):
    f32 = jnp.float32
    split_idx = [int(s) for s in np.cumsum(AB_SPLIT)[:-1]]

    def prep(h):
        Bn, T = h.shape[:2]
        aq, ai, ag, aff, afb, bqk, bv, bo, bg = jnp.split(h @ w_in, split_idx, axis=-1)
        z = jnp.stack([aff, afb], 0).astype(f32).reshape(2, Bn, T, H_A, DK_A)
        lbh = lb[:, None, None]
        logf_a = jnp.log(lbh + (1 - lbh) * jax.nn.sigmoid(z))
        k_a = (1 - lbh) * jax.nn.sigmoid(-z)
        q_a = aq.reshape(Bn, T, H_A, DK_A)
        v_a = ai.reshape(Bn, T, H_A, DV_A)
        q_b, k_b = jnp.split(jax.nn.silu(conv_centred(bqk, conv_w)), 2, axis=-1)
        q_b = q_b.reshape(Bn, T, H_B, DK_B) * (DK_B ** -0.5)
        k_b = k_b.reshape(Bn, T, H_B, DK_B)
        v_b = bv.reshape(Bn, T, H_B, DV_B)
        gates = bg.astype(f32).reshape(Bn, T, 4, H_B) + gate_b.astype(f32)
        ig_b = gates[:, :, 0::2]
        logf_b = jax.nn.log_sigmoid(gates[:, :, 1::2])
        hgrn_dirs = [(q_a, k_a[d], v_a, logf_a[d]) for d in range(2)]
        mlstm_dirs = [(q_b, k_b, v_b, ig_b[:, :, d], logf_b[:, :, d]) for d in range(2)]
        gate = jnp.concatenate([jax.nn.silu(ag), jax.nn.sigmoid(bo)], axis=-1)
        return hgrn_dirs, mlstm_dirs, gate

    ha_c, hb_c, gate_c = prep(h_ctx)
    ha_l, hb_l, gate_l = prep(h_lat)
    Bn = h_lat.shape[0]
    s0_a = jnp.zeros((Bn, H_A, DK_A, DV_A), f32)
    s0_b = (jnp.zeros((Bn, H_B, DK_B, DV_B), f32), jnp.zeros((Bn, H_B, DK_B), f32),
            jnp.zeros((Bn, H_B), f32))
    oa_c, oa_l = bidirectional_prefix(hgrn2_chunk_scan, ha_c, ha_l, s0_a)
    ob_c, ob_l = bidirectional_prefix(mlstm_chunk_scan, hb_c, hb_l, s0_b)

    def out(oa, ob, gate):
        o = jnp.concatenate([oa, ob], axis=2)
        o = rmsnorm(o, out_g.reshape(H_A + H_B, DV_A)).reshape(*o.shape[:2], MIX_W)
        return (o * gate) @ w_out

    y_lat = out(oa_l, ob_l, gate_l)
    y_ctx = out(oa_c, ob_c, gate_c) if need_ctx else None
    return y_ctx, y_lat

def axial_rope_angles(T):
    rows = T // GRID_W
    r, col = jnp.meshgrid(jnp.arange(rows, dtype=jnp.float32),
                          jnp.arange(GRID_W, dtype=jnp.float32), indexing='ij')
    inv = jnp.power(ROPE_THETA, -jnp.arange(0, AXIS_DIM, 2, dtype=jnp.float32) / AXIS_DIM)
    return jnp.stack([r.reshape(-1)[:, None] * inv, col.reshape(-1)[:, None] * inv], axis=1)

def rope2d(x, ang):
    Bn, T, H, _ = x.shape
    xf = x.astype(jnp.float32).reshape(Bn, T, H, 2, AXIS_DIM)
    x1, x2 = xf[..., :AXIS_DIM // 2], xf[..., AXIS_DIM // 2:]
    cos, sin = jnp.cos(ang)[None, :, None], jnp.sin(ang)[None, :, None]
    out = jnp.concatenate([x1 * cos - x2 * sin, x2 * cos + x1 * sin], axis=-1)
    return out.reshape(Bn, T, H, HEAD_DIM).astype(x.dtype)

def attend(q, k, v):
    s = jnp.einsum('bqhgd,bkhd->bhgqk', q, k).astype(jnp.float32)
    p = jax.nn.softmax(s, axis=-1).astype(v.dtype)
    return jnp.einsum('bhgqk,bkhd->bqhgd', p, v)

def blocked_attention(q, k, v):
    Bn, T = q.shape[:2]
    qb = jnp.moveaxis(q.reshape(Bn, T // Q_BLOCK, Q_BLOCK, *q.shape[2:]), 1, 0)
    o = lax.map(lambda qi: attend(qi, k, v), qb)
    return jnp.moveaxis(o, 0, 1).reshape(Bn, T, N_HEADS_C * HEAD_DIM)

def mixer_c(h_ctx, h_lat, w_qkv, qk_g, w_out, ang, need_ctx):
    def prep(h, use_rope):
        Bn, T = h.shape[:2]
        q, k, v = jnp.split(h @ w_qkv, [N_HEADS_C * HEAD_DIM, (N_HEADS_C + N_KV_C) * HEAD_DIM], axis=-1)
        q = rmsnorm(q.reshape(Bn, T, N_HEADS_C, HEAD_DIM), qk_g[0])
        k = rmsnorm(k.reshape(Bn, T, N_KV_C, HEAD_DIM), qk_g[1])
        v = v.reshape(Bn, T, N_KV_C, HEAD_DIM)
        if use_rope:
            q, k = rope2d(q, ang), rope2d(k, ang)
        q = q.reshape(Bn, T, N_KV_C, GROUP_C, HEAD_DIM) * (HEAD_DIM ** -0.5)
        return q, k, v

    q_c, k_c, v_c = prep(h_ctx, False)
    q_l, k_l, v_l = prep(h_lat, True)
    k_all = jnp.concatenate([k_c, k_l], axis=1)
    v_all = jnp.concatenate([v_c, v_l], axis=1)
    y_lat = blocked_attention(q_l, k_all, v_all) @ w_out
    y_ctx = None
    if need_ctx:
        Bn, Tc = h_ctx.shape[:2]
        y_ctx = attend(q_c, k_c, v_c).reshape(Bn, Tc, N_HEADS_C * HEAD_DIM) @ w_out
    return y_ctx, y_lat

def first_inputs(seed: int = 0) -> dict:
    key = jax.random.key(seed)
    ks = jax.random.split(key, 20)
    f32 = jnp.float32

    def nrm(k, shape, s):
        return jax.random.normal(k, shape, f32) * s

    ig_b = nrm(ks[11], (N_EVEN, 2, H_B), 0.01)
    fg_b = jnp.linspace(3.0, 6.0, H_B, dtype=f32) + nrm(ks[12], (N_EVEN, 2, H_B), 0.01)
    return {
        "x": nrm(ks[0], (BATCH, SEQ, D_MODEL), 1.0),
        "c": nrm(ks[1], (BATCH, D_MODEL), 1.0),
        "ctx": nrm(ks[2], (BATCH, CTX_LEN, D_MODEL), 1.0),
        "c_ctx": nrm(ks[3], (D_MODEL,), 1.0),
        "ada_w": nrm(ks[4], (DEPTH, D_MODEL, 6 * D_MODEL), 0.5 * D_MODEL ** -0.5),
        "ada_b": nrm(ks[5], (DEPTH, 6 * D_MODEL), 0.02),
        "norm_g": 1.0 + nrm(ks[6], (DEPTH, 4, D_MODEL), 0.02),
        "ffn_w_in": nrm(ks[7], (DEPTH, D_MODEL, 2 * D_FF), D_MODEL ** -0.5),
        "ffn_w_out": nrm(ks[8], (DEPTH, D_FF, D_MODEL), D_FF ** -0.5),
        "ab_w_in": nrm(ks[9], (N_EVEN, D_MODEL, D_AB_IN), D_MODEL ** -0.5),
        "ab_conv": nrm(ks[10], (N_EVEN, CONV_W, 2 * H_B * DK_B), CONV_W ** -0.5),
        "ab_gate_b": jnp.stack([ig_b, fg_b], axis=2).reshape(N_EVEN, 4, H_B),
        "hgrn_lb": nrm(ks[13], (2, DEPTH + 1, H_A * DK_A), 0.1),
        "ab_out_g": 1.0 + nrm(ks[14], (N_EVEN, MIX_W), 0.02),
        "ab_w_out": nrm(ks[15], (N_EVEN, MIX_W, D_MODEL), MIX_W ** -0.5),
        "attn_w_qkv": nrm(ks[16], (N_ODD, D_MODEL, D_QKV_C), D_MODEL ** -0.5),
        "attn_qk_g": 1.0 + nrm(ks[17], (N_ODD, 2, HEAD_DIM), 0.02),
        "attn_w_out": nrm(ks[18], (N_ODD, N_HEADS_C * HEAD_DIM, D_MODEL), (N_HEADS_C * HEAD_DIM) ** -0.5),
    }

def first_block(x, c, ctx, c_ctx, ada_w, ada_b, norm_g, ffn_w_in, ffn_w_out, ab_w_in, ab_conv,
              ab_gate_b, hgrn_lb, ab_out_g, ab_w_out, attn_w_qkv, attn_qk_g, attn_w_out):
    T = x.shape[1]
    ang = axial_rope_angles(T)
    lb_all = jnp.cumsum(jax.nn.softmax(hgrn_lb.astype(jnp.float32), axis=1), axis=1)
    for l in range(DEPTH):
        need_ctx = l < DEPTH - 1
        sh1, sc1, g1, sh2, sc2, g2 = [a[:, None, :] for a in ada_params(c, ada_w[l], ada_b[l])]
        csh1, csc1, cg1, csh2, csc2, cg2 = ada_params(c_ctx, ada_w[l], ada_b[l])
        h_lat = modulate(x, norm_g[l, 0], sh1, sc1)
        h_ctx = modulate(ctx, norm_g[l, 0], csh1, csc1)
        if l % 2 == 0:
            e = l // 2
            y_ctx, y_lat = mixer_ab(h_ctx, h_lat, ab_w_in[e], ab_conv[e], ab_gate_b[e],
                                    lb_all[:, l].reshape(2, H_A, DK_A), ab_out_g[e], ab_w_out[e],
                                    need_ctx)
        else:
            o = l // 2
            y_ctx, y_lat = mixer_c(h_ctx, h_lat, attn_w_qkv[o], attn_qk_g[o], attn_w_out[o], ang,
                                   need_ctx)
        x = x + g1 * rmsnorm(y_lat, norm_g[l, 1])
        x = x + g2 * rmsnorm(swiglu(modulate(x, norm_g[l, 2], sh2, sc2), ffn_w_in[l], ffn_w_out[l]),
                             norm_g[l, 3])
        if need_ctx:
            ctx = ctx + cg1 * rmsnorm(y_ctx, norm_g[l, 1])
            ctx = ctx + cg2 * rmsnorm(swiglu(modulate(ctx, norm_g[l, 2], csh2, csc2), ffn_w_in[l],
                                             ffn_w_out[l]), norm_g[l, 3])
    return x


CHUNK_2 = 64
N_MIXERS = 2
N_CONV_LAYERS = (DEPTH + 1) // 2
N_GDN_LAYERS = DEPTH // 2
CONV_WIDTH = 3
GDN_HEADS = 8
GDN_HEAD_DIM = D_MODEL // GDN_HEADS
GDN_QK_DIM = GDN_HEADS * GDN_HEAD_DIM
GDN_V_DIM = GDN_HEADS * GDN_HEAD_DIM
GDN_CONV_WIDTH = 4
GDN_IN_DIM = 2 * GDN_QK_DIM + 2 * GDN_V_DIM + 2 * GDN_HEADS
N_GROUPS = 8
EXPERTS_PER_GROUP = 8
N_EXPERTS = N_GROUPS * EXPERTS_PER_GROUP
TOP_K = 2
D_EXPERT = D_MODEL // 4
D_SHARED = D_MODEL // 2
MOE_BLOCK = 128
NORM_EPS = 1e-6


def rmsnorm_2(x, w):
    xf = x.astype(jnp.float32)
    y = xf * lax.rsqrt(jnp.mean(xf * xf, axis=-1, keepdims=True) + NORM_EPS)
    return (y * w.astype(jnp.float32)).astype(x.dtype)

def l2norm(x):
    xf = x.astype(jnp.float32)
    return xf * lax.rsqrt(jnp.sum(xf * xf, axis=-1, keepdims=True) + NORM_EPS)

def causal_dwconv(x, w):
    K = w.shape[0]
    T = x.shape[1]
    xp = jnp.pad(x, ((0, 0), (K - 1, 0), (0, 0)))
    y = xp[:, 0:T] * w[0]
    for k in range(1, K):
        y = y + xp[:, k:k + T] * w[k]
    return y

def short_conv_mixer(h, w_in, conv_w, w_out):
    bcx = h @ w_in
    b, cg, xv = jnp.split(bcx, 3, axis=-1)
    y = b * causal_dwconv(cg * xv, conv_w)
    return y @ w_out

def chunk_gated_delta_rule(q, k, v, g, beta):
    out_dtype = v.dtype
    B, T, H, Dk = q.shape
    Dv = v.shape[-1]
    n = T // CHUNK_2

    def blocks(a):
        a = a.astype(jnp.float32).reshape((B, n, CHUNK_2, H) + a.shape[3:])
        return jnp.moveaxis(a, 3, 1)

    q, k, v, g, beta = (blocks(a) for a in (q, k, v, g, beta))
    gc = jnp.cumsum(g, axis=-1)
    idx = jnp.arange(CHUNK_2)
    causal = idx[:, None] >= idx[None, :]
    strict = idx[:, None] > idx[None, :]
    diff = gc[..., :, None] - gc[..., None, :]
    decay = jnp.exp(jnp.where(causal, diff, -jnp.inf))
    kb = k * beta[..., None]
    lower = jnp.where(strict, jnp.einsum('bhncd,bhnsd->bhncs', kb, k) * decay, 0.0)
    rhs = jnp.concatenate([v * beta[..., None], kb * jnp.exp(gc)[..., None]], axis=-1)
    sol = lax.linalg.triangular_solve(lower, rhs, left_side=True, lower=True,
                                      unit_diagonal=True)
    u, w = sol[..., :Dv], sol[..., Dv:]
    attn = jnp.einsum('bhncd,bhnsd->bhncs', q, k) * decay
    q_dec = q * jnp.exp(gc)[..., None]
    g_last = gc[..., -1]
    k_dec = k * jnp.exp(g_last[..., None] - gc)[..., None]

    def step(S, inp):
        u_n, w_n, qd_n, kd_n, a_n, gl_n = inp
        v_new = u_n - jnp.einsum('bhcd,bhde->bhce', w_n, S)
        o_n = (jnp.einsum('bhcd,bhde->bhce', qd_n, S)
               + jnp.einsum('bhcs,bhse->bhce', a_n, v_new))
        S = S * jnp.exp(gl_n)[..., None, None] + jnp.einsum('bhcd,bhce->bhde', kd_n, v_new)
        return S, o_n

    xs = tuple(jnp.moveaxis(a, 2, 0) for a in (u, w, q_dec, k_dec, attn, g_last))
    S0 = jnp.zeros((B, H, Dk, Dv), jnp.float32)
    _, o = lax.scan(step, S0, xs)
    o = jnp.transpose(o, (1, 0, 3, 2, 4)).reshape(B, T, H, Dv)
    return o.astype(out_dtype)

def gated_deltanet_mixer(h, w_in, conv_w, a_log, dt_bias, norm_w, w_out):
    B, T, _ = h.shape
    H, Dh = GDN_HEADS, GDN_HEAD_DIM
    proj = h @ w_in
    s1 = 2 * GDN_QK_DIM + GDN_V_DIM
    s2 = s1 + GDN_V_DIM
    qkv = proj[..., :s1]
    z = proj[..., s1:s2]
    b = proj[..., s2:s2 + H]
    a = proj[..., s2 + H:]
    qkv = jax.nn.silu(causal_dwconv(qkv, conv_w))
    q = qkv[..., :GDN_QK_DIM].reshape(B, T, H, Dh)
    k = qkv[..., GDN_QK_DIM:2 * GDN_QK_DIM].reshape(B, T, H, Dh)
    v = qkv[..., 2 * GDN_QK_DIM:].reshape(B, T, H, Dh)
    q = l2norm(q) * (Dh ** -0.5)
    k = l2norm(k)
    beta = jax.nn.sigmoid(b.astype(jnp.float32))
    g = -jnp.exp(a_log.astype(jnp.float32)) * jax.nn.softplus(
        a.astype(jnp.float32) + dt_bias.astype(jnp.float32))
    o = chunk_gated_delta_rule(q, k, v, g, beta)
    o = rmsnorm_2(o, norm_w) * jax.nn.silu(z.reshape(B, T, H, Dh))
    return o.reshape(B, T, GDN_V_DIM) @ w_out

def hier_moe(h, w_rg, b_rg, w_re, b_re, w_gate, w_up, w_down, ws_gate, ws_up, ws_down, w_sg):
    B, T, D = h.shape
    xt = h.reshape(-1, D)
    N = xt.shape[0]
    gl = (xt @ w_rg + b_rg).astype(jnp.float32)
    gp = jax.nn.softmax(gl, axis=-1)
    g_sel = jnp.argmax(gl, axis=-1)
    p_sel = jnp.take_along_axis(gp, g_sel[:, None], axis=-1)[:, 0]
    el = (xt @ w_re + b_re).astype(jnp.float32).reshape(N, N_GROUPS, EXPERTS_PER_GROUP)
    el_sel = jnp.take_along_axis(el, g_sel[:, None, None], axis=1)[:, 0]
    top_v, top_i = lax.top_k(el_sel, TOP_K)
    gate = jax.nn.softmax(top_v, axis=-1) * p_sel[:, None]
    eid = g_sel[:, None] * EXPERTS_PER_GROUP + top_i
    S = N * TOP_K
    flat_e = eid.reshape(-1)
    flat_tok = jnp.repeat(jnp.arange(N), TOP_K)
    flat_gate = gate.reshape(-1)
    order = jnp.argsort(flat_e)
    e_sorted = flat_e[order]
    tok_sorted = flat_tok[order]
    gate_sorted = flat_gate[order].astype(xt.dtype)
    counts = jnp.bincount(flat_e, length=N_EXPERTS)
    starts = jnp.cumsum(counts) - counts
    padded = (counts + MOE_BLOCK - 1) // MOE_BLOCK * MOE_BLOCK
    pends = jnp.cumsum(padded)
    pstarts = pends - padded
    dest = pstarts[e_sorted] + (jnp.arange(S) - starts[e_sorted])
    n_blocks = -(-S // MOE_BLOCK) + N_EXPERTS
    P = n_blocks * MOE_BLOCK
    buf = jnp.zeros((P, D), xt.dtype).at[dest].set(xt[tok_sorted])
    block_e = jnp.minimum(
        jnp.searchsorted(pends, jnp.arange(n_blocks) * MOE_BLOCK, side='right'), N_EXPERTS - 1)

    def expert_block(args):
        xb, e = args
        hid = jax.nn.silu(xb @ w_gate[e]) * (xb @ w_up[e])
        return hid @ w_down[e]

    out = lax.map(expert_block, (buf.reshape(n_blocks, MOE_BLOCK, D), block_e)).reshape(P, D)
    y = jnp.zeros((N, D), xt.dtype).at[tok_sorted].add(out[dest] * gate_sorted[:, None])
    ys = (jax.nn.silu(xt @ ws_gate) * (xt @ ws_up)) @ ws_down
    y = y + jax.nn.sigmoid(xt @ w_sg) * ys
    return y.reshape(B, T, D)

def second_inputs(seed: int = 0) -> dict:
    key = jax.random.key(seed)
    ks = jax.random.split(key, 32)
    D = D_MODEL
    nrm = jax.random.normal
    f32 = jnp.float32
    dt = jnp.exp(jax.random.uniform(ks[11], (N_GDN_LAYERS, GDN_HEADS), f32,
                                    np.log(1e-3), np.log(1e-1)))
    return {
        "x": nrm(ks[0], (BATCH, SEQ, D), f32),
        "c": nrm(ks[1], (BATCH, D), f32),
        "ada_w": nrm(ks[2], (DEPTH, D, 6 * D), f32) * (0.3 * D ** -0.5),
        "ada_b": nrm(ks[3], (DEPTH, 6 * D), f32) * 0.02,
        "norm_w": 1.0 + 0.05 * nrm(ks[4], (DEPTH, 4, D), f32),
        "conv_in_w": nrm(ks[5], (N_CONV_LAYERS, D, 3 * D), f32) * D ** -0.5,
        "conv_w": nrm(ks[6], (N_CONV_LAYERS, CONV_WIDTH, D), f32) * CONV_WIDTH ** -0.5,
        "conv_out_w": nrm(ks[7], (N_CONV_LAYERS, D, D), f32) * D ** -0.5,
        "gdn_in_w": nrm(ks[8], (N_GDN_LAYERS, D, GDN_IN_DIM), f32) * D ** -0.5,
        "gdn_conv_w": nrm(ks[9], (N_GDN_LAYERS, GDN_CONV_WIDTH, 2 * GDN_QK_DIM + GDN_V_DIM), f32) * 0.5,
        "gdn_a_log": jnp.log(jax.random.uniform(ks[10], (N_GDN_LAYERS, GDN_HEADS), f32, 1.0, 16.0)),
        "gdn_dt_bias": dt + jnp.log(-jnp.expm1(-dt)),
        "gdn_norm_w": 1.0 + 0.05 * nrm(ks[12], (N_GDN_LAYERS, GDN_HEAD_DIM), f32),
        "gdn_out_w": nrm(ks[13], (N_GDN_LAYERS, GDN_V_DIM, D), f32) * GDN_V_DIM ** -0.5,
        "moe_group_w": nrm(ks[14], (DEPTH, D, N_GROUPS), f32) * D ** -0.5,
        "moe_group_b": nrm(ks[15], (DEPTH, N_GROUPS), f32) * 0.01,
        "moe_expert_w": nrm(ks[16], (DEPTH, D, N_EXPERTS), f32) * D ** -0.5,
        "moe_expert_b": nrm(ks[17], (DEPTH, N_EXPERTS), f32) * 0.01,
        "moe_w_gate": nrm(ks[18], (DEPTH, N_EXPERTS, D, D_EXPERT), f32) * D ** -0.5,
        "moe_w_up": nrm(ks[19], (DEPTH, N_EXPERTS, D, D_EXPERT), f32) * D ** -0.5,
        "moe_w_down": nrm(ks[20], (DEPTH, N_EXPERTS, D_EXPERT, D), f32) * D_EXPERT ** -0.5,
        "shared_w_gate": nrm(ks[21], (DEPTH, D, D_SHARED), f32) * D ** -0.5,
        "shared_w_up": nrm(ks[22], (DEPTH, D, D_SHARED), f32) * D ** -0.5,
        "shared_w_down": nrm(ks[23], (DEPTH, D_SHARED, D), f32) * D_SHARED ** -0.5,
        "shared_gate_w": nrm(ks[24], (DEPTH, D, 1), f32) * D ** -0.5,
    }

def second_block(x, c, ada_w, ada_b, norm_w, conv_in_w, conv_w, conv_out_w,
              gdn_in_w, gdn_conv_w, gdn_a_log, gdn_dt_bias, gdn_norm_w, gdn_out_w,
              moe_group_w, moe_group_b, moe_expert_w, moe_expert_b,
              moe_w_gate, moe_w_up, moe_w_down,
              shared_w_gate, shared_w_up, shared_w_down, shared_gate_w):
    cs = jax.nn.silu(c)
    for i in range(DEPTH):
        mod = (cs @ ada_w[i] + ada_b[i])[:, None, :]
        sh1, sc1, gt1, sh2, sc2, gt2 = jnp.split(mod, 6, axis=-1)
        h = rmsnorm_2(x, norm_w[i, 0]) * (1.0 + sc1) + sh1
        j = i // N_MIXERS
        if i % N_MIXERS == 0:
            y = short_conv_mixer(h, conv_in_w[j], conv_w[j], conv_out_w[j])
        else:
            y = gated_deltanet_mixer(h, gdn_in_w[j], gdn_conv_w[j], gdn_a_log[j],
                                     gdn_dt_bias[j], gdn_norm_w[j], gdn_out_w[j])
        x = x + gt1 * rmsnorm_2(y, norm_w[i, 1])
        h = rmsnorm_2(x, norm_w[i, 2]) * (1.0 + sc2) + sh2
        y = hier_moe(h, moe_group_w[i], moe_group_b[i], moe_expert_w[i], moe_expert_b[i],
                     moe_w_gate[i], moe_w_up[i], moe_w_down[i],
                     shared_w_gate[i], shared_w_up[i], shared_w_down[i], shared_gate_w[i])
        x = x + gt2 * rmsnorm_2(y, norm_w[i, 3])
    return x


def setup_inputs(seed=0):
    out = dict(first_inputs(seed))
    for name, value in second_inputs(seed + 1).items():
        if name != "x":
            out[name + "_2"] = value
    return out


def reference(
    x, c, ctx, c_ctx, ada_w, ada_b, norm_g, ffn_w_in, ffn_w_out, ab_w_in, ab_conv, ab_gate_b,
    hgrn_lb, ab_out_g, ab_w_out, attn_w_qkv, attn_qk_g, attn_w_out, c_2, ada_w_2, ada_b_2,
    norm_w_2, conv_in_w_2, conv_w_2, conv_out_w_2, gdn_in_w_2, gdn_conv_w_2, gdn_a_log_2,
    gdn_dt_bias_2, gdn_norm_w_2, gdn_out_w_2, moe_group_w_2, moe_group_b_2, moe_expert_w_2,
    moe_expert_b_2, moe_w_gate_2, moe_w_up_2, moe_w_down_2, shared_w_gate_2, shared_w_up_2,
    shared_w_down_2, shared_gate_w_2,
):
    x = first_block(
        x, c, ctx, c_ctx, ada_w, ada_b, norm_g, ffn_w_in, ffn_w_out, ab_w_in, ab_conv,
        ab_gate_b, hgrn_lb, ab_out_g, ab_w_out, attn_w_qkv, attn_qk_g, attn_w_out,
    )
    return second_block(
        x, c_2, ada_w_2, ada_b_2, norm_w_2, conv_in_w_2, conv_w_2, conv_out_w_2, gdn_in_w_2,
        gdn_conv_w_2, gdn_a_log_2, gdn_dt_bias_2, gdn_norm_w_2, gdn_out_w_2, moe_group_w_2,
        moe_group_b_2, moe_expert_w_2, moe_expert_b_2, moe_w_gate_2, moe_w_up_2, moe_w_down_2,
        shared_w_gate_2, shared_w_up_2, shared_w_down_2, shared_gate_w_2,
    )


_drawn_inputs = setup_inputs


def setup_inputs(seed=0):
    import zlib

    import numpy as np

    out = dict(_drawn_inputs(seed))
    spreads = {}
    factors = {'hgrn_lb': 3.114,
     'ab_out_g': 4.707,
     'attn_qk_g': 8.0,
     'gdn_norm_w_2': 32.196,
     'moe_group_b_2': 4.625,
     'moe_expert_b_2': 13.532}
    for name, (base, spread) in spreads.items():
        noise = np.random.default_rng([zlib.crc32(name.encode()), seed]).standard_normal(out[name].shape)
        drawn = base * np.exp(spread * noise) if base else spread * noise
        out[name] = __import__('jax').numpy.asarray(drawn.astype(out[name].dtype))
    for name, factor in factors.items():
        out[name] = (out[name] * factor).astype(out[name].dtype)
    return out
```

```python
from contextlib import ExitStack

import numpy as np
import concourse.bass as bass
from concourse import mybir

F32 = mybir.dt.float32
ALU = mybir.AluOpType
ACT = mybir.ActivationFunctionType
AX_X = mybir.AxisListType.X

P = 128
D = 1024
KC = D // P
SEQ = 256
NT = 2 * SEQ
D_FF = 2816
EH = 256
NFF = D_FF // EH
SLOTS = 6
UNIT = 2048
HGRN_HEADS = MLSTM_HEADS = 4
SCAN_CHUNK = 32
NSC = NT // SCAN_CHUNK
ATT_HEADS, KV_HEADS = 8, 2
GDN_HEADS = 8
N_GROUPS, PER_GROUP = 8, 8
N_EXPERTS = N_GROUPS * PER_GROUP
EPS = 1e-6
BIG = 1e30
MAXF = 3.0e38
ROWS = 36
GATE_W = 16
ROUTE_W = N_GROUPS + N_EXPERTS + 1
QUAD = 4
CAP = 32
QUADS = N_EXPERTS // QUAD
LEVELS = 7


def shape_constants():
    i = np.arange(P)
    f = np.float32
    c = {}
    c["ident"] = np.eye(P, dtype=f)
    c["s_le_t"] = (i[:, None] <= i[None, :]).astype(f)
    c["s_ge_t"] = (i[:, None] >= i[None, :]).astype(f)
    same = i[:, None] // SCAN_CHUNK == i[None, :] // SCAN_CHUNK
    c["chunk_masks"] = np.stack([c["s_le_t"] * same, c["s_ge_t"] * same], 1).astype(f)
    seg = np.ones((P, NT), f)
    seg[:, ::SCAN_CHUNK] = 0
    c["chunk_starts"] = seg
    sel = np.zeros((ROWS, 8, P), f)
    for d in range(2):
        for h in range(4):
            sel[32 * d + h, 4 * d + h] = 1
    c["row_select"] = sel
    lv = np.zeros((P, LEVELS, P), f)
    for n in range(LEVELS):
        b = 1 << n
        pair = i[:, None] // (2 * b) == i[None, :] // (2 * b)
        lv[:, n] = pair & (i[:, None] % (2 * b) < b) & (i[None, :] % (2 * b) >= b)
    c["levels"] = lv
    c["slot_index"] = np.broadcast_to(np.arange(CAP, dtype=f), (P, CAP)).copy()
    c["round_limits"] = np.broadcast_to(CAP * np.arange(1, SEQ // CAP, dtype=f), (P, SEQ // CAP - 1)).copy()
    t = np.arange(SEQ)
    inv = np.power(f(10000.0), -np.arange(0, 64, 2, dtype=f) / f(64)).astype(f)
    ang = np.stack([(t // 64).astype(f)[:, None] * inv, (t % 64).astype(f)[:, None] * inv], 1)
    rope = np.stack([np.cos(ang), np.sin(ang)], 1).astype(f).reshape(2, P, 2, 64)
    c["rope"] = np.ascontiguousarray(rope.transpose(1, 0, 2, 3))
    return c


class Counts:

    def __init__(self):
        self.block = 0
        self.gu = 0
        self.tp = 0
        self.h = 0
        self.normed = 0
        self.x = 0
        self.pos = 0

    def slots(self, n):
        at = [(self.pos + i) % SLOTS for i in range(n)]
        self.pos += n
        return at

    def align(self):
        self.pos = -(-self.pos // SLOTS) * SLOTS


def build(nc, I, out):
    ctx = ExitStack()
    with ctx:
        def sb(name, shape):
            return ctx.enter_context(nc.sbuf_tensor(name, shape, F32))

        made = {}

        def sem(name):
            if name not in made:
                made[name] = ctx.enter_context(nc.semaphore(name))
            return made[name]

        ps = ctx.enter_context(nc.psum_tensor("ps", [P, 8, 512], F32))
        y_bank = ps[:, 0:4, :]

        ring = sb("ring", [P, SLOTS, UNIT])
        x_sb = sb("x_sb", [P, 4, D])
        hT = sb("hT", [P, KC, NT])
        h = sb("h", [P, 2, D])
        v_scale = sb("v_scale", [P, D])
        v_shift = sb("v_shift", [P, D])
        v_gate = sb("v_gate", [P, D])
        v_tmp = sb("v_tmp", [P, D])
        junk = sb("junk", [P, D])
        ident = sb("ident", [P, P])
        s_le_t = sb("s_le_t", [P, P])
        s_ge_t = sb("s_ge_t", [P, P])
        ones_t = sb("ones_t", [P, P])
        rounds_i = ctx.enter_context(nc.sbuf_tensor("rounds_i", [P, 1], mybir.dt.int32))
        eps_t = sb("eps_t", [P, 1])
        zero_t = sb("zero_t", [P, 512])
        note = sb("note", [1, 1])
        rs = sb("rs", [P, 2])
        ys = sb("ys", [P, 3])
        stat = sb("stat", [P, 6, 8])
        cond = sb("cond", [P, 3, KC])
        cond_sig = sb("cond_sig", [P, 3, KC])
        w_gdn_ba = sb("w_gdn_ba", [P, KC, 16])
        gdn_vec = sb("gdn_vec", [P, 3, 8])
        ARENA = 23300
        arena = sb("arena", [P, ARENA])

        class Area:
            def __init__(self, at=0):
                self.at = at

            def __call__(self, *shape, parts=P):
                n = int(np.prod(shape))
                v = arena[0:parts, self.at:self.at + n]
                self.at += n
                assert self.at <= ARENA, self.at
                if len(shape) == 2:
                    v = v.rearrange("p (a b) -> p a b", a=shape[0])
                if len(shape) == 3:
                    v = v.rearrange("p (a b c) -> p a b c", a=shape[0], b=shape[1])
                if len(shape) == 4:
                    v = v.rearrange("p (a b c d) -> p a b c d", a=shape[0], b=shape[1], c=shape[2])
                return v

        A = Area()
        mod_rows = A(2, 6 * D, parts=2)
        A = Area()
        v_tok = A(4, 4, 129)
        gate = A(4, D)
        o = A(4, D)
        hg_q = A(2, NT)
        hg_z = A(2, 2, NT)
        state = A(NSC, P)
        lbs = A(8, 2, 4)
        dec = A(2, NSC)
        w_gates = A(KC, 2, ROWS)
        gate_bias = A(2)
        w_conv = A(4, 3)
        tmp_at = A.at
        T1, T2, E1, E2, E3, E4 = (A(2, NT) for _ in range(6))
        chunk_masks = A(2, P)
        chunk_starts = A(NT)
        A = Area(tmp_at)
        g_sig = T1[:, 0, :]
        qk = A(4, NT)
        rows_a, rows_b, rows_c, rows_d, rows_e, rows_f = (A(NT, parts=ROWS) for _ in range(6))
        wexp = A(2, NT)
        g_sig2 = wexp[:, 0, :]
        in_state = state.rearrange("p a b -> p (a b)")
        row_select = in_state[0:ROWS, 0:8 * P].rearrange("p (a b) -> p a b", a=8)
        colsT = in_state[:, 8 * P:8 * P + 8 * ROWS].rearrange("p (a b c) -> p a b c", a=2, b=4)
        out_g = wexp.rearrange("p a b -> p (a b)")
        p_sb = hg_z.rearrange("p a b c -> p (a b) c")
        mden = A(3, 4)
        msum = A(2, 8)
        A = Area()
        sig = A(2, EH)
        swish = A(2, EH)
        hid = A(2, 2, EH)
        hidT = A(2, 2, 2 * P)
        moe_gates = A(2, N_EXPERTS + 2)
        gate_now = A(2, 2)
        w_route = A(KC, ROUTE_W)
        w_sg = A(KC)
        route_b = A(N_GROUPS + N_EXPERTS)
        rt = A(8, N_EXPERTS)
        rt1 = A(16)
        ring_more = A(SLOTS, UNIT)
        picked = A(2, N_EXPERTS)
        rank = A(2, N_EXPERTS)
        r_gate, r_rank, r_rank_x = A(2, QUAD), A(2, QUAD), A(2, QUAD)
        sel = A(2, QUAD * CAP)
        sel_gated = A(2, QUAD * CAP)
        sel_T = A(SEQ)
        x_slots = A(KC, P)
        q_sig, q_swish, q_hid = A(EH), A(EH), A(EH)
        q_hidT = A(2, P)
        z_slots = A(D)
        slot_index = A(CAP)
        round_limits = A(SEQ // CAP - 1)
        over = A(SEQ // CAP + 1)
        A = Area()
        aq = A(2, 8, P)
        ak = A(4, 2, P)
        av = A(4, 2, P)
        aqr = A(2, 8, P)
        akr = A(4, 2, P)
        qT = A(8, SEQ)
        kT = A(2, NT)
        prob = A(2, NT)
        probT = A(2, 4, P)
        rope = A(2, 2, 64)
        qk_g = A(2, P)
        asq = A(8, P)
        astat = A(2, 8)
        smax = A(2, 4)
        A = Area()
        cv_b = A(2, SEQ)
        cv_g = A(2, SEQ)
        cv_y = A(2, SEQ)
        w_sconv = A(KC, 3)
        A = Area()
        gT = A(24, SEQ)
        g_kT, g_kbT, g_qT = (gT[:, 8 * n:8 * n + 8, :] for n in range(3))
        gtok = A(2, 24, P)
        gkb = A(2, 8, P)
        gqe_T = A(8, P)
        g_z = A(2, D)
        g_o = gkb.rearrange("p a b c -> p a (b c)")
        g_kdec = A(8, P)
        w_gconv = A(24, 4)
        g_ba = A(2, 16)
        g_t = A(10, 16)
        g_norm = A(P)
        g_sq = A(8, P)
        lv = A(LEVELS, P)
        LT, AT, U, gS = (A(4, P) for _ in range(4))
        g_o0, g_o1 = gkb[:, 0], gkb[:, 1]
        DD, DT_ = h[:, 0, 0:512].rearrange("p (a b) -> p a b", a=4), h[:, 0, 512:1024].rearrange("p (a b) -> p a b", a=4)
        TT, LM = h[:, 1, 0:512].rearrange("p (a b) -> p a b", a=4), h[:, 1, 512:1024].rearrange("p (a b) -> p a b", a=4)
        WT = v_tmp

        mod_dram = nc.dram_tensor("mod_dram", [6, 6 * D], F32).ap()

        slot_filled = [sem(f"slot_filled_{s}") for s in range(2 * SLOTS)]
        block_done, gu_evacuated = sem("block_done"), sem("gu_evacuated")
        tp_full, tp_evacuated = sem("tp_full"), sem("tp_evacuated")
        h_ready, x_updated = sem("h_ready"), sem("x_updated")
        constants_loaded, x_loaded = sem("constants_loaded"), sem("x_loaded")

        class Teller:

            def __init__(self, engine):
                self.engine, self.told = engine, {}

            def __call__(self, ins, s):
                self.told[s.name] = self.told.get(s.name, 0) + 1
                ins.then_inc(s, 1)
                self.engine.wait_ge(s, self.told[s.name])

        def slot(s):
            return ring[:, s, :] if s < SLOTS else ring_more[:, s - SLOTS, :]

        def slot_pair(s):
            return ring[:, s:s + 2, :] if s < SLOTS else ring_more[:, s - SLOTS:s - SLOTS + 2, :]

        ROW = {"l0": 0, "l0c": 1, "l1": 2, "l1c": 3, "b0": 4, "b1": 5}
        PRE = [("l0c", 0, I["norm_g"][0, 0]), ("l0", 0, I["norm_g"][0, 0]),
               ("l0c", 1, I["norm_g"][0, 2]), ("l0", 1, I["norm_g"][0, 2]),
               ("l1c", 0, I["norm_g"][1, 0]), ("l1", 0, I["norm_g"][1, 0]), ("l1", 1, I["norm_g"][1, 2]),
               ("b0", 0, I["norm_w_2"][0, 0]), ("b0", 1, I["norm_w_2"][0, 2]),
               ("b1", 0, I["norm_w_2"][1, 0]), ("b1", 1, I["norm_w_2"][1, 2])]
        POST = [("l0c", 0, I["norm_g"][0, 1]), ("l0", 0, I["norm_g"][0, 1]),
                ("l0c", 1, I["norm_g"][0, 3]), ("l0", 1, I["norm_g"][0, 3]),
                ("l1", 0, I["norm_g"][1, 1]), ("l1", 1, I["norm_g"][1, 3]),
                ("b0", 0, I["norm_w_2"][0, 1]), ("b0", 1, I["norm_w_2"][0, 3]),
                ("b1", 0, I["norm_w_2"][1, 1]), ("b1", 1, I["norm_w_2"][1, 3])]
        CTX, LAT = (0, 1), (2, 3)
        ADA = [("ada_w", 0, (0, 1)), ("ada_w", 1, (2, 3)), ("ada_w_2", 0, (4,)), ("ada_w_2", 1, (5,))]

        def row_all(ap1d):
            return ap1d.rearrange("(o n) -> o n", o=1).broadcast_to([P, ap1d.shape[0]])

        block = ctx.enter_context(nc.Block())

        @block.sync
        def _(sp):
            n = Counts()
            free_at = [0] * SLOTS

            def sp_loop(count):
                if count > 0:
                    with sp.Fori(0, count) as r:
                        yield r

            def kmajor(w):
                return w.rearrange("(p k) n -> p k n", k=KC)

            def pmajor(w):
                return w.rearrange("(k p) n -> p k n", p=P)

            def fill(s, src, free=None):
                free = free_at[s] if free is None else free
                if not isinstance(free, int) or free > 0:
                    sp.wait_ge(block_done, free)
                dst = slot(s)
                if len(src.shape) == 3:
                    dst = dst.rearrange("p (k n) -> p k n", k=src.shape[1])
                sp.dma_start(dst, src).then_inc(slot_filled[s], 16)

            def stream(units, blocks):
                n.block += blocks
                for src in units:
                    (s,) = n.slots(1)
                    fill(s, src)
                    free_at[s] = n.block

            def columns(w, unit, order):
                return order(w[:, unit * EH:(unit + 1) * EH])

            def conditioning():
                for l, (name, j, _) in enumerate(ADA):
                    w = I[name][j]
                    if l == 0:
                        for s in range(SLOTS):
                            fill(s, columns(w, s, kmajor))
                    first = 1 if l == 0 else 0
                    with sp.Fori(first, 4) as r:
                        for s in range(SLOTS):
                            fill(s, kmajor(w[:, bass.ds(r * (SLOTS * EH) + s * EH, EH)]),
                                 free=r * 3 + (12 * l - 3 + s // 2 + 1))
                n.block = 48
                for s in range(SLOTS):
                    free_at[s] = 45 + s // 2 + 1

            def slice_units(wg, wu, wd):
                return kmajor(wg), kmajor(wu), wd.rearrange("(p j) n -> p (j n)", j=2)

            def mlp(count, units_of, tail=()):
                n.align()
                b0 = n.block
                for i in range(2):
                    for s, src in zip(range(3 * i, 3 * i + 3), units_of(i)):
                        fill(s, src)
                pairs = (count - 2) // 2
                for r in sp_loop(pairs):
                    for j in range(2):
                        g, u, d = units_of(r * 2 + (2 + j))
                        fill(3 * j, g, free=r * 6 + (b0 + 3 * j + 2))
                        fill(3 * j + 1, u, free=r * 6 + (b0 + 3 * j + 2))
                        fill(3 * j + 2, d, free=r * 6 + (b0 + 3 * j + 5))
                rest = [units_of(i) for i in range(2 + 2 * pairs, count)] + list(tail)
                total = count + len(tail)
                for k, (g, u, d) in enumerate(rest):
                    i = 2 + 2 * pairs + k
                    j = i % 2
                    fill(3 * j, g, free=b0 + 3 * (i - 2) + 2)
                    fill(3 * j + 1, u, free=b0 + 3 * (i - 2) + 2)
                    fill(3 * j + 2, d, free=b0 + 3 * (i - 2) + 5)
                n.block += 3 * total
                n.pos = 3 * total
                for s in range(SLOTS):
                    free_at[s] = n.block

            def ffn(l):
                wi, wo = I["ffn_w_in"][l], I["ffn_w_out"][l]
                mlp(NFF, lambda i: slice_units(wi[:, bass.ds(i * EH, EH)], wi[:, bass.ds(i * EH + D_FF, EH)],
                                               wo[bass.ds(i * EH, EH), :]))

            def experts(l):
                n.block += 2
                shared = [slice_units(I["shared_w_gate_2"][l][:, j * EH:(j + 1) * EH],
                                      I["shared_w_up_2"][l][:, j * EH:(j + 1) * EH],
                                      I["shared_w_down_2"][l][j * EH:(j + 1) * EH, :]) for j in range(2)]
                mlp(2, lambda i: shared[i])
                used_gu, used_down = sem("quad_gate_up_used"), sem("quad_down_used")

                def quad(of, q, first):
                    for a in range(QUAD):
                        for s, name in ((2 * a, "moe_w_gate_2"), (2 * a + 1, "moe_w_up_2")):
                            if first and s < SLOTS:
                                sp.wait_ge(block_done, free_at[s])
                            elif first:
                                sp.wait_ge(x_updated, n.x)
                            else:
                                sp.wait_ge(used_gu, q + QUADS * l)
                            sp.dma_start(slot(s).rearrange("p (k n) -> p k n", k=KC),
                                         of(name, a).rearrange("(p k) n -> p k n", k=KC)).then_inc(slot_filled[s], 16)
                    for a in range(QUAD):
                        if not first:
                            sp.wait_ge(used_down, q + QUADS * l)
                        sp.dma_start(slot(8 + a), of("moe_w_down_2", a).rearrange("(p j) n -> p (j n)", j=2)) \
                            .then_inc(slot_filled[8 + a], 16)

                quad(lambda name, a: I[name][l, a], 0, True)
                with sp.Fori(1, QUADS) as q:
                    quad(lambda name, a: I[name][l, bass.ds(q * QUAD + a, 1)].rearrange("o a b -> (o a) b"), q, False)
                n.block += 1
                n.pos = 0
                sp.wait_ge(used_gu, QUADS * (l + 1))
                for s in range(SLOTS):
                    free_at[s] = 0

            conditioning()
            w = I["ab_w_in"][0]
            for at in (512, 1024):
                stream([kmajor(w[:, at + EH * j:at + EH * (j + 1)]) for j in range(2)], 4)
            for hp in range(2):
                for at in (0, 1536, 2048):
                    stream([kmajor(w[:, at + EH * hp:at + EH * (hp + 1)])], 2)
            for at in (3072, 3584):
                stream([kmajor(w[:, at + EH * j:at + EH * (j + 1)]) for j in range(2)], 4)
            for j in range(2):
                stream([kmajor(w[:, 2560 + EH * j:2560 + EH * (j + 1)])], 2)
            stream([columns(I["ab_w_out"][0], j, pmajor) for j in range(4)], 4)
            ffn(0)
            ffn(0)
            w = I["attn_w_qkv"][0]
            for j in range(2):
                stream([columns(w, 2 * j, kmajor), columns(w, 2 * j + 1, kmajor)], 2)
            stream([columns(w, 4, kmajor), columns(w, 5, kmajor)], 4)
            stream([columns(I["attn_w_out"][0], j, pmajor) for j in range(4)], 2)
            ffn(1)
            w = I["conv_in_w_2"][0]
            for c in range(4):
                for part in range(3):
                    stream([columns(w, 4 * part + c, kmajor)], 2)
            stream([columns(I["conv_out_w_2"][0], j, pmajor) for j in range(4)], 2)
            n.x = 14
            experts(0)
            w = I["gdn_in_w_2"][0]
            for j in range(12):
                stream([columns(w, j, kmajor)], 2)
            for j in range(6, 8):
                stream([columns(w, 2 * j, kmajor), columns(w, 2 * j + 1, kmajor)], 2)
            stream([columns(I["gdn_out_w_2"][0], j, pmajor) for j in range(4)], 2)
            n.x = 18
            experts(1)
            n.x = 20
            for t in range(2):
                sp.wait_ge(x_updated, n.x - 1 + t)
                sp.dma_start(out[0, t * P:(t + 1) * P, :], x_sb[:, 2 + t, :]).then_inc(sem("result_stored"), 16)
            sp.wait_ge(sem("result_stored"), 32)

        @block.gpsimd
        def _(pool):
            n = Counts()
            tell = Teller(pool)
            loads = {}
            vec_step = sem("vec_step")
            made_pre, made_post = [0], [0]
            seen = {"h": [], "x": []}

            def load(dst, src, s):
                loads[s.name] = loads.get(s.name, 0) + 16
                pool.dma_start(dst, src).then_inc(s, 16)

            def arrived(s):
                pool.wait_ge(s, loads[s.name])

            def pre():
                which, half, g = PRE[made_pre[0]]
                if made_pre[0] > 0:
                    pool.wait_ge(h_ready, n.h)
                made_pre[0] += 1
                row = mod_dram[ROW[which]]
                load(v_scale[:, :], row_all(row[(3 * half + 1) * D:(3 * half + 2) * D]), sem("vectors_loaded"))
                load(v_shift[:, :], row_all(row[3 * half * D:(3 * half + 1) * D]), sem("vectors_loaded"))
                load(v_tmp[:, :], row_all(g), sem("vectors_loaded"))
                arrived(sem("vectors_loaded"))
                tell(nc.gpsimd.tensor_scalar(v_scale[:, :], v_scale[:, :], 1.0, None, ALU.add), vec_step)
                tell(nc.gpsimd.tensor_tensor(v_scale[:, :], v_scale[:, :], v_tmp[:, :], ALU.mult), sem("pre_ready"))

            def post():
                which, half, g = POST[made_post[0]]
                if made_post[0] > 0:
                    pool.wait_ge(x_updated, n.x)
                made_post[0] += 1
                row = mod_dram[ROW[which]]
                load(v_gate[:, :], row_all(row[(3 * half + 2) * D:(3 * half + 3) * D]), sem("vectors_loaded"))
                load(v_tmp[:, :], row_all(g), sem("vectors_loaded"))
                arrived(sem("vectors_loaded"))
                tell(nc.gpsimd.tensor_tensor(v_gate[:, :], v_gate[:, :], v_tmp[:, :], ALU.mult), sem("post_ready"))

            for i, c in enumerate((I["c"][0], I["c_ctx"], I["c_2"][0])):
                load(cond[:, i, :], c.rearrange("(p k) -> p k", k=KC), sem("cond_loaded"))
            for dst, src in ((ident, "ident"), (s_le_t, "s_le_t"), (s_ge_t, "s_ge_t")):
                load(dst[:, :], I[src], constants_loaded)
            for i, src in enumerate((I["ctx"][0], I["x"][0])):
                load(x_sb[:, 2 * i:2 * i + 2, :], src.rearrange("(t p) d -> p t d", p=P), x_loaded)
            for l, (name, j, rows) in enumerate(ADA):
                if l >= 2:
                    pool.wait_ge(sem(f"mod_stored_{l - 2}"), 16)
                b = I[name.replace("_w", "_b")][j]
                for q in range(len(rows)):
                    load(mod_rows[q:q + 1, l % 2, :], b.rearrange("(o n) -> o n", o=1), sem(f"ada_bias_loaded_{l}"))
                if l >= 1:
                    store_l = l - 1
                    pool.wait_ge(sem("mod_row_ready"), store_l + 1)
                    rr = ADA[store_l][2]
                    pool.dma_start(mod_dram[rr[0]:rr[0] + len(rr), :], mod_rows[0:len(rr), store_l % 2, :]).then_inc(sem(f"mod_stored_{store_l}"), 16)
            pool.wait_ge(sem("mod_row_ready"), 4)
            pool.dma_start(mod_dram[5:6, :], mod_rows[0:1, 1, :]).then_inc(sem("mod_stored_3"), 16)
            for l in range(4):
                pool.wait_ge(sem(f"mod_stored_{l}"), 16)

            tell(nc.gpsimd.memset(w_gates, 0.0), vec_step)
            tell(nc.gpsimd.memset(gate_bias, 0.0), vec_step)
            s = sem("ab_constants")
            load(chunk_masks, I["chunk_masks"], s)
            load(chunk_starts, I["chunk_starts"], s)
            for d in range(2):
                for part in range(2):
                    at = 4 * (2 * d + part)
                    load(w_gates[:, :, part, 32 * d:32 * d + 4],
                         I["ab_w_in"][0][:, 4096 + at:4100 + at].rearrange("(p k) n -> p k n", k=KC), s)
                    load(gate_bias[32 * d:32 * d + 4, part:part + 1],
                         I["ab_gate_b"][0, 2 * d + part].rearrange("(n o) -> n o", o=1), s)
            load(lbs[:, 0:3], I["hgrn_lb"], s)
            load(w_conv, I["ab_conv"], s)
            pre()
            n.h += 2
            pre()
            n.h += 2
            post()
            pool.wait_ge(sem("hgrn_done"), 1)
            load(row_select, I["row_select"], sem("row_select_loaded"))
            pool.wait_ge(sem("mlstm_done"), 1)
            load(out_g, row_all(I["ab_out_g"][0]), sem("out_g_loaded"))
            n.h += 4
            n.x += 2
            post()
            n.x += 2
            pre()
            n.h += 2
            post()
            n.x += 2
            pre()
            n.h += 2
            post()
            n.x += 2
            pool.wait_ge(x_updated, n.x)
            load(rope, I["rope"], sem("att_constants"))
            for i in range(2):
                load(qk_g[:, i, :], row_all(I["attn_qk_g"][0, i]), sem("att_constants"))
            pre()
            n.h += 2
            pre()
            n.h += 2
            post()
            n.x += 2
            pre()
            n.h += 2
            post()
            n.x += 2
            pool.wait_ge(x_updated, n.x)
            load(w_sconv, I["conv_w_2"], sem("sconv_w_loaded"))
            pre()
            n.h += 2
            post()
            n.x += 2

            def router_loads(l):
                pool.wait_ge(x_updated, n.x)
                s = sem("route_w_loaded")
                load(w_route[:, :, 0:N_GROUPS], I["moe_group_w_2"][l].rearrange("(p k) n -> p k n", k=KC), s)
                load(w_route[:, :, N_GROUPS:ROUTE_W - 1], I["moe_expert_w_2"][l].rearrange("(p k) n -> p k n", k=KC), s)
                load(w_sg, I["shared_gate_w_2"][l].rearrange("(p k) n -> p (k n)", k=KC), s)
                load(route_b[:, 0:N_GROUPS], row_all(I["moe_group_b_2"][l]), s)
                load(route_b[:, N_GROUPS:], row_all(I["moe_expert_b_2"][l]), s)
                load(slot_index, I["slot_index"], s)
                load(round_limits, I["round_limits"], s)
                arrived(s)
                tell(nc.gpsimd.tensor_copy(w_route[:, :, ROUTE_W - 1], w_sg), sem("route_w_ready"))

            router_loads(0)
            pre()
            n.h += 2
            post()
            n.x += 2
            pool.wait_ge(x_updated, n.x)
            s = sem("gdn_constants")
            load(w_gconv, I["gdn_conv_w_2"], s)
            load(w_gdn_ba[:, :, :], I["gdn_in_w_2"][0][:, 4096:4112].rearrange("(p k) n -> p k n", k=KC), s)
            load(gdn_vec[:, 0, :], row_all(I["gdn_a_log_2"][0]), s)
            load(gdn_vec[:, 1, :], row_all(I["gdn_dt_bias_2"][0]), s)
            load(g_norm, row_all(I["gdn_norm_w_2"][0]), s)
            load(lv, I["levels"], s)
            pre()
            n.h += 2
            n.h += 2
            pool.wait_ge(h_ready, n.h)
            post()
            n.x += 2
            router_loads(1)
            pre()
            n.h += 2
            post()

        @block.tensor
        def _(pe):
            n = Counts()
            used = [0] * SLOTS

            def filled(s):
                used[s] += 1
                pe.wait_ge(slot_filled[s], 16 * used[s])

            def gu_bank():
                i = n.gu
                if i >= 2:
                    pe.wait_ge(gu_evacuated, i - 1)
                n.gu += 1
                n.block += 1
                return ps[:, 4 + i % 2, :]

            def products(outs, lhsT_of, slots, start=True, stop=True):
                a, b = slots
                if b == a + 1:
                    o3 = outs.rearrange("p (u c) -> p u c", u=2)
                    for k in range(KC):
                        m = pe.matmul(o3, lhsT_of(k), ring[:, a:a + 2, k * EH:(k + 1) * EH],
                                      start=start and k == 0, stop=stop and k == KC - 1)
                else:
                    for u, s in enumerate(slots):
                        for k in range(KC):
                            m = pe.matmul(outs[:, u * EH:(u + 1) * EH], lhsT_of(k), ring[:, s, k * EH:(k + 1) * EH],
                                          start=start and k == 0, stop=stop and k == KC - 1)
                return m

            def token_major(tiles):
                slots = n.slots(2)
                for s in slots:
                    filled(s)
                for t in tiles:
                    outs = gu_bank()
                    products(outs, lambda k: hT[:, k, t * P:(t + 1) * P], slots).then_inc(block_done, 1)

            def feature_major(c0, c1):
                (s,) = n.slots(1)
                filled(s)
                for c in range(2):
                    outs = gu_bank()
                    for k in range(KC):
                        m = pe.matmul(outs[:, 0:c1 - c0], ring[:, s, k * EH + c * P:k * EH + (c + 1) * P],
                                      hT[:, k, c0:c1], start=k == 0, stop=k == KC - 1)
                    m.then_inc(block_done, 1)

            def transposes(srcs, parts=P):
                i = n.tp
                if i >= 2:
                    pe.wait_ge(tp_evacuated, i - 1)
                w = srcs[0].shape[-1]
                for j, src in enumerate(srcs):
                    m = pe.transpose(ps[0:w, 6 + i % 2, j * P:j * P + src.shape[0]], src,
                                     ident[0:src.shape[0], 0:src.shape[0]])
                m.then_inc(tp_full, 1)
                n.tp += 1

            def norm_tiles(tiles):
                for _ in tiles:
                    b = n.h % 2
                    n.h += 1
                    pe.wait_ge(h_ready, n.h)
                    for half in range(2):
                        transposes([h[:, b, 4 * half + kk::KC] for kk in range(4)])

            def mixer_out(tiles, col0):
                slots = n.slots(4)
                for s in slots:
                    filled(s)
                pe.wait_ge(tp_evacuated, n.tp)
                for i, t in enumerate(tiles):
                    pe.wait_ge(x_updated, n.x) if (n.x > 0) else None
                    for half in range(2):
                        m = products(ps[:, 2 * (i % 2) + half, :], lambda k: hT[:, k, t * P - col0:(t + 1) * P - col0],
                                     slots[2 * half:2 * half + 2])
                    m.then_inc(block_done, 1)
                    n.block += 1
                    if i % 2 == 1:
                        n.x += 2

            def pe_loop(count):
                if count > 0:
                    with pe.Fori(0, count) as r:
                        yield r

            def mlp(total, col0, last=True):
                n.align()
                gu0, tp0, filled0 = n.gu, n.tp, list(used)
                assert gu0 % 2 == 0

                def gate_up(i_par, t, gu_wait, fill_wait):
                    if t == 0:
                        for s in (3 * i_par, 3 * i_par + 1):
                            pe.wait_ge(slot_filled[s], fill_wait(s))
                    pe.wait_ge(gu_evacuated, gu_wait)
                    products(ps[:, 4 + t, :], lambda k: hT[:, k, col0 + t * P:col0 + (t + 1) * P],
                             (3 * i_par, 3 * i_par + 1)).then_inc(block_done, 1)

                def turn(i_par, gu_wait, tp_wait):
                    pe.wait_ge(gu_evacuated, gu_wait)
                    pe.wait_ge(tp_evacuated, tp_wait)
                    for j in range(2):
                        for t in range(2):
                            m = pe.transpose(ps[:, 6 + (tp0 + i_par) % 2, j * EH + t * P:j * EH + (t + 1) * P],
                                             hid[:, i_par, t, j::2], ident[:, :])
                    m.then_inc(tp_full, 1)

                def down(i_par, tp_wait, fill_wait):
                    s = 3 * i_par + 2
                    pe.wait_ge(slot_filled[s], fill_wait(s))
                    pe.wait_ge(tp_evacuated, tp_wait)
                    for t in range(2):
                        for half in range(2):
                            for j in range(2):
                                m = pe.matmul(ps[:, 2 * t + half, :], hidT[:, i_par, j, t * P:(t + 1) * P],
                                              ring[:, s, j * D + half * 512:j * D + (half + 1) * 512],
                                              start=False, stop=False, skip_group_check=True)
                    m.then_inc(block_done, 1)

                pe.wait_ge(sem("zero_ready"), 1)
                if n.x > 0:
                    pe.wait_ge(x_updated, n.x)
                for b in range(4):
                    pe.matmul(ps[:, b, :], zero_t[:, 0:P], zero_t[:, :], start=True, stop=False, skip_group_check=True)
                for t in range(2):
                    gate_up(0, t, gu0 - 1 + t, lambda s: 16 * (filled0[s] + 1))
                pairs = (total - 1) // 2
                for r in pe_loop(pairs):
                    for j in range(2):
                        q = 1 - j
                        fw = (lambda s: r * 16 + 16 * (filled0[s] + 1)) if j == 0 else \
                            (lambda s: r * 16 + 16 * (filled0[s] + 2))
                        gate_up(q, 0, r * 4 + (gu0 + 2 * (j + 1) - 1), fw)
                        turn(j, r * 4 + (gu0 + 2 * j + 2), r * 2 + max(tp0 + j - 1, 0))
                        gate_up(q, 1, r * 4 + (gu0 + 2 * (j + 1)), fw)
                        down(j, r * 2 + (tp0 + j + 1), lambda s: r * 16 + 16 * (filled0[s] + 1))
                for i in range(2 * pairs, total):
                    j = i % 2
                    if i + 1 < total:
                        gate_up(1 - j, 0, gu0 + 2 * (i + 1) - 1, lambda s: 16 * (filled0[s] + (i + 1) // 2 + 1))
                    turn(j, gu0 + 2 * i + 2, tp0 + i - 1)
                    if i + 1 < total:
                        gate_up(1 - j, 1, gu0 + 2 * (i + 1), lambda s: 16 * (filled0[s] + (i + 1) // 2 + 1))
                    down(j, tp0 + i + 1, lambda s: 16 * (filled0[s] + i // 2 + 1))
                for s in range(SLOTS):
                    used[s] += (total + 1) // 2 if s < 3 else total // 2
                n.gu += 2 * total
                n.tp += total
                n.block += 3 * total
                n.pos = 3 * total
                n.x += 2 if last else 0

            pe.wait_ge(sem("cond_ready"), 1)
            for l, (name, j, rows) in enumerate(ADA):
                lo, m_ = (0, 2) if l < 2 else (2, 1)
                def turn(r):
                    for q in range(6):
                        a = (2 * q) % SLOTS
                        for s in (a, a + 1):
                            pe.wait_ge(slot_filled[s], r * 32 + 16 * (4 * l + q // 3 + 1))
                        i = 12 * l + q
                        if not isinstance(r, int) or 6 * r + i >= 2:
                            pe.wait_ge(gu_evacuated, r * 6 + (i - 1))
                        o3 = ps[0:m_, 4 + q % 2, :].rearrange("p (u c) -> p u c", u=2)
                        for k in range(KC):
                            m = pe.matmul(o3, cond[:, lo:lo + m_, k], ring[:, a:a + 2, k * EH:(k + 1) * EH],
                                          start=k == 0, stop=k == KC - 1)
                        m.then_inc(block_done, 1)

                if l == 0:
                    turn(0)
                    turn(1)
                else:
                    with pe.Fori(0, 2) as r:
                        turn(r)
            n.gu = n.block = 48
            n.pos = 0
            used = [16] * SLOTS

            pe.wait_ge(constants_loaded, 48)
            norm_tiles(CTX)
            norm_tiles(LAT)
            pe.wait_ge(tp_evacuated, n.tp)
            token_major((0, 1, 2, 3))
            token_major((0, 1, 2, 3))
            for hp in range(2):
                if hp == 1:
                    pe.wait_ge(sem("hg_out_read"), 4)
                for _ in range(3):
                    feature_major(0, NT)
                for hh in range(2):
                    hd = 2 * hp + hh
                    for d in range(2):
                        i = 2 * hd + d
                        pe.wait_ge(sem("hg_factors"), 2 * (hd + 1))
                        if i >= 1:
                            pe.wait_ge(sem("hg_scores_read"), i)
                        for t in range(4):
                            c = slice(t * P, (t + 1) * P)
                            m = pe.matmul(ps[:, 4, c], E2[:, d, c], E1[:, d, c], start=True, stop=True)
                        m.then_inc(sem("hg_scores"), 1)
                        transposes([E4[:, d, t * P:(t + 1) * P] for t in range(4)])
                        pe.wait_ge(tp_evacuated, n.tp)
                        if i >= 1:
                            pe.wait_ge(sem("hg_states"), i)
                        for c in range(NSC):
                            t, q = c // 4, 32 * (c % 4)
                            m = pe.matmul(ps[:, c % 4, t * P:(t + 1) * P],
                                          T2[q:q + 32, d, t * P:(t + 1) * P], v_tok[q:q + 32, t, hd, 0:P],
                                          start=True, stop=True)
                        m.then_inc(sem("hg_updates"), 1)
                        pe.wait_ge(sem("hg_scores_read"), i + 1)
                        pe.wait_ge(sem("hg_states"), i + 1)
                        if i >= 1:
                            pe.wait_ge(sem("hg_out_read"), i)
                        for t in range(4):
                            c0 = ps[:, 5, t * P:(t + 1) * P]
                            m = pe.matmul(c0, T1[:, d, t * P:(t + 1) * P], v_tok[:, t, hd, 0:P],
                                          start=True, stop=False, skip_group_check=True)
                            for q in range(4):
                                c = 4 * t + q
                                if c == (0 if d == 0 else NSC // 2 - 1):
                                    continue
                                m = pe.matmul(ps[32 * q:32 * q + 32, 5, t * P:(t + 1) * P],
                                              E3[:, d, c * 32:(c + 1) * 32], state[:, c, :],
                                              start=False, stop=True, skip_group_check=True)
                        m.then_inc(sem("hg_out"), 1)
            pe.wait_ge(sem("hg_out_read"), 8)
            token_major((0, 1, 2, 3))
            token_major((0, 1, 2, 3))
            feature_major(0, NT)
            feature_major(0, NT)
            pe.wait_ge(sem("hg_states"), 8)
            for part in range(2):
                for k in range(KC):
                    m = pe.matmul(ps[0:ROWS, part, :], w_gates[:, k, part, :], hT[:, k, :], start=k == 0, stop=k == KC - 1)
            m.then_inc(sem("ml_gates"), 1)
            pe.wait_ge(sem("ml_rows"), 1)
            for src in (rows_e, rows_f):
                transposes([src[:, t * P:(t + 1) * P] for t in range(4)])
            pe.wait_ge(sem("row_select_loaded"), 16)
            pe.wait_ge(sem("ml_qk"), 4)
            for hd in range(MLSTM_HEADS):
                q0 = 64 * (hd % 2)
                qh, kh = qk[q0:q0 + 64, hd // 2, :], qk[q0:q0 + 64, 2 + hd // 2, :]
                if hd >= 1:
                    pe.wait_ge(sem("ml_weights"), 8 * hd)
                for si in range(4):
                    c0 = 0 if si < 2 else SEQ
                    m = pe.matmul(ps[:, si, c0:NT], kh[:, si * P:(si + 1) * P], qh[:, c0:NT], start=True, stop=True)
                m.then_inc(sem("ml_scores"), 1)
                for d in range(2):
                    i = 2 * hd + d
                    if i >= 2:
                        pe.wait_ge(sem("ml_weights"), 4 * (i - 1))
                    pe.matmul(ps[:, 4 + d, :], row_select[:, 4 * d + hd, :], rows_d, start=True, stop=True).then_inc(sem("ml_max"), 1)
                    pe.wait_ge(sem("ml_weights"), 4 * (i + 1))
                    pe.wait_ge(tp_evacuated, n.tp)
                    if i >= 1:
                        pe.wait_ge(sem("ml_out_read"), i)
                    for ti in range(4):
                        seg, own = divmod(ti, 2)
                        keys = [s for s in range(2 * seg, 2 * seg + 2) if (s <= ti if d == 0 else s >= ti)]
                        keys = ([0, 1] if seg else []) + keys
                        for si in keys:
                            m = pe.matmul(ps[:, 6 + ti // 2, (ti % 2) * 129:(ti % 2) * 129 + 129],
                                          p_sb[:, si, ti * P:(ti + 1) * P], v_tok[:, si, hd, :],
                                          start=si == keys[0], stop=si == keys[-1])
                    m.then_inc(sem("ml_out"), 1)
            pe.wait_ge(sem("ml_out_read"), 8)

            def mixed_tiles(src, tiles):
                for t in tiles:
                    n.h += 1
                    pe.wait_ge(h_ready, n.h)
                    for half in range(2):
                        transposes([src[:, t, (4 * half + kk) * P:(4 * half + kk + 1) * P] for kk in range(4)])

            mixed_tiles(o, range(4))
            mixer_out((0, 1, 2, 3), 0)
            norm_tiles(CTX)
            pe.wait_ge(tp_evacuated, n.tp)
            mlp(NFF, 0)
            norm_tiles(LAT)
            pe.wait_ge(tp_evacuated, n.tp)
            mlp(NFF, SEQ)
            norm_tiles(CTX)
            norm_tiles(LAT)
            pe.wait_ge(tp_evacuated, n.tp)
            token_major(LAT)
            token_major(LAT)
            token_major((0, 1, 2, 3))
            pe.wait_ge(sem("at_q_ready"), 2)
            for hd in range(0, 8, 2):
                transposes([aqr[:, t, hd + a, :] for a in range(2) for t in range(2)])
            pe.wait_ge(sem("at_k_ready"), 4)
            for kv in range(2):
                transposes([akr[:, t, kv, :] for t in range(4)])
            pe.wait_ge(tp_evacuated, n.tp)
            pe.wait_ge(x_updated, n.x)
            pe.wait_ge(gu_evacuated, n.gu)
            N_AT = 16

            def scores(i):
                hd, t = divmod(i, 2)
                if i >= 2:
                    pe.wait_ge(sem("at_exp"), i - 1)
                pe.matmul(ps[:, 4 + i % 2, :], qT[:, hd, t * P:(t + 1) * P], kT[:, hd // 4, :],
                          start=True, stop=True).then_inc(sem("at_scores"), 1)

            scores(0)
            for i in range(N_AT):
                if i + 1 < N_AT:
                    scores(i + 1)
                hd, t = divmod(i, 2)
                pe.wait_ge(sem("at_prob"), i + 1)
                transposes([prob[:, i % 2, s * P:(s + 1) * P] for s in range(4)])
                pe.wait_ge(tp_evacuated, n.tp)
                for s in range(4):
                    m = pe.matmul(ps[:, i // 4, (i % 4) * P:(i % 4 + 1) * P], av[:, s, hd // 4, :], probT[:, i % 2, s, :],
                                  start=s == 0, stop=s == 3)
                m.then_inc(sem("at_out"), 1)
            pe.wait_ge(sem("at_outT"), 4)
            mixer_out(LAT, 0)
            norm_tiles(LAT)
            pe.wait_ge(tp_evacuated, n.tp)
            mlp(NFF, SEQ)
            norm_tiles(LAT)
            pe.wait_ge(tp_evacuated, n.tp)
            for c in range(12):
                feature_major(SEQ, NT)
            pe.wait_ge(sem("sconv_ready"), KC)
            mixer_out(LAT, SEQ)

            rounds_before = [0]

            def moe(l):
                norm_tiles(LAT)
                pe.wait_ge(tp_evacuated, n.tp)
                pe.wait_ge(sem("route_w_ready"), l + 1)
                for t in range(2):
                    outs = gu_bank()
                    for k in range(KC):
                        m = pe.matmul(outs[:, 0:ROUTE_W], hT[:, k, SEQ + t * P:SEQ + (t + 1) * P], w_route[:, k, :],
                                      start=k == 0, stop=k == KC - 1)
                    m.then_inc(block_done, 1)
                mlp(2, SEQ, last=False)
                pe.wait_ge(sem("picked_ready"), 2 * (l + 1))
                pe.wait_ge(gu_evacuated, n.gu)
                pe.matmul(ps[:, 4, 0:64], s_le_t[:, :], picked[:, 0, :], start=True, stop=True)
                pe.matmul(ps[:, 4, 64:128], s_le_t[:, :], picked[:, 1, :], start=True, stop=False)
                pe.matmul(ps[:, 4, 64:128], ones_t[:, :], picked[:, 0, :], start=False, stop=True)
                pe.matmul(ps[:, 4, 128:192], ones_t[:, :], picked[:, 0, :], start=True, stop=False)
                pe.matmul(ps[:, 4, 128:192], ones_t[:, :], picked[:, 1, :], start=False, stop=True).then_inc(sem("ranks_summed"), 1)
                pe.wait_ge(tp_evacuated, n.tp)
                pe.wait_ge(sem("rounds_known"), l + 1)
                rounds = pe.value_load(rounds_i[0:1, 0:1], min_val=1, max_val=SEQ // CAP)
                S = sem
                before = 0 if l == 0 else rounds_before[0] * QUADS
                rounds_before[0] = rounds

                def one_round(c, filled_gu, filled_down):
                    pe.wait_ge(S("sel_ready"), c + 1)
                    for k in range(KC):
                        for t in range(2):
                            m = pe.matmul(ps[:, 4 + k // 4, (k % 4) * P:(k % 4 + 1) * P], h[:, t, k::KC], sel[:, t, :],
                                          start=t == 0, stop=t == 1)
                    m.then_inc(S("gathered"), 1)
                    pe.wait_ge(S("sel_gated_ready"), c + 1)
                    for t in range(2):
                        m = pe.transpose(ps[:, 7, t * P:(t + 1) * P], sel_gated[:, t, :], ident[:, :])
                    m.then_inc(S("sel_turned"), 1)
                    pe.wait_ge(S("x_slots_lo"), c + 1)
                    pe.wait_ge(S("x_slots_hi"), c + 1)
                    for s in range(8):
                        pe.wait_ge(slot_filled[s], filled_gu(s))
                    for k in range(KC):
                        for a in range(QUAD):
                            m = pe.matmul(ps[a * CAP:(a + 1) * CAP, 6, :].rearrange("p (u c) -> p u c", u=2),
                                          x_slots[:, k, a * CAP:(a + 1) * CAP], slot_pair(2 * a)[:, :, k * EH:(k + 1) * EH],
                                          start=k == 0, stop=k == KC - 1, skip_group_check=True)
                    m.then_inc(S("quad_gate_up"), 1)
                    pe.wait_ge(S("quad_hid"), c + 1)
                    for j in range(2):
                        m = pe.transpose(ps[:, 7, (2 + j) * P:(3 + j) * P], q_hid[:, j::2], ident[:, :])
                    m.then_inc(S("hid_turned"), 1)
                    pe.wait_ge(S("quad_hidT"), c + 1)
                    for s in range(8, 12):
                        pe.wait_ge(slot_filled[s], filled_down(s))
                    for half in range(2):
                        for j in range(2):
                            for a in range(QUAD):
                                m = pe.matmul(ps[a * CAP:(a + 1) * CAP, 4 + half, :], q_hidT[:, j, a * CAP:(a + 1) * CAP],
                                              slot(8 + a)[:, j * D + half * 512:j * D + (half + 1) * 512],
                                              start=j == 0, stop=j == 1, skip_group_check=True)
                    m.then_inc(S("quad_down"), 1)
                    pe.wait_ge(S("sel_T_ready"), c + 1)
                    pe.wait_ge(S("z_lo"), c + 1)
                    pe.wait_ge(S("z_hi"), c + 1)
                    for t in range(2):
                        for half in range(2):
                            m = pe.matmul(ps[:, 2 * t + half, :], sel_T[:, t * P:(t + 1) * P], z_slots[:, half * 512:(half + 1) * 512],
                                          start=False, stop=False, skip_group_check=True)
                    m.then_inc(S("rounds_done"), 1)

                filled0 = list(used)
                more0 = 16 * QUADS * l
                with pe.Fori(0, QUADS) as q:
                    fg = lambda s: q * 16 + 16 + (16 * filled0[s] if s < SLOTS else more0)
                    with pe.If(rounds > 1):
                        with pe.Fori(1, rounds) as r:
                            one_round(q * rounds + before + r - 1, fg, fg)
                    one_round(q * rounds + before + rounds - 1, fg, fg)
                pe.matmul(ps[:, 3, :], zero_t[:, 0:P], zero_t[:, :], start=False, stop=True, skip_group_check=True) \
                    .then_inc(block_done, 1)
                n.block += 1
                n.x += 2
                n.pos = 0
                for s in range(SLOTS):
                    used[s] += QUADS

            moe(0)
            norm_tiles(LAT)
            pe.wait_ge(tp_evacuated, n.tp)
            for c in range(12):
                feature_major(SEQ, NT)
            token_major(LAT)
            token_major(LAT)
            pe.wait_ge(sem("gdn_constants"), 16 * 6)
            pe.wait_ge(x_updated, n.x)
            for t in range(2):
                for k in range(KC):
                    m = pe.matmul(ps[:, t, 0:16], hT[:, k, SEQ + t * P:SEQ + (t + 1) * P], w_gdn_ba[:, k, :],
                                  start=k == 0, stop=k == KC - 1)
            m.then_inc(sem("gd_ba"), 1)
            for t in range(2):
                for c in range(0, 24, 4):
                    if t == 0:
                        pe.wait_ge(sem("gd_conv"), c + 4)
                    transposes([gT[:, c + q, t * P:(t + 1) * P] for q in range(4)])
            pe.wait_ge(sem("gd_decays"), 1)
            pe.matmul(ps[:, 2, 0:16], s_le_t[:, :], g_t[:, 0, :], start=True, stop=True)
            pe.matmul(ps[:, 3, 0:16], ones_t[:, :], g_t[:, 0, :], start=True, stop=True).then_inc(sem("gd_sums"), 1)
            pe.wait_ge(sem("gd_norm"), 1)
            for src in ("k", "kb", "q"):
                for hd in range(0, 8, 2):
                    where = {"q": gtok, "k": gtok, "kb": gkb}[src]
                    off = {"q": 0, "k": 8, "kb": 0}[src]
                    transposes([where[:, t, off + hd + a, :] for a in range(2) for t in range(2)])
            pe.wait_ge(sem("gd_qe"), 1)
            for hd in range(0, 8, 4):
                transposes([gtok[:, 1, hd + a, :] for a in range(4)])
            pe.wait_ge(tp_evacuated, n.tp)
            for b in range(4):
                g, t = divmod(b, 2)
                c = slice(t * P, (t + 1) * P)
                if b >= 1:
                    pe.wait_ge(sem("gd_batch"), b)
                pe.wait_ge(sem("gd_gb"), b + 1)
                for a in range(4):
                    hd = 4 * g + a
                    col = slice(a * P, (a + 1) * P)
                    pe.matmul(ps[:, 0, col], TT[:, a, :], s_le_t[:, :], start=True, stop=True)
                    pe.matmul(ps[:, 1, col], g_kT[:, hd, c], g_kbT[:, hd, c], start=True, stop=True)
                    m = pe.matmul(ps[:, 2, col], g_kT[:, hd, c], g_qT[:, hd, c], start=True, stop=True)
                m.then_inc(sem("gd_scores"), 1)
                for lvl in range(LEVELS):
                    s0 = LEVELS * b + lvl
                    pe.wait_ge(sem("gd_lm"), s0 + 1)
                    for a in range(4):
                        m = pe.matmul(ps[:, 3, a * P:(a + 1) * P], LM[:, a, :], DD[:, a, :], start=True, stop=True)
                    m.then_inc(sem("gd_t"), 1)
                    pe.wait_ge(sem("gd_t_read"), s0 + 1)
                    for a in range(4):
                        pe.matmul(ps[:, 4, a * P:(a + 1) * P], DT_[:, a, :], TT[:, a, :], start=True, stop=True)
                    for a in range(4):
                        m = pe.matmul(ps[:, 5, a * P:(a + 1) * P], TT[:, a, :], DT_[:, a, :], start=True, stop=True)
                    m.then_inc(sem("gd_step"), 1)
                pe.wait_ge(sem("gd_inverse"), LEVELS * (b + 1))
                for a in range(4):
                    m = pe.matmul(ps[:, 0, a * P:(a + 1) * P], DT_[:, a, :], gtok[:, t, 16 + 4 * g + a, :], start=True, stop=True)
                if t == 1:
                    for a in range(4):
                        m = pe.matmul(ps[:, 1, a * P:(a + 1) * P], gkb[:, 1, 4 * g + a, :], DT_[:, a, :], start=True, stop=True)
                m.then_inc(sem("gd_u"), 1)
                pe.wait_ge(sem("gd_u_read"), b + 1)
                if t == 0:
                    for a in range(4):
                        pe.matmul(ps[:, 2, a * P:(a + 1) * P], AT[:, a, :], U[:, a, :], start=True, stop=True)
                    for a in range(4):
                        m = pe.matmul(ps[:, 3, a * P:(a + 1) * P], g_kdec[:, 4 * g + a, :], U[:, a, :], start=True, stop=True)
                    m.then_inc(sem("gd_o"), 1)
                else:
                    for a in range(4):
                        m = pe.matmul(ps[:, 2, a * P:(a + 1) * P], WT[:, a * P:(a + 1) * P], gS[:, a, :], start=True, stop=True)
                    m.then_inc(sem("gd_ws"), 1)
                    pe.wait_ge(sem("gd_vnew"), b // 2 + 1)
                    for a in range(4):
                        pe.matmul(ps[:, 3, a * P:(a + 1) * P], AT[:, a, :], U[:, a, :], start=True, stop=False)
                        m = pe.matmul(ps[:, 3, a * P:(a + 1) * P], gqe_T[:, 4 * g + a, :], gS[:, a, :], start=False, stop=True)
                    m.then_inc(sem("gd_o"), 1)
            mixed_tiles(g_o, range(2))
            mixer_out(LAT, SEQ)
            moe(1)

        @block.scalar
        def _(act):
            n = Counts()
            tell = Teller(act)

            def evacuate(dst, width=512, parts=P):
                act.wait_ge(tp_full, n.tp + 1)
                src = ps[0:parts, 6 + n.tp % 2, 0:width]
                n.tp += 1
                if len(dst.shape) == 3:
                    src = src.rearrange("p (a b) -> p a b", a=dst.shape[1])
                if len(dst.shape) == 4:
                    src = src.rearrange("p (a b c) -> p a b c", a=dst.shape[1], b=dst.shape[2])
                tell(nc.scalar.copy(dst, src), tp_evacuated)

            def root_of_norm():
                n.normed += 1
                act.wait_ge(sem("mean_square"), n.normed)
                tell(nc.scalar.activation(rs[:, 0:1], rs[:, 0:1], ACT.Sqrt), sem("rms_ready"))

            def norm_tiles(tiles):
                for t in tiles:
                    root_of_norm()
                    n.h += 1
                    for half in range(2):
                        evacuate(hT[:, 4 * half:4 * half + 4, t * P:(t + 1) * P])

            def mixed_tiles(tiles, col0):
                for t in tiles:
                    n.h += 1
                    for half in range(2):
                        evacuate(hT[:, 4 * half:4 * half + 4, t * P - col0:(t + 1) * P - col0])

            def update_tiles(tiles, block_of):
                for i, t in enumerate(tiles):
                    act.wait_ge(block_done, block_of(i))
                    if n.x > 0:
                        act.wait_ge(x_updated, n.x)
                    yt = ps[:, 2 * (i % 2):2 * (i % 2) + 2, :].rearrange("p a b -> p (a b)")
                    tell(nc.scalar.activation(junk[:, :], yt, ACT.Square, scale=float(D) ** -0.5,
                                              accum_out=ys[:, 0:1]), sem("act_step"))
                    tell(nc.scalar.activation(ys[:, 1:2], ys[:, 0:1], ACT.Sqrt, bias=eps_t[:, :]), sem("y_rms_ready"))
                    n.x += 1

            def mixer_out(tiles):
                b0 = n.block
                n.block += len(tiles)
                update_tiles(tiles, lambda i: b0 + i + 1)

            def act_loop(count):
                if count > 0:
                    with act.Fori(0, count) as r:
                        yield r

            def mlp(total, last=True):
                b0, tp0, gu0 = n.block, n.tp, n.gu
                told = tell.told.get("sig_ready", 0)

                def sigmoid(t, blk):
                    act.wait_ge(block_done, blk)
                    nc.scalar.activation(sig[:, t, :], ps[:, 4 + t, 0:EH], ACT.Sigmoid).then_inc(sem("sig_ready"), 1)

                def turn(i_par, full):
                    act.wait_ge(tp_full, full)
                    nc.scalar.copy(hidT[:, i_par, :, :], ps[:, 6 + (tp0 + i_par) % 2, :].rearrange("p (a b) -> p a b", a=2)) \
                        .then_inc(tp_evacuated, 1)

                for t in range(2):
                    sigmoid(t, b0 + 1 + t)
                pairs = (total - 1) // 2
                for r in act_loop(pairs):
                    for j in range(2):
                        sigmoid(0, r * 6 + (b0 + 3 * (j + 1)))
                        turn(j, r * 2 + (tp0 + j + 1))
                        sigmoid(1, r * 6 + (b0 + 3 * (j + 1) + 1))
                for i in range(2 * pairs, total):
                    if i + 1 < total:
                        sigmoid(0, b0 + 3 * (i + 1))
                    turn(i % 2, tp0 + i + 1)
                    if i + 1 < total:
                        sigmoid(1, b0 + 3 * (i + 1) + 1)
                tell.told["sig_ready"] = told + 2 * total
                tell.told["tp_evacuated"] = tp0 + total
                n.block += 3 * total
                n.tp += total
                n.gu += 2 * total
                b1 = n.block
                if last:
                    update_tiles(LAT, lambda i: b1)

            def sigmoid_blocks(count, c=None):
                for _ in range(count):
                    i = n.gu
                    n.block += 1
                    n.gu += 1
                    act.wait_ge(block_done, n.block)
                    act.wait_ge(gu_evacuated, i)
                    tell(nc.scalar.activation(g_sig, ps[:, 4 + i % 2, :], ACT.Sigmoid), sem("gate_sig"))

            act.wait_ge(sem("cond_loaded"), 48)
            tell(nc.scalar.activation(cond_sig[:, :, :], cond[:, :, :], ACT.Sigmoid), sem("cond_sig_ready"))
            n.block = n.gu = 48
            act.wait_ge(sem("zero_ready"), 1)
            norm_tiles(CTX)
            norm_tiles(LAT)
            n.block += 4
            n.gu += 4
            sigmoid_blocks(4)
            act.wait_ge(sem("lb_max"), 1)
            tell(nc.scalar.activation(lbs[:, 0:3, :, :], lbs[:, 0:3, :, :], ACT.Exp), sem("lb_exp"))
            for hp in range(2):
                n.block += 6
                n.gu += 6
                for hh in range(2):
                    hd = 2 * hp + hh
                    z = hg_z[:, hh, :, :]
                    act.wait_ge(gu_evacuated, n.gu)
                    if hd >= 1:
                        act.wait_ge(sem("hg_out"), 2 * hd)
                    tell(nc.scalar.activation(T1, z, ACT.Sigmoid), sem("act_step"))
                    tell(nc.scalar.activation(z, z, ACT.Sigmoid, scale=-1.0), sem("hg_sig"))
                    act.wait_ge(sem("hg_f"), hd + 1)
                    tell(nc.scalar.activation(T1, T1, ACT.Ln), sem("hg_log"))
                    act.wait_ge(sem("hg_d1"), hd + 1)
                    tell(nc.scalar.activation(E1, E4, ACT.Exp), sem("act_step"))
                    tell(nc.scalar.activation(E2, E4, ACT.Exp, scale=-1.0), sem("act_step"))
                    tell(nc.scalar.activation(E3, T2, ACT.Exp), sem("act_step"))
                    tell(nc.scalar.activation(E4, T1, ACT.Exp), sem("hg_exp"))
                    for d in range(2):
                        act.wait_ge(sem("hg_factors"), 2 * (hd + 1))
                        evacuate(T2[:, d, :])
            n.block += 4
            n.gu += 4
            sigmoid_blocks(4)
            for c in range(4):
                act.wait_ge(sem("ml_conv"), c + 1)
                tell(nc.scalar.activation(g_sig2, qk[:, c, :], ACT.Sigmoid), sem("ml_sig"))
                n.block += 1
                n.gu += 1
            act.wait_ge(sem("ml_abs"), 1)
            tell(nc.scalar.activation(rows_c, rows_c, ACT.Exp, scale=-1.0), sem("act_step"))
            tell(nc.scalar.activation(rows_c, rows_c, ACT.Ln, bias=1.0), sem("ml_log"))
            act.wait_ge(sem("ml_m"), 1)
            tell(nc.scalar.activation(rows_b, rows_b, ACT.Exp, scale=-1.0), sem("ml_em"))
            for i in range(2):
                act.wait_ge(tp_full, n.tp + 1)
                src = ps[:, 6 + n.tp % 2, :].rearrange("p (t c) -> p t c", t=4)[:, :, 0:ROWS]
                n.tp += 1
                tell(nc.scalar.copy(colsT[:, i, :, :], src), tp_evacuated)
            for i in range(8):
                for si in range(4):
                    k = 4 * i + si
                    act.wait_ge(sem("ml_gap"), k + 1)
                    w = wexp[:, k % 2, (0 if si < 2 else SEQ):NT]
                    tell(nc.scalar.activation(w, w, ACT.Exp, scale=-1.0), sem("ml_exp"))
            for t in range(4):
                act.wait_ge(sem("ab_ms"), t + 1)
                tell(nc.scalar.activation(msum[:, 0, :], msum[:, 0, :], ACT.Sqrt), sem("ab_rms"))
            mixed_tiles(range(4), 0)
            mixer_out((0, 1, 2, 3))
            norm_tiles(CTX)
            mlp(NFF)
            norm_tiles(LAT)
            mlp(NFF)
            norm_tiles(CTX)
            norm_tiles(LAT)
            n.block += 8
            n.gu += 8
            for i in range(6):
                act.wait_ge(sem("at_ms"), i + 1)
                w = 8 if i < 2 else 2
                tell(nc.scalar.activation(astat[:, 0, 0:w], astat[:, 0, 0:w], ACT.Sqrt), sem("at_rms"))
            for hd in range(0, 8, 2):
                evacuate(qT[:, hd:hd + 2, :])
            for kv in range(2):
                evacuate(kT[:, kv, :])
            for i in range(16):
                act.wait_ge(sem("at_max"), i + 1)
                tell(nc.scalar.activation(prob[:, i % 2, :], ps[:, 4 + i % 2, :], ACT.Exp, scale=float(P) ** -0.5,
                                          bias=smax[:, i % 2, 1:2], accum_out=smax[:, i % 2, 2:3]), sem("at_exp"))
                evacuate(probT[:, i % 2, :, :])
            mixer_out(LAT)
            norm_tiles(LAT)
            mlp(NFF)
            norm_tiles(LAT)
            n.block += 24
            n.gu += 24
            mixer_out(LAT)

            rounds_before = [0]

            def moe(l):
                norm_tiles(LAT)
                for t in range(2):
                    i = 2 * l + t
                    n.block += 1
                    n.gu += 1
                    act.wait_ge(sem("rt_shifted"), i + 1)
                    tell(nc.scalar.activation(rt1[:, 0:N_GROUPS], rt1[:, 0:N_GROUPS], ACT.Exp, accum_out=rt1[:, 8:9]), sem("act_step"))
                    tell(nc.scalar.activation(rt1[:, 9:10], rt1[:, 9:10], ACT.Exp), sem("act_step"))
                    tell(nc.scalar.activation(moe_gates[:, t, 64:65], ps[:, 4 + (n.gu - 1) % 2, ROUTE_W - 1:ROUTE_W], ACT.Sigmoid),
                         sem("rt_exp"))
                mlp(2, last=False)
                act.wait_ge(sem("rounds_known"), l + 1)
                rounds = act.value_load(rounds_i[0:1, 0:1], min_val=1, max_val=SEQ // CAP)
                S = sem
                before = 0 if l == 0 else rounds_before[0] * QUADS
                rounds_before[0] = rounds

                def one_round(c):
                    act.wait_ge(S("gathered"), c + 1)
                    nc.scalar.copy(x_slots[:, 0:4, :], ps[:, 4, :].rearrange("p (a b) -> p a b", a=4)).then_inc(S("x_slots_lo"), 1)
                    act.wait_ge(S("sel_turned"), c + 1)
                    nc.scalar.copy(sel_T, ps[:, 7, 0:SEQ]).then_inc(S("sel_T_ready"), 1)
                    act.wait_ge(S("quad_gate_up"), c + 1)
                    nc.scalar.activation(q_sig, ps[:, 6, 0:EH], ACT.Sigmoid).then_inc(S("quad_sig"), 1)
                    act.wait_ge(S("hid_turned"), c + 1)
                    nc.scalar.copy(q_hidT, ps[:, 7, SEQ:512].rearrange("p (a b) -> p a b", a=2)).then_inc(S("quad_hidT"), 1)
                    act.wait_ge(S("quad_down"), c + 1)
                    nc.scalar.copy(z_slots[:, 0:512], ps[:, 4, :]).then_inc(S("z_lo"), 1)

                with act.Fori(0, QUADS) as q:
                    with act.If(rounds > 1):
                        with act.Fori(1, rounds) as r:
                            one_round(q * rounds + before + r - 1)
                    one_round(q * rounds + before + rounds - 1)
                n.block += 1
                b1 = n.block
                update_tiles(LAT, lambda i: b1)

            moe(0)
            norm_tiles(LAT)
            for c in range(24):
                act.wait_ge(sem("gd_pre"), c + 1)
                tell(nc.scalar.activation(h[:, 0, 0:SEQ], gT[:, c, :], ACT.Sigmoid), sem("gd_sig"))
                n.block += 1
                n.gu += 1
            for c in range(4):
                i = n.gu
                n.block += 1
                n.gu += 1
                act.wait_ge(block_done, n.block)
                act.wait_ge(gu_evacuated, i)
                tell(nc.scalar.activation(junk[:, 0:512], ps[:, 4 + i % 2, :], ACT.Sigmoid), sem("gate_sig"))
            act.wait_ge(sem("gd_ba_read"), 1)
            tell(nc.scalar.activation(g_t[:, 1, :], g_t[:, 1, :], ACT.Sigmoid), sem("act_step"))
            tell(nc.scalar.activation(g_t[:, 3, :], g_t[:, 3, :], ACT.Exp, scale=-1.0), sem("act_step"))
            tell(nc.scalar.activation(g_t[:, 3, :], g_t[:, 3, :], ACT.Ln, bias=1.0), sem("act_step"))
            tell(nc.scalar.activation(gdn_vec[:, 2, :], gdn_vec[:, 0, :], ACT.Exp), sem("gd_act"))
            for t in range(2):
                for c in range(0, 24, 4):
                    evacuate(gtok[:, t, c:c + 4, :])
            for t in range(2):
                act.wait_ge(sem("gd_ms"), t + 1)
                tell(nc.scalar.activation(stat[:, 0:2, :], stat[:, 0:2, :], ACT.Sqrt), sem("gd_rms"))
            act.wait_ge(sem("gd_exparg"), 1)
            tell(nc.scalar.activation(g_t[:, 6, :], g_t[:, 4, :], ACT.Exp), sem("act_step"))
            tell(nc.scalar.activation(g_t[:, 7, :], g_t[:, 5, :], ACT.Exp), sem("act_step"))
            tell(nc.scalar.activation(g_t[:, 8, :], g_t[:, 8, :], ACT.Exp), sem("gd_exp"))
            for dst in (g_kT, g_kbT, g_qT):
                for hd in range(0, 8, 2):
                    evacuate(dst[:, hd:hd + 2, :])
            for hd in range(0, 8, 4):
                evacuate(gqe_T[:, hd:hd + 4, :])
            for b in range(4):
                act.wait_ge(sem("gd_gap"), b + 1)
                tell(nc.scalar.activation(LM, LM, ACT.Exp), sem("gd_dec"))
                for lvl in range(LEVELS):
                    act.wait_ge(sem("gd_t"), LEVELS * b + lvl + 1)
                    tell(nc.scalar.copy(TT, ps[:, 3, :].rearrange("p (a b) -> p a b", a=4)), sem("gd_t_read"))
            for t in range(2):
                act.wait_ge(sem("gd_oms"), t + 1)
                tell(nc.scalar.activation(stat[:, 0, :], stat[:, 0, :], ACT.Sqrt), sem("gd_orms"))
            mixed_tiles(range(2), 0)
            mixer_out(LAT)
            moe(1)

        @block.vector
        def _(dve):
            n = Counts()
            tell = Teller(dve)
            V = nc.vector
            step = sem("dve_step")
            h_turned = [0, 0]

            def do(ins):
                tell(ins, step)

            def gu_next():
                i = n.gu
                n.gu += 1
                n.block += 1
                dve.wait_ge(block_done, n.block)
                return ps[:, 4 + i % 2, :]

            pres, posts = [0], [0]

            def norm_tiles(tiles):
                pres[0] += 1
                for k, t in enumerate(tiles):
                    b = n.h % 2
                    if h_turned[b]:
                        dve.wait_ge(tp_full, h_turned[b])
                    do(V.tensor_tensor_reduce(out=h[:, b, :], in0=x_sb[:, t, :], in1=x_sb[:, t, :], scale=1.0 / D,
                                              scalar=0.0, op0=ALU.mult, op1=ALU.add, accum_out=rs[:, 0:1]))
                    tell(V.tensor_scalar(rs[:, 0:1], rs[:, 0:1], EPS, None, ALU.add), sem("mean_square"))
                    n.normed += 1
                    dve.wait_ge(sem("rms_ready"), n.normed)
                    do(V.reciprocal(rs[:, 1:2], rs[:, 0:1]))
                    if k == 0:
                        dve.wait_ge(sem("pre_ready"), pres[0])
                    do(V.scalar_tensor_tensor(out=h[:, b, :], in0=x_sb[:, t, :], scalar=rs[:, 1:2], in1=v_scale[:, :],
                                              op0=ALU.mult, op1=ALU.mult))
                    tell(V.tensor_tensor(h[:, b, :], h[:, b, :], v_shift[:, :], ALU.add), h_ready)
                    n.h += 1
                    n.tp += 2
                    h_turned[b] = n.tp

            def update_tiles(tiles):
                for i, t in enumerate(tiles):
                    if i % 2 == 0:
                        posts[0] += 1
                        dve.wait_ge(sem("post_ready"), posts[0])
                    yt = ps[:, 2 * (i % 2):2 * (i % 2) + 2, :].rearrange("p a b -> p (a b)")
                    dve.wait_ge(sem("y_rms_ready"), n.x + 1)
                    do(V.reciprocal(ys[:, 2:3], ys[:, 1:2]))
                    if h_turned[0]:
                        dve.wait_ge(tp_full, h_turned[0])
                    do(V.scalar_tensor_tensor(out=h[:, 0, :], in0=yt, scalar=ys[:, 2:3], in1=v_gate[:, :],
                                              op0=ALU.mult, op1=ALU.mult))
                    tell(V.tensor_tensor(x_sb[:, t, :], x_sb[:, t, :], h[:, 0, :], ALU.add), x_updated)
                    n.x += 1

            def dve_loop(count):
                if count > 0:
                    with dve.Fori(0, count) as r:
                        yield r

            def mlp(total, tiles, gated, last=True):
                b0, gu0, tp0 = n.block, n.gu, n.tp
                sg0 = tell.told.get("sig_seen", 0)

                def hidden(i_par, t, sig_count, sw_count):
                    dve.wait_ge(sem("sig_ready"), sig_count)
                    g = gate_now[:, t, i_par:i_par + 1] if gated else 1.0
                    V.scalar_tensor_tensor(out=swish[:, t, :], in0=ps[:, 4 + t, 0:EH], scalar=g, in1=sig[:, t, :],
                                           op0=ALU.mult, op1=ALU.mult).then_inc(sem("swish_ready"), 1)
                    dve.wait_ge(sem("swish_ready"), sw_count)
                    V.tensor_tensor(hid[:, i_par, t, :], swish[:, t, :], ps[:, 4 + t, EH:2 * EH], ALU.mult).then_inc(gu_evacuated, 1)

                def pick(i0, count, width=2):
                    if gated:
                        V.tensor_copy(gate_now[:, :, 0:2], moe_gates[:, :, 64:66]).then_inc(sem("gates_picked"), 1)
                        dve.wait_ge(sem("gates_picked"), count)

                pk0 = tell.told.get("gates_picked", 0)
                pairs = total // 2
                for r in dve_loop(pairs):
                    pick(bass.ds(r * 2, 2), r + (pk0 + 1))
                    for j in range(2):
                        for t in range(2):
                            k = 2 * j + t
                            hidden(j, t, r * 4 + (sg0 + k + 1), r * 4 + (sg0 + k + 1))
                for i in range(2 * pairs, total):
                    for t in range(2):
                        k = 2 * i + t
                        hidden(i % 2, t, sg0 + k + 1, sg0 + k + 1)
                if gated:
                    tell.told["gates_picked"] = pk0 + pairs
                tell.told["sig_seen"] = sg0 + 2 * total
                tell.told["gu_evacuated"] = gu0 + 2 * total
                n.gu += 2 * total
                n.block += 3 * total
                n.tp += total
                if last:
                    update_tiles(tiles)

            do(V.memset(eps_t[:, :], EPS))
            do(V.memset(ones_t[:, :], 1.0))
            tell(V.memset(zero_t[:, :], 0.0), sem("zero_ready"))
            dve.wait_ge(sem("cond_sig_ready"), 1)
            tell(V.tensor_tensor(cond[:, :, :], cond[:, :, :], cond_sig[:, :, :], ALU.mult), sem("cond_ready"))
            for l, (name, j, rows) in enumerate(ADA):
                m_ = len(rows)
                dve.wait_ge(sem(f"ada_bias_loaded_{l}"), 16 * m_)
                with dve.Fori(0, 2) as r:
                    for q in range(6):
                        dve.wait_ge(block_done, r * 6 + (12 * l + q + 1))
                        at = mod_rows[0:m_, l % 2, bass.ds(r * (6 * 512) + q * 512, 512)]
                        V.tensor_tensor(at, at, ps[0:m_, 4 + q % 2, :], ALU.add).then_inc(gu_evacuated, 1)
                dve.wait_ge(gu_evacuated, 12 * (l + 1))
                tell(V.tensor_copy(note[:, :], eps_t[0:1, :]), sem("mod_row_ready"))
            tell.told["gu_evacuated"] = 48
            n.gu = n.block = 48

            dve.wait_ge(x_loaded, 32)
            norm_tiles(CTX)
            norm_tiles(LAT)
            for l in range(4):
                dve.wait_ge(sem(f"mod_stored_{l}"), 16)
            do(V.memset(v_tok[:, :, :, 128:129], 1.0))
            for t in range(4):
                src = gu_next()
                tell(V.tensor_copy(v_tok[:, t, :, 0:P], src.rearrange("p (h e) -> p h e", h=4)), gu_evacuated)
            gates_seen = 0
            for t in range(4):
                src = gu_next()
                gates_seen += 1
                dve.wait_ge(sem("gate_sig"), gates_seen)
                tell(V.tensor_tensor(gate[:, t, 0:512], src, g_sig, ALU.mult), gu_evacuated)
            dve.wait_ge(sem("ab_constants"), 16 * (2 + 8 + 2))
            do(V.tensor_tensor(lbs[:, 3], lbs[:, 0], lbs[:, 1], ALU.max))
            do(V.tensor_tensor(lbs[:, 3], lbs[:, 3], lbs[:, 2], ALU.max))
            for k in range(3):
                ins = V.tensor_tensor(lbs[:, k], lbs[:, k], lbs[:, 3], ALU.subtract)
                if k < 2:
                    do(ins)
                else:
                    tell(ins, sem("lb_max"))
            dve.wait_ge(sem("lb_exp"), 1)
            do(V.tensor_tensor(lbs[:, 3], lbs[:, 0], lbs[:, 1], ALU.add))
            do(V.tensor_tensor(lbs[:, 3], lbs[:, 3], lbs[:, 2], ALU.add))
            do(V.reciprocal(lbs[:, 3], lbs[:, 3]))
            do(V.tensor_tensor(lbs[:, 4], lbs[:, 0], lbs[:, 3], ALU.mult))
            do(V.tensor_scalar(lbs[:, 5], lbs[:, 4], -1.0, 1.0, ALU.mult, ALU.add))
            for hp in range(2):
                for part in range(3):
                    for hh in range(2):
                        dst = hg_q[:, hh, :] if part == 0 else hg_z[:, hh, part - 1, :]
                        tell(V.tensor_copy(dst, gu_next()), gu_evacuated)
                for hh in range(2):
                    hd = 2 * hp + hh
                    dve.wait_ge(sem("hg_sig"), hd + 1)
                    for d in range(2):
                        lb, om = lbs[:, 4, d, hd:hd + 1], lbs[:, 5, d, hd:hd + 1]
                        do(V.tensor_scalar(hg_z[:, hh, d, :], hg_z[:, hh, d, :], om, None, ALU.mult))
                        ins = V.tensor_scalar(T1[:, d, :], T1[:, d, :], om, lb, ALU.mult, ALU.add)
                        do(ins) if d == 0 else tell(ins, sem("hg_f"))
                    dve.wait_ge(sem("hg_log"), hd + 1)
                    do(V.tensor_tensor_scan(T2[:, 0, :], chunk_starts, T1[:, 0, :], 0.0, ALU.mult, ALU.add))
                    do(V.tensor_tensor_scan(T2[:, 1, ::-1], chunk_starts, T1[:, 1, ::-1], 0.0, ALU.mult, ALU.add))
                    for d in range(2):
                        bc = T2[:, d, :].rearrange("p (c t) -> p c t", t=SCAN_CHUNK)
                        mid = 15 if d == 0 else 16
                        last = 31 if d == 0 else 0
                        do(V.tensor_tensor(E4[:, d, :].rearrange("p (c t) -> p c t", t=SCAN_CHUNK), bc,
                                           bc[:, :, mid:mid + 1].broadcast_to([P, NSC, SCAN_CHUNK]), ALU.subtract))
                        ins = V.tensor_tensor(T1[:, d, :].rearrange("p (c t) -> p c t", t=SCAN_CHUNK),
                                              bc[:, :, last:last + 1].broadcast_to([P, NSC, SCAN_CHUNK]), bc, ALU.subtract)
                        do(ins) if d == 0 else tell(ins, sem("hg_d1"))
                    dve.wait_ge(sem("hg_exp"), hd + 1)
                    for d in range(2):
                        last = 31 if d == 0 else 0
                        do(V.tensor_copy(dec[:, d, :], E3[:, d, last::SCAN_CHUNK]))
                        do(V.tensor_tensor(E1[:, d, :], E1[:, d, :], hg_q[:, hh, :], ALU.mult))
                        do(V.tensor_tensor(E2[:, d, :], E2[:, d, :], hg_z[:, hh, d, :], ALU.mult))
                        do(V.tensor_tensor(E3[:, d, :], E3[:, d, :], hg_q[:, hh, :], ALU.mult))
                        tell(V.tensor_tensor(E4[:, d, :], E4[:, d, :], hg_z[:, hh, d, :], ALU.mult), sem("hg_factors"))
                    for d in range(2):
                        i = 2 * hd + d
                        dve.wait_ge(sem("hg_scores"), i + 1)
                        at3 = T1[:, d, :].rearrange("p (t c) -> p t c", t=4)
                        do(V.tensor_scalar(T1[:, d, :], ps[:, 4, :], MAXF, -MAXF, ALU.min, ALU.max))
                        tell(V.tensor_tensor(at3, at3, chunk_masks[:, d:d + 1, :].broadcast_to([P, 4, P]), ALU.mult),
                             sem("hg_scores_read"))
                        dve.wait_ge(sem("hg_updates"), i + 1)
                        order = list(range(NSC)) if d == 0 else list(range(7, -1, -1)) + list(range(15, 7, -1))
                        if i >= 1:
                            dve.wait_ge(sem("hg_out"), i)
                        for a, c in zip(order[:-1], order[1:]):
                            upd = ps[:, a % 4, (a // 4) * P:(a // 4 + 1) * P]
                            if a == order[0]:
                                ins = V.tensor_copy(state[:, c, :], upd)
                            else:
                                ins = V.scalar_tensor_tensor(out=state[:, c, :], in0=state[:, a, :], scalar=dec[:, d, a:a + 1],
                                                             in1=upd, op0=ALU.mult, op1=ALU.add)
                            do(ins) if c != order[-1] else tell(ins, sem("hg_states"))
                        dve.wait_ge(sem("hg_out"), i + 1)
                        dst = o[:, :, hd * P:(hd + 1) * P]
                        src = ps[:, 5, :].rearrange("p (t e) -> p t e", t=4)
                        if d == 0:
                            tell(V.tensor_copy(dst, src), sem("hg_out_read"))
                        else:
                            tell(V.tensor_tensor(dst, dst, src, ALU.add), sem("hg_out_read"))
                        n.tp += 1
            tell(V.tensor_copy(note[:, :], eps_t[0:1, :]), sem("hgrn_done"))
            for t in range(4):
                src = gu_next()
                tell(V.tensor_copy(v_tok[:, t, :, 0:P], src.rearrange("p (h e) -> p h e", h=4)), gu_evacuated)
            for t in range(4):
                src = gu_next()
                gates_seen += 1
                dve.wait_ge(sem("gate_sig"), gates_seen)
                tell(V.tensor_copy(gate[:, t, 512:1024], g_sig), gu_evacuated)
            for c in range(4):
                src = gu_next().rearrange("p (s t) -> p s t", s=2)
                dst = qk[:, c, :].rearrange("p (s t) -> p s t", s=2)
                w = [w_conv[:, c, k:k + 1] for k in range(3)]
                do(V.tensor_scalar(dst, src, w[1], None, ALU.mult))
                do(V.scalar_tensor_tensor(out=dst[:, :, 1:SEQ], in0=src[:, :, 0:SEQ - 1], scalar=w[0], in1=dst[:, :, 1:SEQ],
                                          op0=ALU.mult, op1=ALU.add))
                tell(V.scalar_tensor_tensor(out=dst[:, :, 0:SEQ - 1], in0=src[:, :, 1:SEQ], scalar=w[2],
                                            in1=dst[:, :, 0:SEQ - 1], op0=ALU.mult, op1=ALU.add), sem("ml_conv"))
                dve.wait_ge(sem("ml_sig"), c + 1)
                do(V.tensor_tensor(qk[:, c, :], qk[:, c, :], g_sig2, ALU.mult))
                tell(V.tensor_scalar(qk[:, c, :], qk[:, c, :], 0.125 if c < 2 else 1.0, None, ALU.mult), sem("ml_qk"))
                dve.wait_ge(block_done, n.block)
                tell(V.tensor_copy(note[:, :], eps_t[0:1, :]), gu_evacuated)
            dve.wait_ge(sem("ml_gates"), 1)
            R = slice(0, ROWS)
            do(V.tensor_scalar(rows_a, ps[R, 0, :], gate_bias[R, 0:1], None, ALU.add))
            do(V.tensor_scalar(rows_b, ps[R, 1, :], gate_bias[R, 1:2], None, ALU.add))
            do(V.tensor_scalar(rows_c, rows_b, -1.0, None, ALU.mult))
            tell(V.tensor_tensor(rows_c, rows_c, rows_b, ALU.max), sem("ml_abs"))
            dve.wait_ge(sem("ml_log"), 1)
            do(V.scalar_tensor_tensor(out=rows_b, in0=rows_b, scalar=0.0, in1=rows_c, op0=ALU.min, op1=ALU.subtract))

            def turned(dst, src):
                do(V.tensor_copy(dst[0:32, :], src[0:32, :]))
                do(V.tensor_copy(dst[32:ROWS, :].rearrange("p (s t) -> p s t", s=2),
                                 src[32:ROWS, :].rearrange("p (s t) -> p s t", s=2)[:, :, ::-1]))

            turned(rows_e, rows_a)
            turned(rows_f, rows_b)
            do(V.memset(rows_a, 1.0))
            do(V.tensor_tensor_scan(rows_b, rows_a, rows_f, 0.0, ALU.mult, ALU.add))
            do(V.tensor_tensor(rows_e, rows_e, rows_b, ALU.subtract))
            do(V.tensor_tensor_scan(rows_c, rows_e, rows_e, 0.0, ALU.max, ALU.max))
            tell(V.tensor_tensor(rows_b, rows_b, rows_c, ALU.add), sem("ml_m"))
            turned(rows_d, rows_c)
            do(V.tensor_copy(rows_c, rows_e))
            turned(rows_e, rows_c)
            dve.wait_ge(sem("ml_em"), 1)
            turned(rows_f, rows_b)
            tell(V.tensor_copy(note[:, :], eps_t[0:1, :]), sem("ml_rows"))
            n.tp += 2
            dve.wait_ge(tp_evacuated, n.tp)
            for hd in range(MLSTM_HEADS):
                dve.wait_ge(sem("ml_scores"), hd + 1)
                for d in range(2):
                    i = 2 * hd + d
                    row = 32 * d + hd
                    dve.wait_ge(sem("ml_max"), i + 1)
                    if i >= 1:
                        dve.wait_ge(sem("ml_out"), i)
                    for si in range(4):
                        c0 = 0 if si < 2 else SEQ
                        w = wexp[:, (4 * i + si) % 2, c0:NT]
                        tell(V.tensor_scalar(w, ps[:, 4 + d, c0:NT], colsT[:, 0, si, row:row + 1], 0.0,
                                             ALU.subtract, ALU.max), sem("ml_gap"))
                        dve.wait_ge(sem("ml_exp"), 4 * i + si + 1)
                        do(V.tensor_tensor(p_sb[:, si, c0:NT], w, ps[:, si, c0:NT], ALU.mult))
                        own = p_sb[:, si, si * P:(si + 1) * P]
                        tell(V.tensor_tensor(own, own, (s_le_t if d == 0 else s_ge_t)[:, :], ALU.mult), sem("ml_weights"))
                    dve.wait_ge(sem("ml_out"), i + 1)
                    for ti in range(4):
                        src = ps[:, 6 + ti // 2, (ti % 2) * 129:(ti % 2) * 129 + 129]
                        dn, em = mden[:, 0, ti:ti + 1], colsT[:, 1, ti, row:row + 1]
                        do(V.tensor_copy(mden[:, 1, ti:ti + 1], src[:, P:P + 1]))
                        do(V.tensor_scalar(dn, mden[:, 1, ti:ti + 1], -1.0, None, ALU.mult))
                        do(V.tensor_tensor(dn, dn, mden[:, 1, ti:ti + 1], ALU.max))
                        do(V.tensor_tensor(dn, dn, em, ALU.max))
                        do(V.reciprocal(dn, dn))
                        dst = o[:, ti, 512 + hd * P:512 + (hd + 1) * P]
                        if d == 0:
                            ins = V.tensor_scalar(dst, src[:, 0:P], dn, None, ALU.mult)
                        else:
                            ins = V.scalar_tensor_tensor(out=dst, in0=src[:, 0:P], scalar=dn, in1=dst,
                                                         op0=ALU.mult, op1=ALU.add)
                        do(ins) if ti < 3 else tell(ins, sem("ml_out_read"))
            tell(V.tensor_copy(note[:, :], eps_t[0:1, :]), sem("mlstm_done"))
            for t in range(4):
                ot = o[:, t, :]
                oh = ot.rearrange("p (h e) -> p h e", h=8)
                do(V.tensor_tensor(h[:, 0, :], ot, ot, ALU.mult))
                do(V.tensor_reduce(msum[:, 0, :], h[:, 0, :].rearrange("p (h e) -> p h e", h=8), AX_X, ALU.add))
                tell(V.tensor_scalar(msum[:, 0, :], msum[:, 0, :], 1.0 / P, EPS, ALU.mult, ALU.add), sem("ab_ms"))
                dve.wait_ge(sem("ab_rms"), t + 1)
                do(V.reciprocal(msum[:, 1, :], msum[:, 0, :]))
                do(V.tensor_tensor(oh, oh, msum[:, 1, :].rearrange("p (h o) -> p h o", o=1).broadcast_to([P, 8, P]), ALU.mult))
                if t == 0:
                    dve.wait_ge(sem("out_g_loaded"), 16)
                do(V.tensor_tensor(ot, ot, out_g, ALU.mult))
                tell(V.tensor_tensor(ot, ot, gate[:, t, :], ALU.mult), h_ready)
                n.h += 1
                n.tp += 2
            n.block += 4
            update_tiles((0, 1, 2, 3))
            norm_tiles(CTX)
            mlp(NFF, CTX, False)
            norm_tiles(LAT)
            mlp(NFF, LAT, False)

            norm_tiles(CTX)
            norm_tiles(LAT)
            for pair in range(2):
                for t in range(2):
                    tell(V.tensor_copy(aq[:, t, 4 * pair:4 * pair + 4, :], gu_next().rearrange("p (h e) -> p h e", h=4)), gu_evacuated)
            for t in range(4):
                src = gu_next().rearrange("p (h e) -> p h e", h=4)
                do(V.tensor_copy(ak[:, t, :, :], src[:, 0:2, :]))
                tell(V.tensor_copy(av[:, t, :, :], src[:, 2:4, :]), gu_evacuated)

            def head_norm(xin, heads, which, i):
                sq = asq[:, 0:heads, :]
                st0, st1 = astat[:, 0, 0:heads], astat[:, 1, 0:heads]
                do(V.tensor_tensor(sq, xin, xin, ALU.mult))
                do(V.tensor_reduce(st0, sq, AX_X, ALU.add))
                tell(V.tensor_scalar(st0, st0, 1.0 / P, EPS, ALU.mult, ALU.add), sem("at_ms"))
                dve.wait_ge(sem("at_rms"), i + 1)
                do(V.reciprocal(st1, st0))
                do(V.tensor_tensor(xin, xin, st1.rearrange("p (h o) -> p h o", o=1).broadcast_to([P, heads, P]), ALU.mult))
                do(V.tensor_tensor(xin, xin, qk_g[:, which:which + 1, :].broadcast_to([P, heads, P]), ALU.mult))

            def rotate(dst, xin, heads, t, s):
                cs, sn = (rope[:, t, i, :].rearrange("p (o a e) -> p o a e", o=1, a=2).broadcast_to([P, heads, 2, 32]) for i in range(2))
                x4 = xin.rearrange("p h (a q e) -> p h a q e", a=2, q=2)
                d4 = dst.rearrange("p h (a q e) -> p h a q e", a=2, q=2)
                w = asq[:, 0:heads, 0:64].rearrange("p h (a e) -> p h a e", a=2)
                x1, x2 = x4[:, :, :, 0, :], x4[:, :, :, 1, :]
                do(V.tensor_tensor(d4[:, :, :, 0, :], x1, cs, ALU.mult))
                do(V.tensor_tensor(w, x2, sn, ALU.mult))
                do(V.tensor_tensor(d4[:, :, :, 0, :], d4[:, :, :, 0, :], w, ALU.subtract))
                do(V.tensor_tensor(d4[:, :, :, 1, :], x2, cs, ALU.mult))
                do(V.tensor_tensor(w, x1, sn, ALU.mult))
                tell(V.tensor_tensor(d4[:, :, :, 1, :], d4[:, :, :, 1, :], w, ALU.add), s)

            dve.wait_ge(sem("att_constants"), 48)
            for t in range(2):
                head_norm(aq[:, t, :, :], 8, 0, t)
                rotate(aqr[:, t, :, :], aq[:, t, :, :], 8, t, sem("at_q_ready"))
            for t in range(4):
                head_norm(ak[:, t, :, :], 2, 1, 2 + t)
                if t < 2:
                    tell(V.tensor_copy(akr[:, t, :, :], ak[:, t, :, :]), sem("at_k_ready"))
                else:
                    rotate(akr[:, t, :, :], ak[:, t, :, :], 2, t - 2, sem("at_k_ready"))
            n.tp += 6
            for i in range(16):
                dve.wait_ge(sem("at_scores"), i + 1)
                sm = smax[:, i % 2, :]
                if i >= 2:
                    dve.wait_ge(tp_full, n.tp - 1)
                do(V.tensor_reduce(sm[:, 0:1], ps[:, 4 + i % 2, :], AX_X, ALU.max))
                tell(V.tensor_scalar(sm[:, 1:2], sm[:, 0:1], -float(P) ** -0.5, None, ALU.mult), sem("at_max"))
                dve.wait_ge(sem("at_exp"), i + 1)
                do(V.reciprocal(sm[:, 3:4], sm[:, 2:3]))
                tell(V.tensor_scalar(prob[:, i % 2, :], prob[:, i % 2, :], sm[:, 3:4], None, ALU.mult), sem("at_prob"))
                n.tp += 1
            dve.wait_ge(sem("at_out"), 16)
            for b in range(4):
                tell(V.tensor_copy(hT[:, 2 * b:2 * b + 2, SEQ:NT], ps[:, b, :].rearrange("p (h t) -> p h t", h=2)), sem("at_outT"))
            n.block += 2
            update_tiles(LAT)
            norm_tiles(LAT)
            mlp(NFF, LAT, False)

            norm_tiles(LAT)
            dve.wait_ge(sem("sconv_w_loaded"), 16)
            for c in range(4):
                for q in range(2):
                    tell(V.tensor_copy(cv_b[:, q, :], gu_next()[:, 0:SEQ]), gu_evacuated)
                for q in range(2):
                    tell(V.tensor_copy(cv_g[:, q, :], gu_next()[:, 0:SEQ]), gu_evacuated)
                for q in range(2):
                    ch = 2 * c + q
                    tell(V.tensor_tensor(cv_g[:, q, :], cv_g[:, q, :], gu_next()[:, 0:SEQ], ALU.mult), gu_evacuated)
                    u, y = cv_g[:, q, :], cv_y[:, q, :]
                    do(V.tensor_scalar(y, u, w_sconv[:, ch, 2:3], None, ALU.mult))
                    do(V.scalar_tensor_tensor(out=y[:, 1:], in0=u[:, 0:SEQ - 1], scalar=w_sconv[:, ch, 1:2], in1=y[:, 1:],
                                              op0=ALU.mult, op1=ALU.add))
                    do(V.scalar_tensor_tensor(out=y[:, 2:], in0=u[:, 0:SEQ - 2], scalar=w_sconv[:, ch, 0:1], in1=y[:, 2:],
                                              op0=ALU.mult, op1=ALU.add))
                    tell(V.tensor_tensor(hT[:, ch, 0:SEQ], y, cv_b[:, q, :], ALU.mult), sem("sconv_ready"))
            n.block += 2
            update_tiles(LAT)

            rounds_before = [0]

            def moe(l):
                norm_tiles(LAT)
                dve.wait_ge(sem("route_w_ready"), l + 1)
                for t in range(2):
                    i = 2 * l + t
                    src = gu_next()
                    gl, el = rt[:, 0, 0:8], rt[:, 1, :]
                    el3 = el.rearrange("p (g e) -> p g e", g=8)
                    do(V.tensor_tensor(gl, src[:, 0:8], route_b[:, 0:8], ALU.add))
                    do(V.tensor_tensor(el, src[:, 8:72], route_b[:, 8:72], ALU.add))
                    do(V.tensor_reduce(rt1[:, 11:12], gl, AX_X, ALU.max))
                    do(V.tensor_scalar(rt[:, 2, 0:8], gl, rt1[:, 11:12], None, ALU.is_equal))
                    first_of(rt[:, 2, 0:8], rt[:, 3, 0:8])
                    do(V.tensor_scalar(rt[:, 3, 0:8], rt[:, 2, 0:8], -1.0, BIG, ALU.add, ALU.mult))
                    do(V.tensor_tensor(el3, el3, rt[:, 3, 0:8].rearrange("p (g o) -> p g o", o=1).broadcast_to([P, 8, 8]), ALU.add))
                    do(V.tensor_reduce(rt1[:, 12:13], el, AX_X, ALU.max))
                    do(V.tensor_scalar(rt[:, 4, :], el, rt1[:, 12:13], None, ALU.is_equal))
                    first_of(rt[:, 4, :], rt[:, 3, :])
                    do(V.tensor_copy(rt[:, 7, :], rt[:, 4, :]))
                    do(V.scalar_tensor_tensor(out=rt[:, 5, :], in0=rt[:, 4, :], scalar=-2 * BIG, in1=el, op0=ALU.mult, op1=ALU.add))
                    do(V.tensor_reduce(rt1[:, 13:14], rt[:, 5, :], AX_X, ALU.max))
                    do(V.tensor_scalar(rt[:, 6, :], rt[:, 5, :], rt1[:, 13:14], None, ALU.is_equal))
                    first_of(rt[:, 6, :], rt[:, 3, :])
                    do(V.tensor_tensor(rt1[:, 9:10], rt1[:, 13:14], rt1[:, 12:13], ALU.subtract))
                    tell(V.tensor_scalar(rt1[:, 0:8], gl, rt1[:, 11:12], None, ALU.subtract), sem("rt_shifted"))
                    dve.wait_ge(sem("rt_exp"), i + 1)
                    do(V.tensor_scalar(rt1[:, 10:11], rt1[:, 9:10], 1.0, None, ALU.add))
                    do(V.tensor_tensor(rt1[:, 10:11], rt1[:, 10:11], rt1[:, 8:9], ALU.mult))
                    do(V.reciprocal(rt1[:, 10:11], rt1[:, 10:11]))
                    do(V.tensor_tensor(rt1[:, 14:15], rt1[:, 10:11], rt1[:, 9:10], ALU.mult))
                    do(V.tensor_scalar(rt[:, 4, :], rt[:, 4, :], rt1[:, 10:11], None, ALU.mult))
                    do(V.scalar_tensor_tensor(out=moe_gates[:, t, 0:64], in0=rt[:, 6, :], scalar=rt1[:, 14:15], in1=rt[:, 4, :],
                                              op0=ALU.mult, op1=ALU.add))
                    tell(V.tensor_tensor(picked[:, t, :], rt[:, 6, :], rt[:, 7, :], ALU.add), sem("picked_ready"))
                    tell(V.tensor_copy(moe_gates[:, t, 65:66], moe_gates[:, t, 64:65]), gu_evacuated)
                mlp(2, LAT, True, last=False)
                dve.wait_ge(sem("ranks_summed"), l + 1)
                do(V.tensor_tensor(rank, ps[:, 4, 0:128].rearrange("p (t e) -> p t e", t=2), picked, ALU.mult))
                do(V.tensor_scalar(rank, rank, -1.0, None, ALU.add))
                do(V.tensor_reduce(over[:, 0:1], ps[:, 4, 128:192], AX_X, ALU.max))
                do(V.tensor_scalar(over[:, 1:SEQ // CAP], round_limits, over[:, 0:1], None, ALU.is_lt))
                do(V.tensor_reduce(over[:, 0:1], over[:, 1:SEQ // CAP], AX_X, ALU.add))
                do(V.tensor_scalar(over[:, 0:1], over[:, 0:1], 1.0, None, ALU.add))
                tell(V.tensor_copy(rounds_i[:, :], over[:, 0:1]), sem("rounds_known"))
                rounds = dve.value_load(rounds_i[0:1, 0:1], min_val=1, max_val=SEQ // CAP)
                S = sem
                before = 0 if l == 0 else rounds_before[0] * QUADS
                rounds_before[0] = rounds
                if l == 0:
                    V.tensor_copy(note[:, :], eps_t[0:1, :]).then_inc(S("rounds_done"), 1)
                    dve.wait_ge(S("rounds_done"), 1)

                def one_round(c, ranks, q, main=False):
                    dve.wait_ge(S("ranks_picked"), q * 3 + (3 * QUADS * l + 3))
                    V.tensor_scalar(r_rank_x, r_rank_x, -float(CAP), None, ALU.add).then_inc(S("rank_lowered"), 1)
                    dve.wait_ge(S("rank_lowered"), c + 1)
                    dve.wait_ge(S("rounds_done"), c + 1)
                    V.tensor_tensor(sel.rearrange("p t (a s) -> p (t a) s", a=QUAD),
                                    slot_index.rearrange("p (o s) -> p o s", o=1).broadcast_to([P, 2 * QUAD, CAP]),
                                    ranks.rearrange("p t (a o) -> p (t a) o", o=1).broadcast_to([P, 2 * QUAD, CAP]),
                                    ALU.is_equal).then_inc(S("sel_ready"), 1)
                    dve.wait_ge(S("sel_ready"), c + 1)
                    V.tensor_tensor(sel_gated.rearrange("p t (a s) -> p (t a) s", a=QUAD),
                                    sel.rearrange("p t (a s) -> p (t a) s", a=QUAD),
                                    r_gate.rearrange("p t (a o) -> p (t a) o", o=1).broadcast_to([P, 2 * QUAD, CAP]),
                                    ALU.mult).then_inc(S("sel_gated_ready"), 1)
                    dve.wait_ge(S("gathered"), c + 1)
                    V.tensor_copy(x_slots[:, 4:8, :], ps[:, 5, :].rearrange("p (a b) -> p a b", a=4)).then_inc(S("x_slots_hi"), 1)
                    dve.wait_ge(S("quad_sig"), c + 1)
                    V.tensor_tensor(q_swish, ps[:, 6, 0:EH], q_sig, ALU.mult).then_inc(S("quad_swish"), 1)
                    dve.wait_ge(S("quad_swish"), c + 1)
                    V.tensor_tensor(q_hid, q_swish, ps[:, 6, EH:2 * EH], ALU.mult).then_inc(S("quad_hid"), 1)
                    if main:
                        V.tensor_copy(note[:, :], eps_t[0:1, :]).then_inc(S("quad_gate_up_used"), 1)
                        dve.wait_ge(S("quad_gate_up_used"), q + (QUADS * l + 1))
                    dve.wait_ge(S("quad_down"), c + 1)
                    V.tensor_copy(z_slots[:, 512:D], ps[:, 5, :]).then_inc(S("z_hi"), 1)
                    if main:
                        V.tensor_copy(note[:, :], eps_t[0:1, :]).then_inc(S("quad_down_used"), 1)
                        dve.wait_ge(S("quad_down_used"), q + (QUADS * l + 1))

                with dve.Fori(0, QUADS) as q:
                    V.tensor_copy(r_gate, moe_gates[:, :, bass.ds(q * QUAD, QUAD)]).then_inc(S("ranks_picked"), 1)
                    V.tensor_copy(r_rank, rank[:, :, bass.ds(q * QUAD, QUAD)]).then_inc(S("ranks_picked"), 1)
                    dve.wait_ge(S("ranks_picked"), q * 3 + (3 * QUADS * l + 2))
                    V.tensor_copy(r_rank_x, r_rank).then_inc(S("ranks_picked"), 1)
                    with dve.If(rounds > 1):
                        with dve.Fori(1, rounds) as r:
                            one_round(q * rounds + before + r - 1, r_rank_x, q)
                    one_round(q * rounds + before + rounds - 1, r_rank, q, True)
                n.block += 1
                update_tiles(LAT)

            def first_of(mask, w):
                do(V.tensor_tensor_scan(w, mask, mask, 0.0, ALU.add, ALU.max))
                do(V.tensor_scalar(w, w, 1.0, None, ALU.is_equal))
                do(V.tensor_tensor(mask, mask, w, ALU.mult))

            moe(0)
            norm_tiles(LAT)
            dve.wait_ge(sem("gdn_constants"), 16 * 6)
            dve.wait_ge(tp_evacuated, n.tp)
            for c in range(24):
                src, dst = gu_next(), gT[:, c, :]
                do(V.tensor_scalar(dst, src[:, 0:SEQ], w_gconv[:, c, 3:4], None, ALU.mult))
                for k in range(1, 4):
                    ins = V.scalar_tensor_tensor(out=dst[:, k:], in0=src[:, 0:SEQ - k], scalar=w_gconv[:, c, 3 - k:4 - k],
                                                 in1=dst[:, k:], op0=ALU.mult, op1=ALU.add)
                    if k < 3:
                        do(ins)
                    else:
                        tell(ins, gu_evacuated)
                tell(V.tensor_copy(note[:, :], eps_t[0:1, :]), sem("gd_pre"))
                dve.wait_ge(sem("gd_sig"), c + 1)
                tell(V.tensor_tensor(dst, dst, h[:, 0, 0:SEQ], ALU.mult), sem("gd_conv"))
            for half in range(2):
                for t in range(2):
                    src = gu_next()
                    gates_seen += 1
                    dve.wait_ge(sem("gate_sig"), gates_seen)
                    tell(V.tensor_tensor(g_z[:, t, 512 * half:512 * half + 512], src, junk[:, 0:512], ALU.mult), gu_evacuated)
            dve.wait_ge(sem("gd_ba"), 1)
            for t in range(2):
                col = slice(8 * t, 8 * t + 8)
                do(V.tensor_copy(g_t[:, 1, col], ps[:, t, 0:8]))
                do(V.tensor_tensor(g_t[:, 2, col], ps[:, t, 8:16], gdn_vec[:, 1, :], ALU.add))
            do(V.tensor_scalar(g_t[:, 3, :], g_t[:, 2, :], -1.0, None, ALU.mult))
            tell(V.tensor_tensor(g_t[:, 3, :], g_t[:, 3, :], g_t[:, 2, :], ALU.max), sem("gd_ba_read"))
            dve.wait_ge(sem("gd_act"), 1)
            do(V.scalar_tensor_tensor(out=g_t[:, 0, :], in0=g_t[:, 2, :], scalar=0.0, in1=g_t[:, 3, :], op0=ALU.max, op1=ALU.add))
            do(V.tensor_scalar(g_t[:, 0, :], g_t[:, 0, :], -1.0, None, ALU.mult))
            for t in range(2):
                col = slice(8 * t, 8 * t + 8)
                ins = V.tensor_tensor(g_t[:, 0, col], g_t[:, 0, col], gdn_vec[:, 2, :], ALU.mult)
                do(ins)
            tell(V.tensor_copy(note[:, :], eps_t[0:1, :]), sem("gd_decays"))
            n.tp += 12
            dve.wait_ge(tp_evacuated, n.tp)
            qn = [gtok[:, t, 0:8, :] for t in range(2)]
            kn = [gtok[:, t, 8:16, :] for t in range(2)]
            vn = [gtok[:, t, 16:24, :] for t in range(2)]

            def per_head(ap2):
                return ap2.rearrange("p (h o) -> p h o", o=1).broadcast_to([P, ap2.shape[1], P])

            for t in range(2):
                for i, xin in enumerate((qn[t], kn[t])):
                    do(V.tensor_tensor(g_sq, xin, xin, ALU.mult))
                    do(V.tensor_reduce(stat[:, i, :], g_sq, AX_X, ALU.add))
                tell(V.tensor_scalar(stat[:, 0:2, :], stat[:, 0:2, :], EPS, None, ALU.add), sem("gd_ms"))
                dve.wait_ge(sem("gd_rms"), t + 1)
                do(V.reciprocal(stat[:, 2:4, :], stat[:, 0:2, :]))
                do(V.tensor_scalar(stat[:, 2, :], stat[:, 2, :], float(P) ** -0.5, None, ALU.mult))
                do(V.tensor_tensor(qn[t], qn[t], per_head(stat[:, 2, :]), ALU.mult))
                do(V.tensor_tensor(kn[t], kn[t], per_head(stat[:, 3, :]), ALU.mult))
                do(V.tensor_tensor(vn[t], vn[t], per_head(g_t[:, 1, 8 * t:8 * t + 8]), ALU.mult))
                do(V.tensor_tensor(gkb[:, t], kn[t], per_head(g_t[:, 1, 8 * t:8 * t + 8]), ALU.mult))
            tell(V.tensor_copy(note[:, :], eps_t[0:1, :]), sem("gd_norm"))
            dve.wait_ge(sem("gd_sums"), 1)
            do(V.tensor_copy(g_t[:, 4, :], ps[:, 2, 0:16]))
            do(V.tensor_copy(g_t[:, 8, :], ps[:, 3, 0:16]))
            tell(V.tensor_tensor(g_t[:, 5, :], g_t[:, 8, :], g_t[:, 4, :], ALU.subtract), sem("gd_exparg"))
            dve.wait_ge(sem("gd_exp"), 1)
            n.tp += 12
            dve.wait_ge(tp_full, n.tp)
            do(V.tensor_tensor(g_kdec, kn[0], per_head(g_t[:, 7, 0:8]), ALU.mult))
            do(V.tensor_tensor(gkb[:, 1], gkb[:, 1], per_head(g_t[:, 6, 8:16]), ALU.mult))
            tell(V.tensor_tensor(qn[1], qn[1], per_head(g_t[:, 6, 8:16]), ALU.mult), sem("gd_qe"))
            n.tp += 2
            b4 = lambda bank: ps[:, bank, :].rearrange("p (a b) -> p a b", a=4)
            all4 = lambda m: m.rearrange("p (o b) -> p o b", o=1).broadcast_to([P, 4, P])
            for b in range(4):
                g, t = divmod(b, 2)
                hs = slice(8 * t + 4 * g, 8 * t + 4 * g + 4)
                if b >= 1:
                    dve.wait_ge(sem("gd_o"), b)
                tell(V.tensor_copy(TT, per_head(g_t[:, 0, hs])), sem("gd_gb"))
                dve.wait_ge(sem("gd_scores"), b + 1)
                do(V.tensor_tensor(LM, b4(0), per_head(g_t[:, 4, hs]), ALU.subtract))
                tell(V.tensor_scalar(LM, LM, 0.0, None, ALU.min), sem("gd_gap"))
                dve.wait_ge(sem("gd_dec"), b + 1)
                do(V.tensor_tensor(LT, b4(1), LM, ALU.mult))
                do(V.tensor_tensor(AT, b4(2), LM, ALU.mult))
                do(V.tensor_tensor(AT, AT, all4(s_le_t[:, :]), ALU.mult))
                do(V.tensor_copy(DD, all4(ident[:, :])))
                do(V.tensor_copy(DT_, all4(ident[:, :])))
                for lvl in range(LEVELS):
                    s0 = LEVELS * b + lvl
                    tell(V.tensor_tensor(LM, LT, all4(lv[:, lvl, :]), ALU.mult), sem("gd_lm"))
                    dve.wait_ge(sem("gd_step"), s0 + 1)
                    do(V.tensor_tensor(DD, DD, b4(4), ALU.subtract))
                    tell(V.tensor_tensor(DT_, DT_, b4(5), ALU.subtract), sem("gd_inverse"))
                dve.wait_ge(sem("gd_u"), b + 1)
                if t == 1:
                    do(V.tensor_copy(WT[:, 0:512], ps[:, 1, :]))
                tell(V.tensor_copy(U, b4(0)), sem("gd_u_read"))
                if t == 0:
                    dve.wait_ge(sem("gd_o"), b + 1)
                    do(V.tensor_copy(g_o0[:, 4 * g:4 * g + 4, :], b4(2)))
                    tell(V.tensor_copy(gS, b4(3)), sem("gd_batch"))
                else:
                    dve.wait_ge(sem("gd_ws"), b // 2 + 1)
                    tell(V.tensor_tensor(U, U, b4(2), ALU.subtract), sem("gd_vnew"))
                    dve.wait_ge(sem("gd_o"), b + 1)
                    tell(V.tensor_copy(g_o1[:, 4 * g:4 * g + 4, :], b4(3)), sem("gd_batch"))
            for t, ot in enumerate((g_o0, g_o1)):
                do(V.tensor_tensor(g_sq, ot, ot, ALU.mult))
                do(V.tensor_reduce(stat[:, 0, :], g_sq, AX_X, ALU.add))
                tell(V.tensor_scalar(stat[:, 0, :], stat[:, 0, :], 1.0 / P, EPS, ALU.mult, ALU.add), sem("gd_oms"))
                dve.wait_ge(sem("gd_orms"), t + 1)
                do(V.reciprocal(stat[:, 1, :], stat[:, 0, :]))
                do(V.tensor_tensor(ot, ot, per_head(stat[:, 1, :]), ALU.mult))
                do(V.tensor_tensor(ot, ot, g_norm.rearrange("p (o b) -> p o b", o=1).broadcast_to([P, 8, P]), ALU.mult))
                tell(V.tensor_tensor(g_o[:, t, :], ot.rearrange("p a b -> p (a b)"), g_z[:, t, :], ALU.mult), h_ready)
                n.h += 1
                n.tp += 2
            n.block += 2
            update_tiles(LAT)
            moe(1)


def kernel(**inputs):
    import numpy as _np
    import concourse.bacc as _bacc
    from concourse import mybir as _mybir
    from concourse.bass_utils import run_bass_kernel_spmd as _run

    nc = _bacc.Bacc("TRN2", target_bir_lowering=False, num_devices=1)
    arrays, args = {}, {}
    inputs = dict(inputs)
    lb = _np.asarray(inputs["hgrn_lb"])
    inputs["hgrn_lb"] = lb.reshape(2, 3, 4, P).transpose(3, 1, 0, 2)
    for name in ("ab_conv", "conv_w_2", "gdn_conv_w_2"):
        w = _np.asarray(inputs[name])[0]
        inputs[name] = w.reshape(w.shape[0], -1, P).transpose(2, 1, 0)
    for name, a in list(inputs.items()) + list(shape_constants().items()):
        a = _np.ascontiguousarray(a)
        arrays[f"in_{name}"] = a
        args[name] = nc.dram_tensor(f"in_{name}", a.shape, _mybir.dt.from_np(a.dtype), kind="ExternalInput").ap()
    out = nc.dram_tensor("out_0", (1, SEQ, D), F32, kind="ExternalOutput").ap()
    build(nc, args, out)
    r = _run(nc, [arrays], core_ids=[0])
    return r.results[0]["out_0"]
```

```python
from contextlib import ExitStack

import numpy as np
import concourse.bass as bass
from concourse import mybir

F32 = mybir.dt.float32
ALU = mybir.AluOpType
ACT = mybir.ActivationFunctionType
AX_X = mybir.AxisListType.X

P = 128
D = 1024
KC = D // P
SEQ = 256
NT = 2 * SEQ
D_FF = 2816
EH = 256
NFF = D_FF // EH
SLOTS = 6
UNIT = 2048
HGRN_HEADS = MLSTM_HEADS = 4
SCAN_CHUNK = 32
NSC = NT // SCAN_CHUNK
ATT_HEADS, KV_HEADS = 8, 2
GDN_HEADS = 8
N_GROUPS, PER_GROUP = 8, 8
N_EXPERTS = N_GROUPS * PER_GROUP
EPS = 1e-6
BIG = 1e30
MAXF = 3.0e38
ROWS = 36
GATE_W = 16
ROUTE_W = N_GROUPS + N_EXPERTS + 1
QUAD = 4
CAP = 32
QUADS = N_EXPERTS // QUAD
LEVELS = 7


def shape_constants():
    i = np.arange(P)
    f = np.float32
    c = {}
    c["ident"] = np.eye(P, dtype=f)
    c["s_le_t"] = (i[:, None] <= i[None, :]).astype(f)
    c["s_ge_t"] = (i[:, None] >= i[None, :]).astype(f)
    same = i[:, None] // SCAN_CHUNK == i[None, :] // SCAN_CHUNK
    c["chunk_masks"] = np.stack([c["s_le_t"] * same, c["s_ge_t"] * same], 1).astype(f)
    seg = np.ones((P, NT), f)
    seg[:, ::SCAN_CHUNK] = 0
    c["chunk_starts"] = seg
    sel = np.zeros((ROWS, 8, P), f)
    for d in range(2):
        for h in range(4):
            sel[32 * d + h, 4 * d + h] = 1
    c["row_select"] = sel
    lv = np.zeros((P, LEVELS, P), f)
    for n in range(LEVELS):
        b = 1 << n
        pair = i[:, None] // (2 * b) == i[None, :] // (2 * b)
        lv[:, n] = pair & (i[:, None] % (2 * b) < b) & (i[None, :] % (2 * b) >= b)
    c["levels"] = lv
    c["slot_index"] = np.broadcast_to(np.arange(CAP, dtype=f), (P, CAP)).copy()
    c["round_limits"] = np.broadcast_to(CAP * np.arange(1, SEQ // CAP, dtype=f), (P, SEQ // CAP - 1)).copy()
    t = np.arange(SEQ)
    inv = np.power(f(10000.0), -np.arange(0, 64, 2, dtype=f) / f(64)).astype(f)
    ang = np.stack([(t // 64).astype(f)[:, None] * inv, (t % 64).astype(f)[:, None] * inv], 1)
    rope = np.stack([np.cos(ang), np.sin(ang)], 1).astype(f).reshape(2, P, 2, 64)
    c["rope"] = np.ascontiguousarray(rope.transpose(1, 0, 2, 3))
    return c


class Counts:

    def __init__(self):
        self.block = 0
        self.gu = 0
        self.tp = 0
        self.h = 0
        self.normed = 0
        self.x = 0
        self.pos = 0

    def slots(self, n):
        at = [(self.pos + i) % SLOTS for i in range(n)]
        self.pos += n
        return at

    def align(self):
        self.pos = -(-self.pos // SLOTS) * SLOTS


def build(nc, I, out):
    ctx = ExitStack()
    with ctx:
        def sb(name, shape):
            return ctx.enter_context(nc.sbuf_tensor(name, shape, F32))

        made = {}

        def sem(name):
            if name not in made:
                made[name] = ctx.enter_context(nc.semaphore(name))
            return made[name]

        ps = ctx.enter_context(nc.psum_tensor("ps", [P, 8, 512], F32))
        y_bank = ps[:, 0:4, :]

        ring = sb("ring", [P, SLOTS, UNIT])
        x_sb = sb("x_sb", [P, 4, D])
        hT = sb("hT", [P, KC, NT])
        h = sb("h", [P, 2, D])
        v_scale = sb("v_scale", [P, D])
        v_shift = sb("v_shift", [P, D])
        v_gate = sb("v_gate", [P, D])
        v_tmp = sb("v_tmp", [P, D])
        junk = sb("junk", [P, D])
        ident = sb("ident", [P, P])
        s_le_t = sb("s_le_t", [P, P])
        s_ge_t = sb("s_ge_t", [P, P])
        ones_t = sb("ones_t", [P, P])
        rounds_i = ctx.enter_context(nc.sbuf_tensor("rounds_i", [P, 1], mybir.dt.int32))
        eps_t = sb("eps_t", [P, 1])
        zero_t = sb("zero_t", [P, 512])
        note = sb("note", [1, 1])
        rs = sb("rs", [P, 2])
        ys = sb("ys", [P, 3])
        stat = sb("stat", [P, 6, 8])
        cond = sb("cond", [P, 3, KC])
        cond_sig = sb("cond_sig", [P, 3, KC])
        w_gdn_ba = sb("w_gdn_ba", [P, KC, 16])
        gdn_vec = sb("gdn_vec", [P, 3, 8])
        ARENA = 23330
        arena = sb("arena", [P, ARENA])

        class Area:
            def __init__(self, at=0):
                self.at = at

            def __call__(self, *shape, parts=P):
                n = int(np.prod(shape))
                v = arena[0:parts, self.at:self.at + n]
                self.at += n
                assert self.at <= ARENA, self.at
                if len(shape) == 2:
                    v = v.rearrange("p (a b) -> p a b", a=shape[0])
                if len(shape) == 3:
                    v = v.rearrange("p (a b c) -> p a b c", a=shape[0], b=shape[1])
                if len(shape) == 4:
                    v = v.rearrange("p (a b c d) -> p a b c d", a=shape[0], b=shape[1], c=shape[2])
                return v

        A = Area()
        mod_rows = A(3 * D, parts=2)
        A = Area()
        v_tok = A(4, 4, 129)
        gate = A(4, D)
        o = A(4, D)
        hg_q = A(2, NT)
        hg_z = A(2, 2, NT)
        state = A(NSC, P)
        lbs = A(8, 2, 4)
        dec = A(2, NSC)
        w_gates = A(KC, 2, ROWS)
        gate_bias = A(2)
        w_conv = A(4, 3)
        tmp_at = A.at
        T1, T2, E1, E2, E3, E4 = (A(2, NT) for _ in range(6))
        chunk_masks = A(2, P)
        chunk_starts = A(NT)
        A = Area(tmp_at)
        g_sig = T1[:, 0, :]
        qk = A(4, NT)
        rows_a, rows_b, rows_c, rows_d, rows_e, rows_f = (A(NT, parts=ROWS) for _ in range(6))
        wexp = A(2, NT)
        g_sig2 = wexp[:, 0, :]
        in_state = state.rearrange("p a b -> p (a b)")
        row_select = in_state[0:ROWS, 0:8 * P].rearrange("p (a b) -> p a b", a=8)
        colsT = in_state[:, 8 * P:8 * P + 8 * ROWS].rearrange("p (a b c) -> p a b c", a=2, b=4)
        out_g = wexp.rearrange("p a b -> p (a b)")
        p_sb = hg_z.rearrange("p a b c -> p (a b) c")
        mden = A(3, 4)
        msum = A(2, 8)
        A = Area()
        sig = A(2, EH)
        swish = A(2, EH)
        hid = A(2, 2, EH)
        hidT = A(2, 2, 2 * P)
        moe_gates = A(2, N_EXPERTS + 2)
        gate_now = A(2, 2)
        w_route = A(KC, ROUTE_W)
        w_sg = A(KC)
        route_b = A(N_GROUPS + N_EXPERTS)
        rt = A(8, N_EXPERTS)
        rt1 = A(16)
        ring_more = A(SLOTS, UNIT)
        picked = A(2, N_EXPERTS)
        rank = A(2, N_EXPERTS)
        r_gate, r_rank, r_rank_x = A(2, QUAD), A(2, QUAD), A(2, QUAD)
        sel = A(2, QUAD * CAP)
        sel_gated = A(2, QUAD * CAP)
        sel_T = A(SEQ)
        x_slots = A(KC, P)
        q_sig, q_swish, q_hid = A(EH), A(EH), A(EH)
        q_hidT = A(2, P)
        z_slots = A(D)
        slot_index = A(CAP)
        round_limits = A(SEQ // CAP - 1)
        over = A(SEQ // CAP + 1)
        A = Area()
        aq = A(2, 8, P)
        ak = A(4, 2, P)
        av = A(4, 2, P)
        aqr = A(2, 8, P)
        akr = A(4, 2, P)
        qT = A(8, SEQ)
        kT = A(2, NT)
        prob = A(2, NT)
        probT = A(2, 4, P)
        rope = A(2, 2, 64)
        qk_g = A(2, P)
        asq = A(8, P)
        astat = A(2, 8)
        smax = A(2, 4)
        A = Area()
        cv_b = A(2, SEQ)
        cv_g = A(2, SEQ)
        cv_y = A(2, SEQ)
        w_sconv = A(KC, 3)
        A = Area()
        gT = A(24, SEQ)
        g_kT, g_kbT, g_qT = (gT[:, 8 * n:8 * n + 8, :] for n in range(3))
        gtok = A(2, 24, P)
        gkb = A(2, 8, P)
        gqe_T = A(8, P)
        g_z = A(2, D)
        g_o = gkb.rearrange("p a b c -> p a (b c)")
        g_kdec = A(8, P)
        w_gconv = A(24, 4)
        g_ba = A(2, 16)
        g_t = A(10, 16)
        g_norm = A(P)
        g_sq = A(8, P)
        lv = A(LEVELS, P)
        gS = A(4, P)
        LT, AT, U = [], [], []
        quarter = lambda v: v.rearrange("p (a b) -> p a b", a=4)
        sq2 = g_sq.rearrange("p a b -> p (a b)")
        LT = [A(4, P), quarter(sq2[:, 0:512])]
        AT = [A(4, P), quarter(sq2[:, 512:1024])]
        U = A(4, P)
        g_o0, g_o1 = gkb[:, 0], gkb[:, 1]
        DD = [quarter(h[:, 0, 0:512]), quarter(junk[:, 0:512])]
        DT_ = [quarter(h[:, 0, 512:1024]), quarter(junk[:, 512:1024])]
        TT = [quarter(h[:, 1, 0:512]), quarter(v_tmp[:, 512:1024])]
        LM = [quarter(h[:, 1, 512:1024]), A(4, P)]
        WT = v_tmp

        mod_dram = nc.dram_tensor("mod_dram", [6, 6 * D], F32).ap()

        slot_filled = [sem(f"slot_filled_{s}") for s in range(2 * SLOTS)]
        block_done, gu_evacuated = sem("block_done"), sem("gu_evacuated")
        tp_full, tp_evacuated = sem("tp_full"), sem("tp_evacuated")
        h_ready, x_updated = sem("h_ready"), sem("x_updated")
        constants_loaded, x_loaded = sem("constants_loaded"), sem("x_loaded")

        class Teller:

            def __init__(self, engine):
                self.engine, self.told = engine, {}

            def __call__(self, ins, s):
                self.told[s.name] = self.told.get(s.name, 0) + 1
                ins.then_inc(s, 1)
                self.engine.wait_ge(s, self.told[s.name])

        def slot(s):
            return ring[:, s, :] if s < SLOTS else ring_more[:, s - SLOTS, :]

        def slot_pair(s):
            return ring[:, s:s + 2, :] if s < SLOTS else ring_more[:, s - SLOTS:s - SLOTS + 2, :]

        GATE_UP_SLOT = [6, 8, 10, 0]
        DOWN_SLOT = [2, 3, 4, 5]

        ROW = {"l0": 0, "l0c": 1, "l1": 2, "l1c": 3, "b0": 4, "b1": 5}
        PRE = [("l0c", 0, I["norm_g"][0, 0]), ("l0", 0, I["norm_g"][0, 0]),
               ("l0c", 1, I["norm_g"][0, 2]), ("l0", 1, I["norm_g"][0, 2]),
               ("l1c", 0, I["norm_g"][1, 0]), ("l1", 0, I["norm_g"][1, 0]), ("l1", 1, I["norm_g"][1, 2]),
               ("b0", 0, I["norm_w_2"][0, 0]), ("b0", 1, I["norm_w_2"][0, 2]),
               ("b1", 0, I["norm_w_2"][1, 0]), ("b1", 1, I["norm_w_2"][1, 2])]
        POST = [("l0c", 0, I["norm_g"][0, 1]), ("l0", 0, I["norm_g"][0, 1]),
                ("l0c", 1, I["norm_g"][0, 3]), ("l0", 1, I["norm_g"][0, 3]),
                ("l1", 0, I["norm_g"][1, 1]), ("l1", 1, I["norm_g"][1, 3]),
                ("b0", 0, I["norm_w_2"][0, 1]), ("b0", 1, I["norm_w_2"][0, 3]),
                ("b1", 0, I["norm_w_2"][1, 1]), ("b1", 1, I["norm_w_2"][1, 3])]
        CTX, LAT = (0, 1), (2, 3)
        ADA = [("ada_w", 0, (0, 1)), ("ada_w", 1, (2, 3)), ("ada_w_2", 0, (4,)), ("ada_w_2", 1, (5,))]
        PAIR = SLOTS * EH
        PAIRS_PER_LAYER = 6 * D // PAIR
        ADA_A = (2, 1) * 4
        ADA_B = (1,) * 8
        PROJECTION_GROUPS = (1, 2)
        ADA_BEFORE_B = 2 + sum(PROJECTION_GROUPS) + sum(ADA_A)
        ADA_PROJECTIONS = 2 + sum(PROJECTION_GROUPS) + 3
        N_ADA = sum(ADA_A) + sum(ADA_B) + ADA_PROJECTIONS
        N_PAIRS = N_ADA // 2
        FIRST_PAIRS = PAIRS_PER_LAYER // 2
        assert N_PAIRS == PAIRS_PER_LAYER * len(ADA) - FIRST_PAIRS
        ADA_STORED = [16 + 48 * (N_PAIRS // 2), 48 * (N_PAIRS // 2)]
        group_rows = junk.rearrange("p (b c) -> p b c", b=2)
        PROJECTION_BANK = 3

        def step_bank(mixer, i):
            return {"A": 7, "B": 5}[mixer] - i % 2

        def ada_pair_of(p):
            l, i = divmod(FIRST_PAIRS + p, PAIRS_PER_LAYER)
            name, j, rows = ADA[l]
            return name, j, (0 if len(rows) == 2 else 2), len(rows), rows[0], PAIR * i

        def row_all(ap1d):
            return ap1d.rearrange("(o n) -> o n", o=1).broadcast_to([P, ap1d.shape[0]])

        block = ctx.enter_context(nc.Block())

        @block.sync
        def _(sp):
            n = Counts()
            free_at = [0] * SLOTS
            ada_free = [0] * SLOTS
            ada_next = [0]

            def sp_loop(count):
                if count > 0:
                    with sp.Fori(0, count) as r:
                        yield r

            def kmajor(w):
                return w.rearrange("(p k) n -> p k n", k=KC)

            def pmajor(w):
                return w.rearrange("(k p) n -> p k n", p=P)

            def fill(s, src, free=None):
                free = free_at[s] if free is None else free
                if ada_free[s] > 0:
                    sp.wait_ge(sem("ada_group_done"), ada_free[s])
                    ada_free[s] = 0
                elif not isinstance(free, int) or free > 0:
                    sp.wait_ge(block_done, free)
                dst = slot(s)
                if len(src.shape) == 3:
                    dst = dst.rearrange("p (k n) -> p k n", k=src.shape[1])
                sp.dma_start(dst, src).then_inc(slot_filled[s], 16)

            def stream(units, blocks):
                n.block += blocks
                for src in units:
                    (s,) = n.slots(1)
                    fill(s, src)
                    free_at[s] = n.block

            def columns(w, unit, order):
                return order(w[:, unit * EH:(unit + 1) * EH])

            def conditioning():
                name, j, _ = ADA[0]
                w = I[name][j]
                for s in range(SLOTS):
                    fill(s, columns(w, s, kmajor))
                for s in range(SLOTS):
                    fill(s, columns(w, SLOTS + s, kmajor), free=s // 2 + 1)
                n.block = 6
                for s in range(SLOTS):
                    free_at[s] = 3 + s // 2 + 1

            def ada_groups(count):
                for _ in range(count):
                    name, j, _, _, _, col = ada_pair_of(ada_next[0] // 2)
                    col += EH * (ada_next[0] % 2)
                    ada_next[0] += 1
                    for u, s in enumerate(n.slots(3)):
                        fill(s, kmajor(I[name][j][:, col + 512 * u:col + 512 * u + EH]))
                        ada_free[s] = ada_next[0]

            def slice_units(wg, wu, wd):
                return kmajor(wg), kmajor(wu), wd.rearrange("(p j) n -> p (j n)", j=2)

            def mlp(count, units_of, tail=()):
                n.align()
                b0 = n.block
                for i in range(2):
                    for s, src in zip(range(3 * i, 3 * i + 3), units_of(i)):
                        fill(s, src)
                pairs = (count - 2) // 2
                for r in sp_loop(pairs):
                    for j in range(2):
                        g, u, d = units_of(r * 2 + (2 + j))
                        fill(3 * j, g, free=r * 6 + (b0 + 3 * j + 2))
                        fill(3 * j + 1, u, free=r * 6 + (b0 + 3 * j + 2))
                        fill(3 * j + 2, d, free=r * 6 + (b0 + 3 * j + 5))
                rest = [units_of(i) for i in range(2 + 2 * pairs, count)] + list(tail)
                total = count + len(tail)
                for k, (g, u, d) in enumerate(rest):
                    i = 2 + 2 * pairs + k
                    j = i % 2
                    fill(3 * j, g, free=b0 + 3 * (i - 2) + 2)
                    fill(3 * j + 1, u, free=b0 + 3 * (i - 2) + 2)
                    fill(3 * j + 2, d, free=b0 + 3 * (i - 2) + 5)
                n.block += 3 * total
                n.pos = 3 * total
                for s in range(SLOTS):
                    free_at[s] = n.block

            def ffn(l):
                wi, wo = I["ffn_w_in"][l], I["ffn_w_out"][l]
                mlp(NFF, lambda i: slice_units(wi[:, bass.ds(i * EH, EH)], wi[:, bass.ds(i * EH + D_FF, EH)],
                                               wo[bass.ds(i * EH, EH), :]))

            def experts(l):
                n.block += 2
                shared = [slice_units(I["shared_w_gate_2"][l][:, j * EH:(j + 1) * EH],
                                      I["shared_w_up_2"][l][:, j * EH:(j + 1) * EH],
                                      I["shared_w_down_2"][l][j * EH:(j + 1) * EH, :]) for j in range(2)]
                mlp(2, lambda i: shared[i])
                used_gu, used_down = sem("quad_gate_up_used"), sem("quad_down_used")

                def quad(of, q, first):
                    for a in range(QUAD):
                        for s, name in ((GATE_UP_SLOT[a], "moe_w_gate_2"), (GATE_UP_SLOT[a] + 1, "moe_w_up_2")):
                            if first and s < SLOTS:
                                sp.wait_ge(block_done, free_at[s])
                            elif first:
                                sp.wait_ge(x_updated, n.x)
                            else:
                                sp.wait_ge(used_gu, q + QUADS * l)
                            sp.dma_start(slot(s).rearrange("p (k n) -> p k n", k=KC),
                                         of(name, a).rearrange("(p k) n -> p k n", k=KC)).then_inc(slot_filled[s], 16)
                    for a, s in enumerate(DOWN_SLOT):
                        if first:
                            sp.wait_ge(block_done, free_at[s])
                        else:
                            sp.wait_ge(used_down, q + QUADS * l)
                        sp.dma_start(slot(s), of("moe_w_down_2", a).rearrange("(p j) n -> p (j n)", j=2)) \
                            .then_inc(slot_filled[s], 16)

                quad(lambda name, a: I[name][l, a], 0, True)
                with sp.Fori(1, QUADS) as q:
                    quad(lambda name, a: I[name][l, bass.ds(q * QUAD + a, 1)].rearrange("o a b -> (o a) b"), q, False)
                n.block += 1
                n.pos = 0
                sp.wait_ge(used_gu, QUADS * (l + 1))
                for s in range(SLOTS):
                    free_at[s] = n.block if s in DOWN_SLOT else 0

            conditioning()
            w = I["ab_w_in"][0]
            for at in (512, 1024):
                stream([kmajor(w[:, at + EH * j:at + EH * (j + 1)]) for j in range(2)], 4)
                ada_groups(1)
            for hp in range(2):
                for at in (0, 1536, 2048):
                    stream([kmajor(w[:, at + EH * hp:at + EH * (hp + 1)])], 2)
                ada_groups(PROJECTION_GROUPS[hp])
                ada_groups(sum(ADA_A[4 * hp:4 * hp + 4]))
            for at in (3072, 3584):
                stream([kmajor(w[:, at + EH * j:at + EH * (j + 1)]) for j in range(2)], 4)
                ada_groups(1)
            for j in range(2):
                stream([kmajor(w[:, 2560 + EH * j:2560 + EH * (j + 1)])], 2)
            ada_groups(1 + sum(ADA_B))
            stream([columns(I["ab_w_out"][0], j, pmajor) for j in range(4)], 4)
            ffn(0)
            ffn(0)
            w = I["attn_w_qkv"][0]
            for j in range(2):
                stream([columns(w, 2 * j, kmajor), columns(w, 2 * j + 1, kmajor)], 2)
            stream([columns(w, 4, kmajor), columns(w, 5, kmajor)], 4)
            stream([columns(I["attn_w_out"][0], j, pmajor) for j in range(4)], 2)
            ffn(1)
            w = I["conv_in_w_2"][0]
            for c in range(4):
                for part in range(3):
                    stream([columns(w, 4 * part + c, kmajor)], 2)
            stream([columns(I["conv_out_w_2"][0], j, pmajor) for j in range(4)], 2)
            n.x = 14
            experts(0)
            w = I["gdn_in_w_2"][0]
            for j in range(12):
                stream([columns(w, j, kmajor)], 2)
            for j in range(6, 8):
                stream([columns(w, 2 * j, kmajor), columns(w, 2 * j + 1, kmajor)], 2)
            stream([columns(I["gdn_out_w_2"][0], j, pmajor) for j in range(4)], 2)
            n.x = 18
            experts(1)
            n.x = 20
            for t in range(2):
                sp.wait_ge(x_updated, n.x - 1 + t)
                sp.dma_start(out[0, t * P:(t + 1) * P, :], x_sb[:, 2 + t, :]).then_inc(sem("result_stored"), 16)
            sp.wait_ge(sem("result_stored"), 32)

        @block.gpsimd
        def _(pool):
            n = Counts()
            tell = Teller(pool)
            loads = {}
            vec_step = sem("vec_step")
            made_pre, made_post = [0], [0]
            seen = {"h": [], "x": []}

            def load(dst, src, s):
                loads[s.name] = loads.get(s.name, 0) + 16
                pool.dma_start(dst, src).then_inc(s, 16)

            def arrived(s):
                pool.wait_ge(s, loads[s.name])

            def pre():
                which, half, g = PRE[made_pre[0]]
                if made_pre[0] > 0:
                    pool.wait_ge(h_ready, n.h)
                made_pre[0] += 1
                row = mod_dram[ROW[which]]
                load(v_scale[:, :], row_all(row[(3 * half + 1) * D:(3 * half + 2) * D]), sem("vectors_loaded"))
                load(v_shift[:, :], row_all(row[3 * half * D:(3 * half + 1) * D]), sem("vectors_loaded"))
                load(v_tmp[:, :], row_all(g), sem("vectors_loaded"))
                arrived(sem("vectors_loaded"))
                tell(nc.gpsimd.tensor_scalar(v_scale[:, :], v_scale[:, :], 1.0, None, ALU.add), vec_step)
                tell(nc.gpsimd.tensor_tensor(v_scale[:, :], v_scale[:, :], v_tmp[:, :], ALU.mult), sem("pre_ready"))

            def post():
                which, half, g = POST[made_post[0]]
                if made_post[0] > 0:
                    pool.wait_ge(x_updated, n.x)
                made_post[0] += 1
                row = mod_dram[ROW[which]]
                load(v_gate[:, :], row_all(row[(3 * half + 2) * D:(3 * half + 3) * D]), sem("vectors_loaded"))
                load(v_tmp[:, :], row_all(g), sem("vectors_loaded"))
                arrived(sem("vectors_loaded"))
                tell(nc.gpsimd.tensor_tensor(v_gate[:, :], v_gate[:, :], v_tmp[:, :], ALU.mult), sem("post_ready"))

            for i, c in enumerate((I["c"][0], I["c_ctx"], I["c_2"][0])):
                load(cond[:, i, :], c.rearrange("(p k) -> p k", k=KC), sem("cond_loaded"))
            for dst, src in ((ident, "ident"), (s_le_t, "s_le_t"), (s_ge_t, "s_ge_t")):
                load(dst[:, :], I[src], constants_loaded)
            for i, src in enumerate((I["ctx"][0], I["x"][0])):
                load(x_sb[:, 2 * i:2 * i + 2, :], src.rearrange("(t p) d -> p t d", p=P), x_loaded)
            b = I["ada_b"][0]
            for q in range(2):
                load(mod_rows[q:q + 1, :], b[0:3 * D].rearrange("(o n) -> o n", o=1), sem("ada_bias_loaded_0"))

            def pair_bias(g):
                name, j, _, m_, _, col = ada_pair_of(g)
                b = I[name.replace("_w", "_b")][j]
                for u in range(3):
                    src = b[col + 512 * u:col + 512 * (u + 1)].rearrange("(o n) -> o n", o=1)
                    load(group_rows[32 * u:32 * u + m_, g % 2, :], src.broadcast_to([m_, 512]), sem(f"ada_bias_loaded_{g % 2}"))

            def pair_store(g):
                _, _, _, m_, row, col = ada_pair_of(g)
                pool.wait_ge(sem("ada_rows_ready"), 2 * (g + 1))
                for u in range(3):
                    pool.dma_start(mod_dram[row:row + m_, col + 512 * u:col + 512 * (u + 1)],
                                   group_rows[32 * u:32 * u + m_, g % 2, :]).then_inc(sem(f"mod_stored_{g % 2}"), 16)
                pool.wait_ge(sem(f"mod_stored_{g % 2}"), (16 if g % 2 == 0 else 0) + 48 * (g // 2 + 1))
                if g + 2 < N_PAIRS:
                    pair_bias(g + 2)

            pool.wait_ge(sem("mod_row_ready"), 1)
            pool.dma_start(mod_dram[0:2, 0:3 * D], mod_rows[:, :]).then_inc(sem("mod_stored_0"), 16)
            pool.wait_ge(sem("mod_stored_0"), 16)
            pre()
            n.h += 2
            pre()
            n.h += 2
            pair_bias(0)
            pair_bias(1)

            tell(nc.gpsimd.memset(w_gates, 0.0), vec_step)
            tell(nc.gpsimd.memset(gate_bias, 0.0), vec_step)
            s = sem("ab_constants")
            load(chunk_masks, I["chunk_masks"], s)
            load(chunk_starts, I["chunk_starts"], s)
            for d in range(2):
                for part in range(2):
                    at = 4 * (2 * d + part)
                    load(w_gates[:, :, part, 32 * d:32 * d + 4],
                         I["ab_w_in"][0][:, 4096 + at:4100 + at].rearrange("(p k) n -> p k n", k=KC), s)
                    load(gate_bias[32 * d:32 * d + 4, part:part + 1],
                         I["ab_gate_b"][0, 2 * d + part].rearrange("(n o) -> n o", o=1), s)
            load(lbs[:, 0:3], I["hgrn_lb"], s)
            load(w_conv, I["ab_conv"], s)
            post()
            pairs_a = ADA_BEFORE_B // 2
            for g in range(pairs_a):
                pair_store(g)
            pool.wait_ge(sem("hgrn_done"), 1)
            load(row_select, I["row_select"], sem("row_select_loaded"))
            pair_store(pairs_a)
            pool.wait_ge(sem("ml_qk"), 4)
            load(out_g, row_all(I["ab_out_g"][0]), sem("out_g_loaded"))
            for g in range(pairs_a + 1, N_PAIRS):
                pair_store(g)
            n.h += 4
            pre()
            n.x += 2
            post()
            n.x += 2
            n.h += 2
            post()
            n.x += 2
            pre()
            n.h += 2
            post()
            n.x += 2
            pre()
            n.h += 2
            pre()
            load(rope, I["rope"], sem("att_constants"))
            for i in range(2):
                load(qk_g[:, i, :], row_all(I["attn_qk_g"][0, i]), sem("att_constants"))
            n.h += 2
            post()
            n.x += 2
            pre()
            n.h += 2
            post()
            n.x += 2
            def router_weights(l):
                s = sem("route_w_loaded")
                load(w_route[:, :, 0:N_GROUPS], I["moe_group_w_2"][l].rearrange("(p k) n -> p k n", k=KC), s)
                load(w_route[:, :, N_GROUPS:ROUTE_W - 1], I["moe_expert_w_2"][l].rearrange("(p k) n -> p k n", k=KC), s)
                load(w_sg, I["shared_gate_w_2"][l].rearrange("(p k) n -> p (k n)", k=KC), s)
                load(route_b[:, 0:N_GROUPS], row_all(I["moe_group_b_2"][l]), s)
                load(route_b[:, N_GROUPS:], row_all(I["moe_expert_b_2"][l]), s)
                arrived(s)
                tell(nc.gpsimd.tensor_copy(w_route[:, :, ROUTE_W - 1], w_sg), sem("route_w_ready"))

            def slot_constants():
                pool.wait_ge(x_updated, n.x)
                load(slot_index, I["slot_index"], sem("slot_constants_loaded"))
                load(round_limits, I["round_limits"], sem("slot_constants_loaded"))

            pre()
            pool.wait_ge(x_updated, n.x)
            load(w_sconv, I["conv_w_2"], sem("sconv_w_loaded"))
            n.h += 2
            post()
            router_weights(0)
            n.x += 2

            pre()
            slot_constants()
            n.h += 2
            post()
            n.x += 2
            pre()
            pool.wait_ge(x_updated, n.x)
            s = sem("gdn_constants")
            load(w_gconv, I["gdn_conv_w_2"], s)
            load(w_gdn_ba[:, :, :], I["gdn_in_w_2"][0][:, 4096:4112].rearrange("(p k) n -> p k n", k=KC), s)
            load(gdn_vec[:, 0, :], row_all(I["gdn_a_log_2"][0]), s)
            load(gdn_vec[:, 1, :], row_all(I["gdn_dt_bias_2"][0]), s)
            load(g_norm, row_all(I["gdn_norm_w_2"][0]), s)
            load(lv, I["levels"], s)
            n.h += 2
            n.h += 2
            pool.wait_ge(sem("gd_scores"), 4)
            router_weights(1)
            pool.wait_ge(h_ready, n.h)
            post()
            n.x += 2
            pre()
            slot_constants()
            n.h += 2
            post()

        @block.tensor
        def _(pe):
            n = Counts()
            used = [0] * SLOTS

            def filled(s):
                used[s] += 1
                pe.wait_ge(slot_filled[s], 16 * used[s])

            def gu_bank():
                i = n.gu
                if i >= 2:
                    pe.wait_ge(gu_evacuated, i - 1)
                n.gu += 1
                n.block += 1
                return ps[:, 4 + i % 2, :]

            def products(outs, lhsT_of, slots, start=True, stop=True):
                a, b = slots
                if b == a + 1:
                    o3 = outs.rearrange("p (u c) -> p u c", u=2)
                    for k in range(KC):
                        m = pe.matmul(o3, lhsT_of(k), ring[:, a:a + 2, k * EH:(k + 1) * EH],
                                      start=start and k == 0, stop=stop and k == KC - 1)
                else:
                    for u, s in enumerate(slots):
                        for k in range(KC):
                            m = pe.matmul(outs[:, u * EH:(u + 1) * EH], lhsT_of(k), ring[:, s, k * EH:(k + 1) * EH],
                                          start=start and k == 0, stop=stop and k == KC - 1)
                return m

            def token_major(tiles):
                slots = n.slots(2)
                for s in slots:
                    filled(s)
                for t in tiles:
                    outs = gu_bank()
                    products(outs, lambda k: hT[:, k, t * P:(t + 1) * P], slots).then_inc(block_done, 1)

            def feature_major(c0, c1):
                (s,) = n.slots(1)
                filled(s)
                for c in range(2):
                    outs = gu_bank()
                    for k in range(KC):
                        m = pe.matmul(outs[:, 0:c1 - c0], ring[:, s, k * EH + c * P:k * EH + (c + 1) * P],
                                      hT[:, k, c0:c1], start=k == 0, stop=k == KC - 1)
                    m.then_inc(block_done, 1)

            def transposes(srcs, parts=P):
                i = n.tp
                if i >= 2:
                    pe.wait_ge(tp_evacuated, i - 1)
                w = srcs[0].shape[-1]
                for j, src in enumerate(srcs):
                    m = pe.transpose(ps[0:w, 6 + i % 2, j * P:j * P + src.shape[0]], src,
                                     ident[0:src.shape[0], 0:src.shape[0]])
                m.then_inc(tp_full, 1)
                n.tp += 1

            def norm_tiles(tiles):
                for _ in tiles:
                    b = n.h % 2
                    n.h += 1
                    pe.wait_ge(h_ready, n.h)
                    for half in range(2):
                        transposes([h[:, b, 4 * half + kk::KC] for kk in range(4)])

            def mixer_out(tiles, col0):
                slots = n.slots(4)
                for s in slots:
                    filled(s)
                pe.wait_ge(tp_evacuated, n.tp)
                for i, t in enumerate(tiles):
                    pe.wait_ge(x_updated, n.x) if (n.x > 0) else None
                    for half in range(2):
                        m = products(ps[:, 2 * (i % 2) + half, :], lambda k: hT[:, k, t * P - col0:(t + 1) * P - col0],
                                     slots[2 * half:2 * half + 2])
                    m.then_inc(block_done, 1)
                    n.block += 1
                    if i % 2 == 1:
                        n.x += 2

            def pe_loop(count):
                if count > 0:
                    with pe.Fori(0, count) as r:
                        yield r

            def mlp(total, col0, last=True):
                n.align()
                gu0, tp0, filled0 = n.gu, n.tp, list(used)
                assert gu0 % 2 == 0

                def gate_up(i_par, t, gu_wait, fill_wait):
                    if t == 0:
                        for s in (3 * i_par, 3 * i_par + 1):
                            pe.wait_ge(slot_filled[s], fill_wait(s))
                    pe.wait_ge(gu_evacuated, gu_wait)
                    products(ps[:, 4 + t, :], lambda k: hT[:, k, col0 + t * P:col0 + (t + 1) * P],
                             (3 * i_par, 3 * i_par + 1)).then_inc(block_done, 1)

                def turn(i_par, gu_wait, tp_wait):
                    pe.wait_ge(gu_evacuated, gu_wait)
                    pe.wait_ge(tp_evacuated, tp_wait)
                    for j in range(2):
                        for t in range(2):
                            m = pe.transpose(ps[:, 6 + (tp0 + i_par) % 2, j * EH + t * P:j * EH + (t + 1) * P],
                                             hid[:, i_par, t, j::2], ident[:, :])
                    m.then_inc(tp_full, 1)

                def down(i_par, tp_wait, fill_wait):
                    s = 3 * i_par + 2
                    pe.wait_ge(slot_filled[s], fill_wait(s))
                    pe.wait_ge(tp_evacuated, tp_wait)
                    for t in range(2):
                        for half in range(2):
                            for j in range(2):
                                m = pe.matmul(ps[:, 2 * t + half, :], hidT[:, i_par, j, t * P:(t + 1) * P],
                                              ring[:, s, j * D + half * 512:j * D + (half + 1) * 512],
                                              start=False, stop=False, skip_group_check=True)
                    m.then_inc(block_done, 1)

                pe.wait_ge(sem("zero_ready"), 1)
                if n.x > 0:
                    pe.wait_ge(x_updated, n.x)
                for b in range(4):
                    pe.matmul(ps[:, b, :], zero_t[:, 0:P], zero_t[:, :], start=True, stop=False, skip_group_check=True)
                for t in range(2):
                    gate_up(0, t, gu0 - 1 + t, lambda s: 16 * (filled0[s] + 1))
                pairs = (total - 1) // 2
                for r in pe_loop(pairs):
                    for j in range(2):
                        q = 1 - j
                        fw = (lambda s: r * 16 + 16 * (filled0[s] + 1)) if j == 0 else \
                            (lambda s: r * 16 + 16 * (filled0[s] + 2))
                        gate_up(q, 0, r * 4 + (gu0 + 2 * (j + 1) - 1), fw)
                        turn(j, r * 4 + (gu0 + 2 * j + 2), r * 2 + max(tp0 + j - 1, 0))
                        gate_up(q, 1, r * 4 + (gu0 + 2 * (j + 1)), fw)
                        down(j, r * 2 + (tp0 + j + 1), lambda s: r * 16 + 16 * (filled0[s] + 1))
                for i in range(2 * pairs, total):
                    j = i % 2
                    if i + 1 < total:
                        gate_up(1 - j, 0, gu0 + 2 * (i + 1) - 1, lambda s: 16 * (filled0[s] + (i + 1) // 2 + 1))
                    turn(j, gu0 + 2 * i + 2, tp0 + i - 1)
                    if i + 1 < total:
                        gate_up(1 - j, 1, gu0 + 2 * (i + 1), lambda s: 16 * (filled0[s] + (i + 1) // 2 + 1))
                    down(j, tp0 + i + 1, lambda s: 16 * (filled0[s] + i // 2 + 1))
                for s in range(SLOTS):
                    used[s] += (total + 1) // 2 if s < 3 else total // 2
                n.gu += 2 * total
                n.tp += total
                n.block += 3 * total
                n.pos = 3 * total
                n.x += 2 if last else 0

            pe.wait_ge(sem("cond_ready"), 1)
            for q in range(6):
                a = (2 * q) % SLOTS
                for s in (a, a + 1):
                    pe.wait_ge(slot_filled[s], 16 * (q // 3 + 1))
                if q >= 2:
                    pe.wait_ge(gu_evacuated, q - 1)
                o3 = ps[0:2, 4 + q % 2, :].rearrange("p (u c) -> p u c", u=2)
                for k in range(KC):
                    m = pe.matmul(o3, cond[:, 0:2, k], ring[:, a:a + 2, k * EH:(k + 1) * EH],
                                  start=k == 0, stop=k == KC - 1)
                m.then_inc(block_done, 1)
            n.gu = n.block = 6
            n.pos = 0
            used = [2] * SLOTS
            ada_next = [0]

            def ada_groups(count, bank):
                for _ in range(count):
                    g = ada_next[0]
                    _, _, lo, m_, _, _ = ada_pair_of(g // 2)
                    ada_next[0] += 1
                    slots = n.slots(3)
                    for s in slots:
                        filled(s)
                    half = slice(EH * (g % 2), EH * (g % 2) + EH)
                    for k in range(KC):
                        for u, s in enumerate(slots):
                            m = pe.matmul(ps[32 * u:32 * u + m_, bank, half], cond[:, lo:lo + m_, k],
                                          ring[:, s, k * EH:(k + 1) * EH],
                                          start=k == 0, stop=k == KC - 1, skip_group_check=True)
                    m.then_inc(sem("ada_group_done"), 1)

            def ada_bank_free():
                if ada_next[0] > 0:
                    pe.wait_ge(sem("ada_rows_ready"), ada_next[0])

            pe.wait_ge(constants_loaded, 48)
            norm_tiles(CTX)
            norm_tiles(LAT)
            pe.wait_ge(tp_evacuated, n.tp)
            token_major((0, 1, 2, 3))
            ada_groups(1, PROJECTION_BANK)
            token_major((0, 1, 2, 3))
            ada_groups(1, PROJECTION_BANK)
            for hp in range(2):
                if hp == 1:
                    pe.wait_ge(sem("hg_out_read"), 4)
                for _ in range(3):
                    feature_major(0, NT)
                ada_bank_free()
                ada_groups(PROJECTION_GROUPS[hp], PROJECTION_BANK)
                for hh in range(2):
                    hd = 2 * hp + hh
                    for d in range(2):
                        i = 2 * hd + d
                        pe.wait_ge(sem("hg_factors"), i + 1)
                        if i >= 1:
                            pe.wait_ge(sem("hg_scores_read"), i)
                        for t in range(4):
                            c = slice(t * P, (t + 1) * P)
                            m = pe.matmul(ps[:, 4, c], E2[:, d, c], E1[:, d, c], start=True, stop=True)
                        m.then_inc(sem("hg_scores"), 1)
                        ada_bank_free()
                        transposes([E4[:, d, t * P:(t + 1) * P] for t in range(4)])
                        pe.wait_ge(tp_evacuated, n.tp)
                        if i >= 1:
                            pe.wait_ge(sem("hg_states"), i)
                        for c in range(NSC):
                            t, q = c // 4, 32 * (c % 4)
                            m = pe.matmul(ps[:, c % 4, t * P:(t + 1) * P],
                                          T2[q:q + 32, d, t * P:(t + 1) * P], v_tok[q:q + 32, t, hd, 0:P],
                                          start=True, stop=True)
                        m.then_inc(sem("hg_updates"), 1)
                        ada_groups(ADA_A[i], step_bank("A", i))
                        pe.wait_ge(sem("hg_scores_read"), i + 1)
                        pe.wait_ge(sem("hg_states"), i + 1)
                        if i >= 1:
                            pe.wait_ge(sem("hg_out_read"), i)
                        for t in range(4):
                            c0 = ps[:, 5, t * P:(t + 1) * P]
                            m = pe.matmul(c0, T1[:, d, t * P:(t + 1) * P], v_tok[:, t, hd, 0:P],
                                          start=True, stop=False, skip_group_check=True)
                            for q in range(4):
                                c = 4 * t + q
                                if c == (0 if d == 0 else NSC // 2 - 1):
                                    continue
                                m = pe.matmul(ps[32 * q:32 * q + 32, 5, t * P:(t + 1) * P],
                                              E3[:, d, c * 32:(c + 1) * 32], state[:, c, :],
                                              start=False, stop=True, skip_group_check=True)
                        m.then_inc(sem("hg_out"), 1)
            pe.wait_ge(sem("hg_out_read"), 8)
            token_major((0, 1, 2, 3))
            ada_bank_free()
            ada_groups(1, PROJECTION_BANK)
            token_major((0, 1, 2, 3))
            ada_bank_free()
            ada_groups(1, PROJECTION_BANK)
            feature_major(0, NT)
            feature_major(0, NT)
            ada_bank_free()
            ada_groups(1, PROJECTION_BANK)
            pe.wait_ge(sem("hg_states"), 8)
            ada_bank_free()
            for part in range(2):
                for k in range(KC):
                    m = pe.matmul(ps[0:ROWS, part, :], w_gates[:, k, part, :], hT[:, k, :], start=k == 0, stop=k == KC - 1)
            m.then_inc(sem("ml_gates"), 1)
            pe.wait_ge(sem("ml_rows"), 1)
            for src in (rows_e, rows_f):
                transposes([src[:, t * P:(t + 1) * P] for t in range(4)])
            pe.wait_ge(sem("row_select_loaded"), 16)
            pe.wait_ge(sem("ml_qk"), 4)
            for hd in range(MLSTM_HEADS):
                q0 = 64 * (hd % 2)
                qh, kh = qk[q0:q0 + 64, hd // 2, :], qk[q0:q0 + 64, 2 + hd // 2, :]
                if hd >= 1:
                    pe.wait_ge(sem("ml_weights"), 8 * hd)
                for si in range(4):
                    c0 = 0 if si < 2 else SEQ
                    m = pe.matmul(ps[:, si, c0:NT], kh[:, si * P:(si + 1) * P], qh[:, c0:NT], start=True, stop=True)
                m.then_inc(sem("ml_scores"), 1)
                for d in range(2):
                    i = 2 * hd + d
                    ada_bank_free()
                    if i >= 2:
                        pe.wait_ge(sem("ml_weights"), 4 * (i - 1))
                    pe.matmul(ps[:, 4 + d, :], row_select[:, 4 * d + hd, :], rows_d, start=True, stop=True).then_inc(sem("ml_max"), 1)
                    ada_groups(ADA_B[i], step_bank("B", i))
                    pe.wait_ge(sem("ml_weights"), 4 * (i + 1))
                    pe.wait_ge(tp_evacuated, n.tp)
                    if i >= 1:
                        pe.wait_ge(sem("ml_out_read"), i)
                    for ti in range(4):
                        seg, own = divmod(ti, 2)
                        keys = [s for s in range(2 * seg, 2 * seg + 2) if (s <= ti if d == 0 else s >= ti)]
                        keys = ([0, 1] if seg else []) + keys
                        for si in keys:
                            m = pe.matmul(ps[:, 6 + ti // 2, (ti % 2) * 129:(ti % 2) * 129 + 129],
                                          p_sb[:, si, ti * P:(ti + 1) * P], v_tok[:, si, hd, :],
                                          start=si == keys[0], stop=si == keys[-1])
                    m.then_inc(sem("ml_out"), 1)
            pe.wait_ge(sem("ml_out_read"), 8)
            ada_bank_free()

            def mixed_tiles(src, tiles):
                for t in tiles:
                    n.h += 1
                    pe.wait_ge(h_ready, n.h)
                    for half in range(2):
                        transposes([src[:, t, (4 * half + kk) * P:(4 * half + kk + 1) * P] for kk in range(4)])

            mixed_tiles(o, range(4))
            mixer_out((0, 1, 2, 3), 0)
            norm_tiles(CTX)
            pe.wait_ge(tp_evacuated, n.tp)
            mlp(NFF, 0)
            norm_tiles(LAT)
            pe.wait_ge(tp_evacuated, n.tp)
            mlp(NFF, SEQ)
            norm_tiles(CTX)
            norm_tiles(LAT)
            pe.wait_ge(tp_evacuated, n.tp)
            token_major(LAT)
            token_major(LAT)
            token_major((0, 1, 2, 3))
            pe.wait_ge(sem("at_q_ready"), 2)
            for hd in range(0, 8, 2):
                transposes([aqr[:, t, hd + a, :] for a in range(2) for t in range(2)])
            pe.wait_ge(sem("at_k_ready"), 4)
            for kv in range(2):
                transposes([akr[:, t, kv, :] for t in range(4)])
            pe.wait_ge(tp_evacuated, n.tp)
            pe.wait_ge(x_updated, n.x)
            pe.wait_ge(gu_evacuated, n.gu)
            N_AT = 16

            def scores(i):
                hd, t = divmod(i, 2)
                if i >= 2:
                    pe.wait_ge(sem("at_exp"), i - 1)
                pe.matmul(ps[:, 4 + i % 2, :], qT[:, hd, t * P:(t + 1) * P], kT[:, hd // 4, :],
                          start=True, stop=True).then_inc(sem("at_scores"), 1)

            scores(0)
            for i in range(N_AT):
                if i + 1 < N_AT:
                    scores(i + 1)
                hd, t = divmod(i, 2)
                pe.wait_ge(sem("at_prob"), i + 1)
                transposes([prob[:, i % 2, s * P:(s + 1) * P] for s in range(4)])
                pe.wait_ge(tp_evacuated, n.tp)
                for s in range(4):
                    m = pe.matmul(ps[:, i // 4, (i % 4) * P:(i % 4 + 1) * P], av[:, s, hd // 4, :], probT[:, i % 2, s, :],
                                  start=s == 0, stop=s == 3)
                m.then_inc(sem("at_out"), 1)
            pe.wait_ge(sem("at_outT"), 4)
            mixer_out(LAT, 0)
            norm_tiles(LAT)
            pe.wait_ge(tp_evacuated, n.tp)
            mlp(NFF, SEQ)
            norm_tiles(LAT)
            pe.wait_ge(tp_evacuated, n.tp)
            for c in range(12):
                feature_major(SEQ, NT)
            pe.wait_ge(sem("sconv_ready"), KC)
            mixer_out(LAT, SEQ)

            rounds_before = [0]

            def moe(l):
                norm_tiles(LAT)
                pe.wait_ge(tp_evacuated, n.tp)
                pe.wait_ge(sem("route_w_ready"), l + 1)
                for t in range(2):
                    outs = gu_bank()
                    for k in range(KC):
                        m = pe.matmul(outs[:, 0:ROUTE_W], hT[:, k, SEQ + t * P:SEQ + (t + 1) * P], w_route[:, k, :],
                                      start=k == 0, stop=k == KC - 1)
                    m.then_inc(block_done, 1)
                mlp(2, SEQ, last=False)
                pe.wait_ge(sem("picked_ready"), 2 * (l + 1))
                pe.wait_ge(gu_evacuated, n.gu)
                pe.matmul(ps[:, 4, 0:64], s_le_t[:, :], picked[:, 0, :], start=True, stop=True)
                pe.matmul(ps[:, 4, 64:128], s_le_t[:, :], picked[:, 1, :], start=True, stop=False)
                pe.matmul(ps[:, 4, 64:128], ones_t[:, :], picked[:, 0, :], start=False, stop=True)
                pe.matmul(ps[:, 4, 128:192], ones_t[:, :], picked[:, 0, :], start=True, stop=False)
                pe.matmul(ps[:, 4, 128:192], ones_t[:, :], picked[:, 1, :], start=False, stop=True).then_inc(sem("ranks_summed"), 1)
                pe.wait_ge(tp_evacuated, n.tp)
                pe.wait_ge(sem("rounds_known"), l + 1)
                rounds = pe.value_load(rounds_i[0:1, 0:1], min_val=1, max_val=SEQ // CAP)
                S = sem
                before = 0 if l == 0 else rounds_before[0] * QUADS
                rounds_before[0] = rounds

                def one_round(c, filled_gu, filled_down):
                    pe.wait_ge(S("sel_ready"), c + 1)
                    for k in range(KC):
                        for t in range(2):
                            m = pe.matmul(ps[:, 4 + k // 4, (k % 4) * P:(k % 4 + 1) * P], h[:, t, k::KC], sel[:, t, :],
                                          start=t == 0, stop=t == 1)
                    m.then_inc(S("gathered"), 1)
                    pe.wait_ge(S("sel_gated_ready"), c + 1)
                    for t in range(2):
                        m = pe.transpose(ps[:, 7, t * P:(t + 1) * P], sel_gated[:, t, :], ident[:, :])
                    m.then_inc(S("sel_turned"), 1)
                    pe.wait_ge(S("x_slots_lo"), c + 1)
                    pe.wait_ge(S("x_slots_hi"), c + 1)
                    for s in GATE_UP_SLOT:
                        pe.wait_ge(slot_filled[s], filled_gu(s))
                        pe.wait_ge(slot_filled[s + 1], filled_gu(s + 1))
                    for k in range(KC):
                        for a in range(QUAD):
                            m = pe.matmul(ps[a * CAP:(a + 1) * CAP, 6, :].rearrange("p (u c) -> p u c", u=2),
                                          x_slots[:, k, a * CAP:(a + 1) * CAP], slot_pair(GATE_UP_SLOT[a])[:, :, k * EH:(k + 1) * EH],
                                          start=k == 0, stop=k == KC - 1, skip_group_check=True)
                    m.then_inc(S("quad_gate_up"), 1)
                    pe.wait_ge(S("quad_hid"), c + 1)
                    for j in range(2):
                        m = pe.transpose(ps[:, 7, (2 + j) * P:(3 + j) * P], q_hid[:, j::2], ident[:, :])
                    m.then_inc(S("hid_turned"), 1)
                    pe.wait_ge(S("quad_hidT"), c + 1)
                    for s in DOWN_SLOT:
                        pe.wait_ge(slot_filled[s], filled_down(s))
                    for half in range(2):
                        for j in range(2):
                            for a in range(QUAD):
                                m = pe.matmul(ps[a * CAP:(a + 1) * CAP, 4 + half, :], q_hidT[:, j, a * CAP:(a + 1) * CAP],
                                              slot(DOWN_SLOT[a])[:, j * D + half * 512:j * D + (half + 1) * 512],
                                              start=j == 0, stop=j == 1, skip_group_check=True)
                    m.then_inc(S("quad_down"), 1)
                    pe.wait_ge(S("sel_T_ready"), c + 1)
                    pe.wait_ge(S("z_lo"), c + 1)
                    pe.wait_ge(S("z_hi"), c + 1)
                    for t in range(2):
                        for half in range(2):
                            m = pe.matmul(ps[:, 2 * t + half, :], sel_T[:, t * P:(t + 1) * P], z_slots[:, half * 512:(half + 1) * 512],
                                          start=False, stop=False, skip_group_check=True)
                    m.then_inc(S("rounds_done"), 1)

                filled0 = list(used)
                more0 = 16 * QUADS * l
                with pe.Fori(0, QUADS) as q:
                    fg = lambda s: q * 16 + 16 + (16 * filled0[s] if s < SLOTS else more0)
                    with pe.If(rounds > 1):
                        with pe.Fori(1, rounds) as r:
                            one_round(q * rounds + before + r - 1, fg, fg)
                    one_round(q * rounds + before + rounds - 1, fg, fg)
                pe.matmul(ps[:, 3, :], zero_t[:, 0:P], zero_t[:, :], start=False, stop=True, skip_group_check=True) \
                    .then_inc(block_done, 1)
                n.block += 1
                n.x += 2
                n.pos = 0
                for s in range(SLOTS):
                    used[s] += QUADS

            moe(0)
            norm_tiles(LAT)
            pe.wait_ge(tp_evacuated, n.tp)
            for c in range(12):
                feature_major(SEQ, NT)
            token_major(LAT)
            token_major(LAT)
            pe.wait_ge(sem("gdn_constants"), 16 * 6)
            pe.wait_ge(x_updated, n.x)
            for t in range(2):
                for k in range(KC):
                    m = pe.matmul(ps[:, t, 0:16], hT[:, k, SEQ + t * P:SEQ + (t + 1) * P], w_gdn_ba[:, k, :],
                                  start=k == 0, stop=k == KC - 1)
            m.then_inc(sem("gd_ba"), 1)
            for t in range(2):
                for c in range(0, 24, 4):
                    if t == 0:
                        pe.wait_ge(sem("gd_conv"), c + 4)
                    transposes([gT[:, c + q, t * P:(t + 1) * P] for q in range(4)])
            pe.wait_ge(sem("gd_decays"), 1)
            pe.matmul(ps[:, 2, 0:16], s_le_t[:, :], g_t[:, 0, :], start=True, stop=True)
            pe.matmul(ps[:, 3, 0:16], ones_t[:, :], g_t[:, 0, :], start=True, stop=True).then_inc(sem("gd_sums"), 1)
            pe.wait_ge(sem("gd_norm"), 1)
            for src in ("k", "kb", "q"):
                for hd in range(0, 8, 2):
                    where = {"q": gtok, "k": gtok, "kb": gkb}[src]
                    off = {"q": 0, "k": 8, "kb": 0}[src]
                    transposes([where[:, t, off + hd + a, :] for a in range(2) for t in range(2)])
            pe.wait_ge(sem("gd_qe"), 1)
            for hd in range(0, 8, 4):
                transposes([gtok[:, 1, hd + a, :] for a in range(4)])
            pe.wait_ge(tp_evacuated, n.tp)
            for g in range(2):
                if g == 1:
                    pe.wait_ge(sem("gd_batch"), 2)
                for t in range(2):
                    c = slice(t * P, (t + 1) * P)
                    pe.wait_ge(sem("gd_gb"), 2 * g + t + 1)
                    if t == 1:
                        pe.wait_ge(sem("gd_scores_read"), 2 * g + 1)
                    for a in range(4):
                        hd = 4 * g + a
                        col = slice(a * P, (a + 1) * P)
                        pe.matmul(ps[:, 0, col], TT[t][:, a, :], s_le_t[:, :], start=True, stop=True)
                        pe.matmul(ps[:, 1, col], g_kT[:, hd, c], g_kbT[:, hd, c], start=True, stop=True)
                        m = pe.matmul(ps[:, 2, col], g_kT[:, hd, c], g_qT[:, hd, c], start=True, stop=True)
                    m.then_inc(sem("gd_scores"), 1)
                pe.wait_ge(sem("gd_scores_read"), 2 * g + 2)
                for lvl in range(LEVELS):
                    for t in range(2):
                        s0 = 2 * (LEVELS * g + lvl) + t
                        pe.wait_ge(sem("gd_lm"), s0 + 1)
                        for a in range(4):
                            m = pe.matmul(ps[:, 3 * t, a * P:(a + 1) * P], LM[t][:, a, :], DD[t][:, a, :], start=True, stop=True)
                        m.then_inc(sem("gd_t"), 1)
                    for t in range(2):
                        s0 = 2 * (LEVELS * g + lvl) + t
                        pe.wait_ge(sem("gd_t_read"), s0 + 1)
                        for a in range(4):
                            pe.matmul(ps[:, 3 * t + 1, a * P:(a + 1) * P], DT_[t][:, a, :], TT[t][:, a, :], start=True, stop=True)
                        for a in range(4):
                            m = pe.matmul(ps[:, 3 * t + 2, a * P:(a + 1) * P], TT[t][:, a, :], DT_[t][:, a, :], start=True, stop=True)
                        m.then_inc(sem("gd_step"), 1)
                pe.wait_ge(sem("gd_inverse"), 2 * LEVELS * (g + 1))
                for t in range(2):
                    for a in range(4):
                        m = pe.matmul(ps[:, 4 * t, a * P:(a + 1) * P], DT_[t][:, a, :], gtok[:, t, 16 + 4 * g + a, :], start=True, stop=True)
                    if t == 0:
                        m.then_inc(sem("gd_u"), 1)
                for a in range(4):
                    m = pe.matmul(ps[:, 1, a * P:(a + 1) * P], gkb[:, 1, 4 * g + a, :], DT_[1][:, a, :], start=True, stop=True)
                m.then_inc(sem("gd_w"), 1)
                pe.wait_ge(sem("gd_u_read"), g + 1)
                for a in range(4):
                    pe.matmul(ps[:, 2, a * P:(a + 1) * P], AT[0][:, a, :], U[:, a, :], start=True, stop=True)
                for a in range(4):
                    m = pe.matmul(ps[:, 3, a * P:(a + 1) * P], g_kdec[:, 4 * g + a, :], U[:, a, :], start=True, stop=True)
                m.then_inc(sem("gd_o"), 1)
                pe.wait_ge(sem("gd_batch"), 2 * g + 1)
                for a in range(4):
                    m = pe.matmul(ps[:, 5, a * P:(a + 1) * P], WT[:, a * P:(a + 1) * P], gS[:, a, :], start=True, stop=True)
                m.then_inc(sem("gd_ws"), 1)
                pe.wait_ge(sem("gd_vnew"), g + 1)
                for a in range(4):
                    pe.matmul(ps[:, 3, a * P:(a + 1) * P], AT[1][:, a, :], U[:, a, :], start=True, stop=False)
                    m = pe.matmul(ps[:, 3, a * P:(a + 1) * P], gqe_T[:, 4 * g + a, :], gS[:, a, :], start=False, stop=True)
                m.then_inc(sem("gd_o"), 1)
            mixed_tiles(g_o, range(2))
            mixer_out(LAT, SEQ)
            moe(1)

        @block.scalar
        def _(act):
            n = Counts()
            tell = Teller(act)

            def evacuate(dst, width=512, parts=P):
                act.wait_ge(tp_full, n.tp + 1)
                src = ps[0:parts, 6 + n.tp % 2, 0:width]
                n.tp += 1
                if len(dst.shape) == 3:
                    src = src.rearrange("p (a b) -> p a b", a=dst.shape[1])
                if len(dst.shape) == 4:
                    src = src.rearrange("p (a b c) -> p a b c", a=dst.shape[1], b=dst.shape[2])
                tell(nc.scalar.copy(dst, src), tp_evacuated)

            def root_of_norm():
                n.normed += 1
                act.wait_ge(sem("mean_square"), n.normed)
                tell(nc.scalar.activation(rs[:, 0:1], rs[:, 0:1], ACT.Sqrt), sem("rms_ready"))

            def norm_tiles(tiles):
                for t in tiles:
                    root_of_norm()
                    n.h += 1
                    for half in range(2):
                        evacuate(hT[:, 4 * half:4 * half + 4, t * P:(t + 1) * P])

            def mixed_tiles(tiles, col0):
                for t in tiles:
                    n.h += 1
                    for half in range(2):
                        evacuate(hT[:, 4 * half:4 * half + 4, t * P - col0:(t + 1) * P - col0])

            def update_tiles(tiles, block_of):
                for i, t in enumerate(tiles):
                    update_tile(i, block_of(i))

            def update_tile(i, complete):
                act.wait_ge(block_done, complete)
                if n.x > 0:
                    act.wait_ge(x_updated, n.x)
                yt = ps[:, 2 * (i % 2):2 * (i % 2) + 2, :].rearrange("p a b -> p (a b)")
                tell(nc.scalar.activation(junk[:, :], yt, ACT.Square, scale=float(D) ** -0.5,
                                          accum_out=ys[:, 0:1]), sem("act_step"))
                tell(nc.scalar.activation(ys[:, 1:2], ys[:, 0:1], ACT.Sqrt, bias=eps_t[:, :]), sem("y_rms_ready"))
                n.x += 1

            def turned(t):
                for half in range(2):
                    evacuate(hT[:, 4 * half:4 * half + 4, t * P:(t + 1) * P])

            def mixer_out(tiles):
                b0 = n.block
                n.block += len(tiles)
                update_tiles(tiles, lambda i: b0 + i + 1)

            def update_and_norm(blocks):
                for i, t in enumerate(LAT):
                    update_tile(i, blocks[i])
                    if i == 1:
                        turned(LAT[0])
                    root_of_norm()
                n.h += 2
                turned(LAT[1])

            def act_loop(count):
                if count > 0:
                    with act.Fori(0, count) as r:
                        yield r

            def mlp(total, last=True):
                b0, tp0, gu0 = n.block, n.tp, n.gu
                told = tell.told.get("sig_ready", 0)

                def sigmoid(t, blk):
                    act.wait_ge(block_done, blk)
                    nc.scalar.activation(sig[:, t, :], ps[:, 4 + t, 0:EH], ACT.Sigmoid).then_inc(sem("sig_ready"), 1)

                def turn(i_par, full):
                    act.wait_ge(tp_full, full)
                    nc.scalar.copy(hidT[:, i_par, :, :], ps[:, 6 + (tp0 + i_par) % 2, :].rearrange("p (a b) -> p a b", a=2)) \
                        .then_inc(tp_evacuated, 1)

                for t in range(2):
                    sigmoid(t, b0 + 1 + t)
                pairs = (total - 1) // 2
                for r in act_loop(pairs):
                    for j in range(2):
                        sigmoid(0, r * 6 + (b0 + 3 * (j + 1)))
                        turn(j, r * 2 + (tp0 + j + 1))
                        sigmoid(1, r * 6 + (b0 + 3 * (j + 1) + 1))
                for i in range(2 * pairs, total):
                    if i + 1 < total:
                        sigmoid(0, b0 + 3 * (i + 1))
                    turn(i % 2, tp0 + i + 1)
                    if i + 1 < total:
                        sigmoid(1, b0 + 3 * (i + 1) + 1)
                tell.told["sig_ready"] = told + 2 * total
                tell.told["tp_evacuated"] = tp0 + total
                n.block += 3 * total
                n.tp += total
                n.gu += 2 * total
                b1 = n.block
                if last:
                    update_tiles(LAT, lambda i: b1)

            def sigmoid_blocks(count, c=None):
                for _ in range(count):
                    i = n.gu
                    n.block += 1
                    n.gu += 1
                    act.wait_ge(block_done, n.block)
                    act.wait_ge(gu_evacuated, i)
                    tell(nc.scalar.activation(g_sig, ps[:, 4 + i % 2, :], ACT.Sigmoid), sem("gate_sig"))

            act.wait_ge(sem("cond_loaded"), 48)
            tell(nc.scalar.activation(cond_sig[:, :, :], cond[:, :, :], ACT.Sigmoid), sem("cond_sig_ready"))
            n.block = n.gu = 6
            act.wait_ge(sem("zero_ready"), 1)
            norm_tiles(CTX)
            norm_tiles(LAT)
            n.block += 4
            n.gu += 4
            sigmoid_blocks(4)
            act.wait_ge(sem("lb_max"), 1)
            tell(nc.scalar.activation(lbs[:, 0:3, :, :], lbs[:, 0:3, :, :], ACT.Exp), sem("lb_exp"))
            for hp in range(2):
                n.block += 6
                n.gu += 6
                act.wait_ge(gu_evacuated, n.gu)

                def sigmoids(i):
                    d, z = i % 2, hg_z[:, (i // 2) % 2, i % 2, :]
                    if i >= 2:
                        act.wait_ge(sem("hg_out"), i - 1)
                    tell(nc.scalar.activation(T1[:, d, :], z, ACT.Sigmoid), sem("act_step"))
                    tell(nc.scalar.activation(z, z, ACT.Sigmoid, scale=-1.0), sem("hg_sig"))

                def decays(i):
                    d = i % 2
                    act.wait_ge(sem("hg_f"), i + 1)
                    tell(nc.scalar.activation(T1[:, d, :], T1[:, d, :], ACT.Ln), sem("hg_log"))
                    act.wait_ge(sem("hg_d1"), i + 1)
                    tell(nc.scalar.activation(E1[:, d, :], E4[:, d, :], ACT.Exp), sem("act_step"))
                    tell(nc.scalar.activation(E2[:, d, :], E4[:, d, :], ACT.Exp, scale=-1.0), sem("act_step"))
                    tell(nc.scalar.activation(E3[:, d, :], T2[:, d, :], ACT.Exp), sem("act_step"))
                    tell(nc.scalar.activation(E4[:, d, :], T1[:, d, :], ACT.Exp), sem("hg_exp"))

                sigmoids(4 * hp)
                decays(4 * hp)
                for i in range(4 * hp, 4 * hp + 4):
                    ahead = i + 1 < 4 * hp + 4
                    if ahead:
                        sigmoids(i + 1)
                    act.wait_ge(sem("hg_factors"), i + 1)
                    evacuate(T2[:, i % 2, :])
                    if ahead:
                        decays(i + 1)
            n.block += 4
            n.gu += 4
            sigmoid_blocks(4)
            for c in range(4):
                act.wait_ge(sem("ml_conv"), c + 1)
                tell(nc.scalar.activation(g_sig2, qk[:, c, :], ACT.Sigmoid), sem("ml_sig"))
                n.block += 1
                n.gu += 1
            act.wait_ge(sem("ml_abs"), 1)
            tell(nc.scalar.activation(rows_c, rows_c, ACT.Exp, scale=-1.0), sem("act_step"))
            tell(nc.scalar.activation(rows_c, rows_c, ACT.Ln, bias=1.0), sem("ml_log"))
            act.wait_ge(sem("ml_m"), 1)
            tell(nc.scalar.activation(rows_b, rows_b, ACT.Exp, scale=-1.0), sem("ml_em"))
            for i in range(2):
                act.wait_ge(tp_full, n.tp + 1)
                src = ps[:, 6 + n.tp % 2, :].rearrange("p (t c) -> p t c", t=4)[:, :, 0:ROWS]
                n.tp += 1
                tell(nc.scalar.copy(colsT[:, i, :, :], src), tp_evacuated)
            for i in range(8):
                for si in range(4):
                    k = 4 * i + si
                    act.wait_ge(sem("ml_gap"), k + 1)
                    w = p_sb[:, si, (0 if si < 2 else SEQ):NT]
                    tell(nc.scalar.activation(w, w, ACT.Exp, scale=-1.0), sem("ml_exp"))
            for t in range(4):
                act.wait_ge(sem("ab_ms"), t + 1)
                tell(nc.scalar.activation(msum[:, 0, :], msum[:, 0, :], ACT.Sqrt), sem("ab_rms"))
            mixed_tiles(range(4), 0)
            for b in range(2):
                act.wait_ge(sem(f"mod_stored_{b}"), ADA_STORED[b])
            mixer_out((0, 1, 2, 3))
            norm_tiles(CTX)
            mlp(NFF)
            norm_tiles(LAT)
            mlp(NFF)
            norm_tiles(CTX)
            norm_tiles(LAT)
            n.block += 8
            n.gu += 8
            for i in range(6):
                act.wait_ge(sem("at_ms"), i + 1)
                w = 8 if i < 2 else 2
                tell(nc.scalar.activation(astat[:, 0, 0:w], astat[:, 0, 0:w], ACT.Sqrt), sem("at_rms"))
            for hd in range(0, 8, 2):
                evacuate(qT[:, hd:hd + 2, :])
            for kv in range(2):
                evacuate(kT[:, kv, :])
            for i in range(16):
                act.wait_ge(sem("at_max"), i + 1)
                tell(nc.scalar.activation(prob[:, i % 2, :], ps[:, 4 + i % 2, :], ACT.Exp, scale=float(P) ** -0.5,
                                          bias=smax[:, i % 2, 1:2], accum_out=smax[:, i % 2, 2:3]), sem("at_exp"))
                evacuate(probT[:, i % 2, :, :])
            n.block += 2
            update_and_norm((n.block - 1, n.block))
            mlp(NFF, False)
            update_and_norm((n.block, n.block))
            n.block += 24
            n.gu += 24
            n.block += 2
            update_and_norm((n.block - 1, n.block))

            rounds_before = [0]

            def moe(l):
                for t in range(2):
                    i = 2 * l + t
                    n.block += 1
                    n.gu += 1
                    act.wait_ge(sem("rt_shifted"), i + 1)
                    tell(nc.scalar.activation(rt1[:, 0:N_GROUPS], rt1[:, 0:N_GROUPS], ACT.Exp, accum_out=rt1[:, 8:9]), sem("act_step"))
                    tell(nc.scalar.activation(rt1[:, 9:10], rt1[:, 9:10], ACT.Exp), sem("act_step"))
                    tell(nc.scalar.activation(moe_gates[:, t, 64:65], ps[:, 4 + (n.gu - 1) % 2, ROUTE_W - 1:ROUTE_W], ACT.Sigmoid),
                         sem("rt_exp"))
                mlp(2, last=False)
                act.wait_ge(sem("rounds_known"), l + 1)
                rounds = act.value_load(rounds_i[0:1, 0:1], min_val=1, max_val=SEQ // CAP)
                S = sem
                before = 0 if l == 0 else rounds_before[0] * QUADS
                rounds_before[0] = rounds

                def one_round(c):
                    act.wait_ge(S("gathered"), c + 1)
                    nc.scalar.copy(x_slots[:, 0:4, :], ps[:, 4, :].rearrange("p (a b) -> p a b", a=4)).then_inc(S("x_slots_lo"), 1)
                    act.wait_ge(S("sel_turned"), c + 1)
                    nc.scalar.copy(sel_T, ps[:, 7, 0:SEQ]).then_inc(S("sel_T_ready"), 1)
                    act.wait_ge(S("quad_gate_up"), c + 1)
                    nc.scalar.activation(q_sig, ps[:, 6, 0:EH], ACT.Sigmoid).then_inc(S("quad_sig"), 1)
                    act.wait_ge(S("hid_turned"), c + 1)
                    nc.scalar.copy(q_hidT, ps[:, 7, SEQ:512].rearrange("p (a b) -> p a b", a=2)).then_inc(S("quad_hidT"), 1)
                    act.wait_ge(S("quad_down"), c + 1)
                    nc.scalar.copy(z_slots[:, 0:512], ps[:, 4, :]).then_inc(S("z_lo"), 1)

                with act.Fori(0, QUADS) as q:
                    with act.If(rounds > 1):
                        with act.Fori(1, rounds) as r:
                            one_round(q * rounds + before + r - 1)
                    one_round(q * rounds + before + rounds - 1)
                n.block += 1

            moe(0)
            update_and_norm((n.block, n.block))
            for c in range(24):
                act.wait_ge(sem("gd_pre"), c + 1)
                tell(nc.scalar.activation(h[:, 0, 0:SEQ], gT[:, c, :], ACT.Sigmoid), sem("gd_sig"))
                n.block += 1
                n.gu += 1
            for c in range(4):
                i = n.gu
                n.block += 1
                n.gu += 1
                act.wait_ge(block_done, n.block)
                act.wait_ge(gu_evacuated, i)
                tell(nc.scalar.activation(junk[:, 0:512], ps[:, 4 + i % 2, :], ACT.Sigmoid), sem("gate_sig"))
            act.wait_ge(sem("gd_ba_read"), 1)
            tell(nc.scalar.activation(g_t[:, 1, :], g_t[:, 1, :], ACT.Sigmoid), sem("act_step"))
            tell(nc.scalar.activation(g_t[:, 3, :], g_t[:, 3, :], ACT.Exp, scale=-1.0), sem("act_step"))
            tell(nc.scalar.activation(g_t[:, 3, :], g_t[:, 3, :], ACT.Ln, bias=1.0), sem("act_step"))
            tell(nc.scalar.activation(gdn_vec[:, 2, :], gdn_vec[:, 0, :], ACT.Exp), sem("gd_act"))
            for t in range(2):
                for c in range(0, 24, 4):
                    evacuate(gtok[:, t, c:c + 4, :])
            for t in range(2):
                act.wait_ge(sem("gd_ms"), t + 1)
                tell(nc.scalar.activation(stat[:, 0:2, :], stat[:, 0:2, :], ACT.Sqrt), sem("gd_rms"))
            act.wait_ge(sem("gd_exparg"), 1)
            tell(nc.scalar.activation(g_t[:, 6, :], g_t[:, 4, :], ACT.Exp), sem("act_step"))
            tell(nc.scalar.activation(g_t[:, 7, :], g_t[:, 5, :], ACT.Exp), sem("act_step"))
            tell(nc.scalar.activation(g_t[:, 8, :], g_t[:, 8, :], ACT.Exp), sem("gd_exp"))
            for dst in (g_kT, g_kbT, g_qT):
                for hd in range(0, 8, 2):
                    evacuate(dst[:, hd:hd + 2, :])
            for hd in range(0, 8, 4):
                evacuate(gqe_T[:, hd:hd + 4, :])
            for g in range(2):
                for t in range(2):
                    act.wait_ge(sem("gd_gap"), 2 * g + t + 1)
                    tell(nc.scalar.activation(LM[t], LM[t], ACT.Exp), sem("gd_dec"))
                for lvl in range(LEVELS):
                    for t in range(2):
                        act.wait_ge(sem("gd_t"), 2 * (LEVELS * g + lvl) + t + 1)
                        nc.scalar.copy(TT[t], quarter(ps[:, 3 * t, :])).then_inc(sem("gd_t_read"), 1)
            for t in range(2):
                act.wait_ge(sem("gd_oms"), t + 1)
                tell(nc.scalar.activation(stat[:, 0, :], stat[:, 0, :], ACT.Sqrt), sem("gd_orms"))
            mixed_tiles(range(2), 0)
            n.block += 2
            update_and_norm((n.block - 1, n.block))
            moe(1)
            update_tiles(LAT, lambda i: n.block)

        @block.vector
        def _(dve):
            n = Counts()
            tell = Teller(dve)
            V = nc.vector
            step = sem("dve_step")
            h_turned = [0, 0]

            def do(ins):
                tell(ins, step)

            def gu_next():
                i = n.gu
                n.gu += 1
                n.block += 1
                dve.wait_ge(block_done, n.block)
                return ps[:, 4 + i % 2, :]

            pres, posts = [0], [0]

            def norm_tile(t, first):
                b = n.h % 2
                if h_turned[b]:
                    dve.wait_ge(tp_full, h_turned[b])
                do(V.tensor_tensor_reduce(out=h[:, b, :], in0=x_sb[:, t, :], in1=x_sb[:, t, :], scale=1.0 / D,
                                          scalar=0.0, op0=ALU.mult, op1=ALU.add, accum_out=rs[:, 0:1]))
                tell(V.tensor_scalar(rs[:, 0:1], rs[:, 0:1], EPS, None, ALU.add), sem("mean_square"))
                n.normed += 1
                dve.wait_ge(sem("rms_ready"), n.normed)
                do(V.reciprocal(rs[:, 1:2], rs[:, 0:1]))
                if first:
                    pres[0] += 1
                    dve.wait_ge(sem("pre_ready"), pres[0])
                do(V.scalar_tensor_tensor(out=h[:, b, :], in0=x_sb[:, t, :], scalar=rs[:, 1:2], in1=v_scale[:, :],
                                          op0=ALU.mult, op1=ALU.mult))
                tell(V.tensor_tensor(h[:, b, :], h[:, b, :], v_shift[:, :], ALU.add), h_ready)
                n.h += 1
                n.tp += 2
                h_turned[b] = n.tp

            def update_tile(t, i):
                b = n.h % 2
                if i % 2 == 0:
                    posts[0] += 1
                    dve.wait_ge(sem("post_ready"), posts[0])
                yt = ps[:, 2 * (i % 2):2 * (i % 2) + 2, :].rearrange("p a b -> p (a b)")
                dve.wait_ge(sem("y_rms_ready"), n.x + 1)
                do(V.reciprocal(ys[:, 2:3], ys[:, 1:2]))
                if h_turned[b]:
                    dve.wait_ge(tp_full, h_turned[b])
                do(V.scalar_tensor_tensor(out=h[:, b, :], in0=yt, scalar=ys[:, 2:3], in1=v_gate[:, :],
                                          op0=ALU.mult, op1=ALU.mult))
                tell(V.tensor_tensor(x_sb[:, t, :], x_sb[:, t, :], h[:, b, :], ALU.add), x_updated)
                n.x += 1

            def norm_tiles(tiles):
                for k, t in enumerate(tiles):
                    norm_tile(t, k == 0)

            def update_tiles(tiles):
                for i, t in enumerate(tiles):
                    update_tile(t, i)

            def update_and_norm():
                for i, t in enumerate(LAT):
                    update_tile(t, i)
                    norm_tile(t, i == 0)

            def dve_loop(count):
                if count > 0:
                    with dve.Fori(0, count) as r:
                        yield r

            def mlp(total, tiles, gated, last=True):
                b0, gu0, tp0 = n.block, n.gu, n.tp
                sg0 = tell.told.get("sig_seen", 0)

                def hidden(i_par, t, sig_count, sw_count):
                    dve.wait_ge(sem("sig_ready"), sig_count)
                    g = gate_now[:, t, i_par:i_par + 1] if gated else 1.0
                    V.scalar_tensor_tensor(out=swish[:, t, :], in0=ps[:, 4 + t, 0:EH], scalar=g, in1=sig[:, t, :],
                                           op0=ALU.mult, op1=ALU.mult).then_inc(sem("swish_ready"), 1)
                    dve.wait_ge(sem("swish_ready"), sw_count)
                    V.tensor_tensor(hid[:, i_par, t, :], swish[:, t, :], ps[:, 4 + t, EH:2 * EH], ALU.mult).then_inc(gu_evacuated, 1)

                def pick(i0, count, width=2):
                    if gated:
                        V.tensor_copy(gate_now[:, :, 0:2], moe_gates[:, :, 64:66]).then_inc(sem("gates_picked"), 1)
                        dve.wait_ge(sem("gates_picked"), count)

                pk0 = tell.told.get("gates_picked", 0)
                pairs = total // 2
                for r in dve_loop(pairs):
                    pick(bass.ds(r * 2, 2), r + (pk0 + 1))
                    for j in range(2):
                        for t in range(2):
                            k = 2 * j + t
                            hidden(j, t, r * 4 + (sg0 + k + 1), r * 4 + (sg0 + k + 1))
                for i in range(2 * pairs, total):
                    for t in range(2):
                        k = 2 * i + t
                        hidden(i % 2, t, sg0 + k + 1, sg0 + k + 1)
                if gated:
                    tell.told["gates_picked"] = pk0 + pairs
                tell.told["sig_seen"] = sg0 + 2 * total
                tell.told["gu_evacuated"] = gu0 + 2 * total
                n.gu += 2 * total
                n.block += 3 * total
                n.tp += total
                if last:
                    update_tiles(tiles)

            do(V.memset(eps_t[:, :], EPS))
            do(V.memset(ones_t[:, :], 1.0))
            tell(V.memset(zero_t[:, :], 0.0), sem("zero_ready"))
            dve.wait_ge(sem("cond_sig_ready"), 1)
            tell(V.tensor_tensor(cond[:, :, :], cond[:, :, :], cond_sig[:, :, :], ALU.mult), sem("cond_ready"))
            dve.wait_ge(sem("ada_bias_loaded_0"), 32)
            with dve.Fori(0, 3) as r:
                for q in range(2):
                    dve.wait_ge(block_done, r * 2 + (q + 1))
                    at = mod_rows[:, bass.ds(r * (2 * 512) + q * 512, 512)]
                    V.tensor_tensor(at, at, ps[0:2, 4 + q, :], ALU.add).then_inc(gu_evacuated, 1)
            dve.wait_ge(gu_evacuated, 6)
            tell(V.tensor_copy(note[:, :], eps_t[0:1, :]), sem("mod_row_ready"))
            tell.told["gu_evacuated"] = 6
            n.gu = n.block = 6
            ada_next = [0]

            def ada_rows(count, bank):
                g0 = ada_next[0]
                ada_next[0] += count
                dve.wait_ge(sem("ada_group_done"), g0 + count)
                for g in range(g0, g0 + count):
                    p = g // 2
                    m_ = ada_pair_of(p)[3]
                    dve.wait_ge(sem(f"ada_bias_loaded_{p % 2}"), (32 if p % 2 == 0 else 0) + 48 * (p // 2 + 1))
                    half = slice(EH * (g % 2), EH * (g % 2) + EH)
                    for u in range(3):
                        at = group_rows[32 * u:32 * u + m_, p % 2, half]
                        ins = V.tensor_tensor(at, at, ps[32 * u:32 * u + m_, bank, half], ALU.add)
                        do(ins) if u < 2 else tell(ins, sem("ada_rows_ready"))

            dve.wait_ge(x_loaded, 32)
            norm_tiles(CTX)
            norm_tiles(LAT)
            dve.wait_ge(sem("mod_stored_0"), 16)
            do(V.memset(v_tok[:, :, :, 128:129], 1.0))
            for t in range(4):
                src = gu_next()
                tell(V.tensor_copy(v_tok[:, t, :, 0:P], src.rearrange("p (h e) -> p h e", h=4)), gu_evacuated)
            ada_rows(1, PROJECTION_BANK)
            gates_seen = 0
            for t in range(4):
                src = gu_next()
                gates_seen += 1
                dve.wait_ge(sem("gate_sig"), gates_seen)
                tell(V.tensor_tensor(gate[:, t, 0:512], src, g_sig, ALU.mult), gu_evacuated)
            ada_rows(1, PROJECTION_BANK)
            dve.wait_ge(sem("ab_constants"), 16 * (2 + 8 + 2))
            do(V.tensor_tensor(lbs[:, 3], lbs[:, 0], lbs[:, 1], ALU.max))
            do(V.tensor_tensor(lbs[:, 3], lbs[:, 3], lbs[:, 2], ALU.max))
            for k in range(3):
                ins = V.tensor_tensor(lbs[:, k], lbs[:, k], lbs[:, 3], ALU.subtract)
                if k < 2:
                    do(ins)
                else:
                    tell(ins, sem("lb_max"))
            dve.wait_ge(sem("lb_exp"), 1)
            do(V.tensor_tensor(lbs[:, 3], lbs[:, 0], lbs[:, 1], ALU.add))
            do(V.tensor_tensor(lbs[:, 3], lbs[:, 3], lbs[:, 2], ALU.add))
            do(V.reciprocal(lbs[:, 3], lbs[:, 3]))
            do(V.tensor_tensor(lbs[:, 4], lbs[:, 0], lbs[:, 3], ALU.mult))
            do(V.tensor_scalar(lbs[:, 5], lbs[:, 4], -1.0, 1.0, ALU.mult, ALU.add))
            for hp in range(2):
                for part in range(3):
                    for hh in range(2):
                        dst = hg_q[:, hh, :] if part == 0 else hg_z[:, hh, part - 1, :]
                        tell(V.tensor_copy(dst, gu_next()), gu_evacuated)
                ada_rows(PROJECTION_GROUPS[hp], PROJECTION_BANK)
                def forget_gates(i):
                    hd, d = divmod(i, 2)
                    hh = hd % 2
                    lb, om = lbs[:, 4, d, hd:hd + 1], lbs[:, 5, d, hd:hd + 1]
                    dve.wait_ge(sem("hg_sig"), i + 1)
                    do(V.tensor_scalar(hg_z[:, hh, d, :], hg_z[:, hh, d, :], om, None, ALU.mult))
                    tell(V.tensor_scalar(T1[:, d, :], T1[:, d, :], om, lb, ALU.mult, ALU.add), sem("hg_f"))

                def log_decays(i):
                    d = i % 2
                    dve.wait_ge(sem("hg_log"), i + 1)
                    along = slice(None) if d == 0 else slice(None, None, -1)
                    do(V.tensor_tensor_scan(T2[:, d, along], chunk_starts, T1[:, d, along], 0.0, ALU.mult, ALU.add))
                    bc = T2[:, d, :].rearrange("p (c t) -> p c t", t=SCAN_CHUNK)
                    mid, last = (15, 31) if d == 0 else (16, 0)
                    do(V.tensor_tensor(E4[:, d, :].rearrange("p (c t) -> p c t", t=SCAN_CHUNK), bc,
                                       bc[:, :, mid:mid + 1].broadcast_to([P, NSC, SCAN_CHUNK]), ALU.subtract))
                    tell(V.tensor_tensor(T1[:, d, :].rearrange("p (c t) -> p c t", t=SCAN_CHUNK),
                                         bc[:, :, last:last + 1].broadcast_to([P, NSC, SCAN_CHUNK]), bc, ALU.subtract),
                         sem("hg_d1"))

                def factors(i):
                    hd, d = divmod(i, 2)
                    hh, last = hd % 2, 31 if d == 0 else 0
                    dve.wait_ge(sem("hg_exp"), i + 1)
                    do(V.tensor_copy(dec[:, d, :], E3[:, d, last::SCAN_CHUNK]))
                    do(V.tensor_tensor(E1[:, d, :], E1[:, d, :], hg_q[:, hh, :], ALU.mult))
                    do(V.tensor_tensor(E2[:, d, :], E2[:, d, :], hg_z[:, hh, d, :], ALU.mult))
                    do(V.tensor_tensor(E3[:, d, :], E3[:, d, :], hg_q[:, hh, :], ALU.mult))
                    tell(V.tensor_tensor(E4[:, d, :], E4[:, d, :], hg_z[:, hh, d, :], ALU.mult), sem("hg_factors"))

                forget_gates(4 * hp)
                log_decays(4 * hp)
                factors(4 * hp)
                for i in range(4 * hp, 4 * hp + 4):
                    hd, d = divmod(i, 2)
                    ahead = i + 1 < 4 * hp + 4
                    if ahead:
                        forget_gates(i + 1)
                    dve.wait_ge(sem("hg_scores"), i + 1)
                    at3 = T1[:, d, :].rearrange("p (t c) -> p t c", t=4)
                    do(V.tensor_scalar(T1[:, d, :], ps[:, 4, :], MAXF, -MAXF, ALU.min, ALU.max))
                    tell(V.tensor_tensor(at3, at3, chunk_masks[:, d:d + 1, :].broadcast_to([P, 4, P]), ALU.mult),
                         sem("hg_scores_read"))
                    if ahead:
                        log_decays(i + 1)
                    dve.wait_ge(sem("hg_updates"), i + 1)
                    order = list(range(NSC)) if d == 0 else list(range(7, -1, -1)) + list(range(15, 7, -1))
                    if i >= 1:
                        dve.wait_ge(sem("hg_out"), i)
                    for a, c in zip(order[:-1], order[1:]):
                        upd = ps[:, a % 4, (a // 4) * P:(a // 4 + 1) * P]
                        if a == order[0]:
                            ins = V.tensor_copy(state[:, c, :], upd)
                        else:
                            ins = V.scalar_tensor_tensor(out=state[:, c, :], in0=state[:, a, :], scalar=dec[:, d, a:a + 1],
                                                         in1=upd, op0=ALU.mult, op1=ALU.add)
                        do(ins) if c != order[-1] else tell(ins, sem("hg_states"))
                    if ahead:
                        factors(i + 1)
                    ada_rows(ADA_A[i], step_bank("A", i))
                    dve.wait_ge(sem("hg_out"), i + 1)
                    dst = o[:, :, hd * P:(hd + 1) * P]
                    src = ps[:, 5, :].rearrange("p (t e) -> p t e", t=4)
                    if d == 0:
                        tell(V.tensor_copy(dst, src), sem("hg_out_read"))
                    else:
                        tell(V.tensor_tensor(dst, dst, src, ALU.add), sem("hg_out_read"))
                    n.tp += 1
            tell(V.tensor_copy(note[:, :], eps_t[0:1, :]), sem("hgrn_done"))
            for t in range(4):
                src = gu_next()
                tell(V.tensor_copy(v_tok[:, t, :, 0:P], src.rearrange("p (h e) -> p h e", h=4)), gu_evacuated)
            ada_rows(1, PROJECTION_BANK)
            for t in range(4):
                src = gu_next()
                gates_seen += 1
                dve.wait_ge(sem("gate_sig"), gates_seen)
                tell(V.tensor_copy(gate[:, t, 512:1024], g_sig), gu_evacuated)
            ada_rows(1, PROJECTION_BANK)
            for c in range(4):
                src = gu_next().rearrange("p (s t) -> p s t", s=2)
                dst = qk[:, c, :].rearrange("p (s t) -> p s t", s=2)
                w = [w_conv[:, c, k:k + 1] for k in range(3)]
                do(V.tensor_scalar(dst, src, w[1], None, ALU.mult))
                do(V.scalar_tensor_tensor(out=dst[:, :, 1:SEQ], in0=src[:, :, 0:SEQ - 1], scalar=w[0], in1=dst[:, :, 1:SEQ],
                                          op0=ALU.mult, op1=ALU.add))
                tell(V.scalar_tensor_tensor(out=dst[:, :, 0:SEQ - 1], in0=src[:, :, 1:SEQ], scalar=w[2],
                                            in1=dst[:, :, 0:SEQ - 1], op0=ALU.mult, op1=ALU.add), sem("ml_conv"))
                dve.wait_ge(sem("ml_sig"), c + 1)
                do(V.tensor_tensor(qk[:, c, :], qk[:, c, :], g_sig2, ALU.mult))
                tell(V.tensor_scalar(qk[:, c, :], qk[:, c, :], 0.125 if c < 2 else 1.0, None, ALU.mult), sem("ml_qk"))
                dve.wait_ge(block_done, n.block)
                tell(V.tensor_copy(note[:, :], eps_t[0:1, :]), gu_evacuated)
            ada_rows(1, PROJECTION_BANK)
            dve.wait_ge(sem("ml_gates"), 1)
            R = slice(0, ROWS)
            do(V.tensor_scalar(rows_a, ps[R, 0, :], gate_bias[R, 0:1], None, ALU.add))
            do(V.tensor_scalar(rows_b, ps[R, 1, :], gate_bias[R, 1:2], None, ALU.add))
            do(V.tensor_scalar(rows_c, rows_b, -1.0, None, ALU.mult))
            tell(V.tensor_tensor(rows_c, rows_c, rows_b, ALU.max), sem("ml_abs"))
            dve.wait_ge(sem("ml_log"), 1)
            do(V.scalar_tensor_tensor(out=rows_b, in0=rows_b, scalar=0.0, in1=rows_c, op0=ALU.min, op1=ALU.subtract))

            def turned(dst, src):
                do(V.tensor_copy(dst[0:32, :], src[0:32, :]))
                do(V.tensor_copy(dst[32:ROWS, :].rearrange("p (s t) -> p s t", s=2),
                                 src[32:ROWS, :].rearrange("p (s t) -> p s t", s=2)[:, :, ::-1]))

            turned(rows_e, rows_a)
            turned(rows_f, rows_b)
            do(V.memset(rows_a, 1.0))
            do(V.tensor_tensor_scan(rows_b, rows_a, rows_f, 0.0, ALU.mult, ALU.add))
            do(V.tensor_tensor(rows_e, rows_e, rows_b, ALU.subtract))
            do(V.tensor_tensor_scan(rows_c, rows_e, rows_e, 0.0, ALU.max, ALU.max))
            tell(V.tensor_tensor(rows_b, rows_b, rows_c, ALU.add), sem("ml_m"))
            turned(rows_d, rows_c)
            do(V.tensor_copy(rows_c, rows_e))
            turned(rows_e, rows_c)
            dve.wait_ge(sem("ml_em"), 1)
            turned(rows_f, rows_b)
            tell(V.tensor_copy(note[:, :], eps_t[0:1, :]), sem("ml_rows"))
            n.tp += 2
            dve.wait_ge(tp_evacuated, n.tp)
            for hd in range(MLSTM_HEADS):
                dve.wait_ge(sem("ml_scores"), hd + 1)
                for d in range(2):
                    i = 2 * hd + d
                    row = 32 * d + hd
                    dve.wait_ge(sem("ml_max"), i + 1)
                    if i >= 1:
                        dve.wait_ge(sem("ml_out"), i)
                    for si in range(4):
                        c0 = 0 if si < 2 else SEQ
                        V.tensor_scalar(p_sb[:, si, c0:NT], ps[:, 4 + d, c0:NT], colsT[:, 0, si, row:row + 1], 0.0,
                                        ALU.subtract, ALU.max).then_inc(sem("ml_gap"), 1)
                    for si in range(4):
                        c0 = 0 if si < 2 else SEQ
                        dve.wait_ge(sem("ml_exp"), 4 * i + si + 1)
                        do(V.tensor_tensor(p_sb[:, si, c0:NT], p_sb[:, si, c0:NT], ps[:, si, c0:NT], ALU.mult))
                        own = p_sb[:, si, si * P:(si + 1) * P]
                        tell(V.tensor_tensor(own, own, (s_le_t if d == 0 else s_ge_t)[:, :], ALU.mult), sem("ml_weights"))
                    ada_rows(ADA_B[i], step_bank("B", i))
                    dve.wait_ge(sem("ml_out"), i + 1)
                    dn = mden[:, 0, :]
                    for b in range(2):
                        ins = V.tensor_copy(mden[:, 1, 2 * b:2 * b + 2], ps[:, 6 + b, P:258:129])
                        do(ins)
                    do(V.tensor_scalar(dn, mden[:, 1, :], -1.0, None, ALU.mult))
                    do(V.tensor_tensor(dn, dn, mden[:, 1, :], ALU.max))
                    do(V.tensor_tensor(dn, dn, colsT[:, 1, :, row], ALU.max))
                    do(V.reciprocal(dn, dn))
                    for ti in range(4):
                        src = ps[:, 6 + ti // 2, (ti % 2) * 129:(ti % 2) * 129 + 129]
                        dn = mden[:, 0, ti:ti + 1]
                        dst = o[:, ti, 512 + hd * P:512 + (hd + 1) * P]
                        if d == 0:
                            ins = V.tensor_scalar(dst, src[:, 0:P], dn, None, ALU.mult)
                        else:
                            ins = V.scalar_tensor_tensor(out=dst, in0=src[:, 0:P], scalar=dn, in1=dst,
                                                         op0=ALU.mult, op1=ALU.add)
                        do(ins) if ti < 3 else tell(ins, sem("ml_out_read"))
            for t in range(4):
                ot = o[:, t, :]
                oh = ot.rearrange("p (h e) -> p h e", h=8)
                do(V.tensor_tensor(h[:, 0, :], ot, ot, ALU.mult))
                do(V.tensor_reduce(msum[:, 0, :], h[:, 0, :].rearrange("p (h e) -> p h e", h=8), AX_X, ALU.add))
                tell(V.tensor_scalar(msum[:, 0, :], msum[:, 0, :], 1.0 / P, EPS, ALU.mult, ALU.add), sem("ab_ms"))
                dve.wait_ge(sem("ab_rms"), t + 1)
                do(V.reciprocal(msum[:, 1, :], msum[:, 0, :]))
                do(V.tensor_tensor(oh, oh, msum[:, 1, :].rearrange("p (h o) -> p h o", o=1).broadcast_to([P, 8, P]), ALU.mult))
                if t == 0:
                    dve.wait_ge(sem("out_g_loaded"), 16)
                do(V.tensor_tensor(ot, ot, out_g, ALU.mult))
                tell(V.tensor_tensor(ot, ot, gate[:, t, :], ALU.mult), h_ready)
                n.h += 1
                n.tp += 2
            n.block += 4
            update_tiles((0, 1, 2, 3))
            norm_tiles(CTX)
            mlp(NFF, CTX, False)
            norm_tiles(LAT)
            mlp(NFF, LAT, False)

            norm_tiles(CTX)
            norm_tiles(LAT)
            for pair in range(2):
                for t in range(2):
                    tell(V.tensor_copy(aq[:, t, 4 * pair:4 * pair + 4, :], gu_next().rearrange("p (h e) -> p h e", h=4)), gu_evacuated)
            for t in range(4):
                src = gu_next().rearrange("p (h e) -> p h e", h=4)
                do(V.tensor_copy(ak[:, t, :, :], src[:, 0:2, :]))
                tell(V.tensor_copy(av[:, t, :, :], src[:, 2:4, :]), gu_evacuated)

            def head_norm(xin, heads, which, i):
                sq = asq[:, 0:heads, :]
                st0, st1 = astat[:, 0, 0:heads], astat[:, 1, 0:heads]
                do(V.tensor_tensor(sq, xin, xin, ALU.mult))
                do(V.tensor_reduce(st0, sq, AX_X, ALU.add))
                tell(V.tensor_scalar(st0, st0, 1.0 / P, EPS, ALU.mult, ALU.add), sem("at_ms"))
                dve.wait_ge(sem("at_rms"), i + 1)
                do(V.reciprocal(st1, st0))
                do(V.tensor_tensor(xin, xin, st1.rearrange("p (h o) -> p h o", o=1).broadcast_to([P, heads, P]), ALU.mult))
                do(V.tensor_tensor(xin, xin, qk_g[:, which:which + 1, :].broadcast_to([P, heads, P]), ALU.mult))

            def rotate(dst, xin, heads, t, s):
                cs, sn = (rope[:, t, i, :].rearrange("p (o a e) -> p o a e", o=1, a=2).broadcast_to([P, heads, 2, 32]) for i in range(2))
                x4 = xin.rearrange("p h (a q e) -> p h a q e", a=2, q=2)
                d4 = dst.rearrange("p h (a q e) -> p h a q e", a=2, q=2)
                w = asq[:, 0:heads, 0:64].rearrange("p h (a e) -> p h a e", a=2)
                x1, x2 = x4[:, :, :, 0, :], x4[:, :, :, 1, :]
                do(V.tensor_tensor(d4[:, :, :, 0, :], x1, cs, ALU.mult))
                do(V.tensor_tensor(w, x2, sn, ALU.mult))
                do(V.tensor_tensor(d4[:, :, :, 0, :], d4[:, :, :, 0, :], w, ALU.subtract))
                do(V.tensor_tensor(d4[:, :, :, 1, :], x2, cs, ALU.mult))
                do(V.tensor_tensor(w, x1, sn, ALU.mult))
                tell(V.tensor_tensor(d4[:, :, :, 1, :], d4[:, :, :, 1, :], w, ALU.add), s)

            dve.wait_ge(sem("att_constants"), 48)
            for t in range(2):
                head_norm(aq[:, t, :, :], 8, 0, t)
                rotate(aqr[:, t, :, :], aq[:, t, :, :], 8, t, sem("at_q_ready"))
            for t in range(4):
                head_norm(ak[:, t, :, :], 2, 1, 2 + t)
                if t < 2:
                    tell(V.tensor_copy(akr[:, t, :, :], ak[:, t, :, :]), sem("at_k_ready"))
                else:
                    rotate(akr[:, t, :, :], ak[:, t, :, :], 2, t - 2, sem("at_k_ready"))
            n.tp += 6
            for i in range(16):
                dve.wait_ge(sem("at_scores"), i + 1)
                sm = smax[:, i % 2, :]
                if i >= 2:
                    dve.wait_ge(tp_full, n.tp - 1)
                do(V.tensor_reduce(sm[:, 0:1], ps[:, 4 + i % 2, :], AX_X, ALU.max))
                tell(V.tensor_scalar(sm[:, 1:2], sm[:, 0:1], -float(P) ** -0.5, None, ALU.mult), sem("at_max"))
                dve.wait_ge(sem("at_exp"), i + 1)
                do(V.reciprocal(sm[:, 3:4], sm[:, 2:3]))
                tell(V.tensor_scalar(prob[:, i % 2, :], prob[:, i % 2, :], sm[:, 3:4], None, ALU.mult), sem("at_prob"))
                n.tp += 1
            dve.wait_ge(sem("at_out"), 16)
            for b in range(4):
                tell(V.tensor_copy(hT[:, 2 * b:2 * b + 2, SEQ:NT], ps[:, b, :].rearrange("p (h t) -> p h t", h=2)), sem("at_outT"))
            n.block += 2
            update_and_norm()
            mlp(NFF, LAT, False, last=False)
            update_and_norm()

            dve.wait_ge(sem("sconv_w_loaded"), 16)
            for c in range(4):
                for q in range(2):
                    tell(V.tensor_copy(cv_b[:, q, :], gu_next()[:, 0:SEQ]), gu_evacuated)
                for q in range(2):
                    tell(V.tensor_copy(cv_g[:, q, :], gu_next()[:, 0:SEQ]), gu_evacuated)
                for q in range(2):
                    ch = 2 * c + q
                    tell(V.tensor_tensor(cv_g[:, q, :], cv_g[:, q, :], gu_next()[:, 0:SEQ], ALU.mult), gu_evacuated)
                    u, y = cv_g[:, q, :], cv_y[:, q, :]
                    do(V.tensor_scalar(y, u, w_sconv[:, ch, 2:3], None, ALU.mult))
                    do(V.scalar_tensor_tensor(out=y[:, 1:], in0=u[:, 0:SEQ - 1], scalar=w_sconv[:, ch, 1:2], in1=y[:, 1:],
                                              op0=ALU.mult, op1=ALU.add))
                    do(V.scalar_tensor_tensor(out=y[:, 2:], in0=u[:, 0:SEQ - 2], scalar=w_sconv[:, ch, 0:1], in1=y[:, 2:],
                                              op0=ALU.mult, op1=ALU.add))
                    tell(V.tensor_tensor(hT[:, ch, 0:SEQ], y, cv_b[:, q, :], ALU.mult), sem("sconv_ready"))
            n.block += 2
            update_and_norm()

            rounds_before = [0]

            def moe(l):
                dve.wait_ge(sem("route_w_ready"), l + 1)
                for t in range(2):
                    i = 2 * l + t
                    src = gu_next()
                    gl, el = rt[:, 0, 0:8], rt[:, 1, :]
                    el3 = el.rearrange("p (g e) -> p g e", g=8)
                    do(V.tensor_tensor(gl, src[:, 0:8], route_b[:, 0:8], ALU.add))
                    do(V.tensor_tensor(el, src[:, 8:72], route_b[:, 8:72], ALU.add))
                    do(V.tensor_reduce(rt1[:, 11:12], gl, AX_X, ALU.max))
                    do(V.tensor_scalar(rt[:, 2, 0:8], gl, rt1[:, 11:12], None, ALU.is_equal))
                    first_of(rt[:, 2, 0:8], rt[:, 3, 0:8])
                    do(V.tensor_scalar(rt[:, 3, 0:8], rt[:, 2, 0:8], -1.0, BIG, ALU.add, ALU.mult))
                    do(V.tensor_tensor(el3, el3, rt[:, 3, 0:8].rearrange("p (g o) -> p g o", o=1).broadcast_to([P, 8, 8]), ALU.add))
                    do(V.tensor_reduce(rt1[:, 12:13], el, AX_X, ALU.max))
                    do(V.tensor_scalar(rt[:, 4, :], el, rt1[:, 12:13], None, ALU.is_equal))
                    first_of(rt[:, 4, :], rt[:, 3, :])
                    do(V.tensor_copy(rt[:, 7, :], rt[:, 4, :]))
                    do(V.scalar_tensor_tensor(out=rt[:, 5, :], in0=rt[:, 4, :], scalar=-2 * BIG, in1=el, op0=ALU.mult, op1=ALU.add))
                    do(V.tensor_reduce(rt1[:, 13:14], rt[:, 5, :], AX_X, ALU.max))
                    do(V.tensor_scalar(rt[:, 6, :], rt[:, 5, :], rt1[:, 13:14], None, ALU.is_equal))
                    first_of(rt[:, 6, :], rt[:, 3, :])
                    do(V.tensor_tensor(rt1[:, 9:10], rt1[:, 13:14], rt1[:, 12:13], ALU.subtract))
                    tell(V.tensor_scalar(rt1[:, 0:8], gl, rt1[:, 11:12], None, ALU.subtract), sem("rt_shifted"))
                    dve.wait_ge(sem("rt_exp"), i + 1)
                    do(V.tensor_scalar(rt1[:, 10:11], rt1[:, 9:10], 1.0, None, ALU.add))
                    do(V.tensor_tensor(rt1[:, 10:11], rt1[:, 10:11], rt1[:, 8:9], ALU.mult))
                    do(V.reciprocal(rt1[:, 10:11], rt1[:, 10:11]))
                    do(V.tensor_tensor(rt1[:, 14:15], rt1[:, 10:11], rt1[:, 9:10], ALU.mult))
                    do(V.tensor_scalar(rt[:, 4, :], rt[:, 4, :], rt1[:, 10:11], None, ALU.mult))
                    do(V.scalar_tensor_tensor(out=moe_gates[:, t, 0:64], in0=rt[:, 6, :], scalar=rt1[:, 14:15], in1=rt[:, 4, :],
                                              op0=ALU.mult, op1=ALU.add))
                    tell(V.tensor_tensor(picked[:, t, :], rt[:, 6, :], rt[:, 7, :], ALU.add), sem("picked_ready"))
                    tell(V.tensor_copy(moe_gates[:, t, 65:66], moe_gates[:, t, 64:65]), gu_evacuated)
                mlp(2, LAT, True, last=False)
                dve.wait_ge(sem("ranks_summed"), l + 1)
                do(V.tensor_tensor(rank, ps[:, 4, 0:128].rearrange("p (t e) -> p t e", t=2), picked, ALU.mult))
                do(V.tensor_scalar(rank, rank, -1.0, None, ALU.add))
                do(V.tensor_reduce(over[:, 0:1], ps[:, 4, 128:192], AX_X, ALU.max))
                dve.wait_ge(sem("slot_constants_loaded"), 32 * (l + 1))
                do(V.tensor_scalar(over[:, 1:SEQ // CAP], round_limits, over[:, 0:1], None, ALU.is_lt))
                do(V.tensor_reduce(over[:, 0:1], over[:, 1:SEQ // CAP], AX_X, ALU.add))
                do(V.tensor_scalar(over[:, 0:1], over[:, 0:1], 1.0, None, ALU.add))
                tell(V.tensor_copy(rounds_i[:, :], over[:, 0:1]), sem("rounds_known"))
                rounds = dve.value_load(rounds_i[0:1, 0:1], min_val=1, max_val=SEQ // CAP)
                S = sem
                before = 0 if l == 0 else rounds_before[0] * QUADS
                rounds_before[0] = rounds
                if l == 0:
                    V.tensor_copy(note[:, :], eps_t[0:1, :]).then_inc(S("rounds_done"), 1)
                    dve.wait_ge(S("rounds_done"), 1)

                def one_round(c, ranks, q, main=False):
                    dve.wait_ge(S("ranks_picked"), q * 3 + (3 * QUADS * l + 3))
                    V.tensor_scalar(r_rank_x, r_rank_x, -float(CAP), None, ALU.add).then_inc(S("rank_lowered"), 1)
                    dve.wait_ge(S("rank_lowered"), c + 1)
                    dve.wait_ge(S("rounds_done"), c + 1)
                    V.tensor_tensor(sel.rearrange("p t (a s) -> p (t a) s", a=QUAD),
                                    slot_index.rearrange("p (o s) -> p o s", o=1).broadcast_to([P, 2 * QUAD, CAP]),
                                    ranks.rearrange("p t (a o) -> p (t a) o", o=1).broadcast_to([P, 2 * QUAD, CAP]),
                                    ALU.is_equal).then_inc(S("sel_ready"), 1)
                    dve.wait_ge(S("sel_ready"), c + 1)
                    V.tensor_tensor(sel_gated.rearrange("p t (a s) -> p (t a) s", a=QUAD),
                                    sel.rearrange("p t (a s) -> p (t a) s", a=QUAD),
                                    r_gate.rearrange("p t (a o) -> p (t a) o", o=1).broadcast_to([P, 2 * QUAD, CAP]),
                                    ALU.mult).then_inc(S("sel_gated_ready"), 1)
                    dve.wait_ge(S("gathered"), c + 1)
                    V.tensor_copy(x_slots[:, 4:8, :], ps[:, 5, :].rearrange("p (a b) -> p a b", a=4)).then_inc(S("x_slots_hi"), 1)
                    dve.wait_ge(S("quad_sig"), c + 1)
                    V.tensor_tensor(q_swish, ps[:, 6, 0:EH], q_sig, ALU.mult).then_inc(S("quad_swish"), 1)
                    dve.wait_ge(S("quad_swish"), c + 1)
                    V.tensor_tensor(q_hid, q_swish, ps[:, 6, EH:2 * EH], ALU.mult).then_inc(S("quad_hid"), 1)
                    if main:
                        V.tensor_copy(note[:, :], eps_t[0:1, :]).then_inc(S("quad_gate_up_used"), 1)
                        dve.wait_ge(S("quad_gate_up_used"), q + (QUADS * l + 1))
                    dve.wait_ge(S("quad_down"), c + 1)
                    V.tensor_copy(z_slots[:, 512:D], ps[:, 5, :]).then_inc(S("z_hi"), 1)
                    if main:
                        V.tensor_copy(note[:, :], eps_t[0:1, :]).then_inc(S("quad_down_used"), 1)
                        dve.wait_ge(S("quad_down_used"), q + (QUADS * l + 1))

                with dve.Fori(0, QUADS) as q:
                    V.tensor_copy(r_gate, moe_gates[:, :, bass.ds(q * QUAD, QUAD)]).then_inc(S("ranks_picked"), 1)
                    V.tensor_copy(r_rank, rank[:, :, bass.ds(q * QUAD, QUAD)]).then_inc(S("ranks_picked"), 1)
                    dve.wait_ge(S("ranks_picked"), q * 3 + (3 * QUADS * l + 2))
                    V.tensor_copy(r_rank_x, r_rank).then_inc(S("ranks_picked"), 1)
                    with dve.If(rounds > 1):
                        with dve.Fori(1, rounds) as r:
                            one_round(q * rounds + before + r - 1, r_rank_x, q)
                    one_round(q * rounds + before + rounds - 1, r_rank, q, True)
                n.block += 1

            def first_of(mask, w):
                do(V.tensor_tensor_scan(w, mask, mask, 0.0, ALU.add, ALU.max))
                do(V.tensor_scalar(w, w, 1.0, None, ALU.is_equal))
                do(V.tensor_tensor(mask, mask, w, ALU.mult))

            moe(0)
            update_and_norm()
            dve.wait_ge(sem("gdn_constants"), 16 * 6)
            dve.wait_ge(tp_evacuated, n.tp)
            for c in range(24):
                src, dst = gu_next(), gT[:, c, :]
                do(V.tensor_scalar(dst, src[:, 0:SEQ], w_gconv[:, c, 3:4], None, ALU.mult))
                for k in range(1, 4):
                    ins = V.scalar_tensor_tensor(out=dst[:, k:], in0=src[:, 0:SEQ - k], scalar=w_gconv[:, c, 3 - k:4 - k],
                                                 in1=dst[:, k:], op0=ALU.mult, op1=ALU.add)
                    if k < 3:
                        do(ins)
                    else:
                        tell(ins, gu_evacuated)
                tell(V.tensor_copy(note[:, :], eps_t[0:1, :]), sem("gd_pre"))
                dve.wait_ge(sem("gd_sig"), c + 1)
                tell(V.tensor_tensor(dst, dst, h[:, 0, 0:SEQ], ALU.mult), sem("gd_conv"))
            for half in range(2):
                for t in range(2):
                    src = gu_next()
                    gates_seen += 1
                    dve.wait_ge(sem("gate_sig"), gates_seen)
                    tell(V.tensor_tensor(g_z[:, t, 512 * half:512 * half + 512], src, junk[:, 0:512], ALU.mult), gu_evacuated)
            dve.wait_ge(sem("gd_ba"), 1)
            for t in range(2):
                col = slice(8 * t, 8 * t + 8)
                do(V.tensor_copy(g_t[:, 1, col], ps[:, t, 0:8]))
                do(V.tensor_tensor(g_t[:, 2, col], ps[:, t, 8:16], gdn_vec[:, 1, :], ALU.add))
            do(V.tensor_scalar(g_t[:, 3, :], g_t[:, 2, :], -1.0, None, ALU.mult))
            tell(V.tensor_tensor(g_t[:, 3, :], g_t[:, 3, :], g_t[:, 2, :], ALU.max), sem("gd_ba_read"))
            dve.wait_ge(sem("gd_act"), 1)
            do(V.scalar_tensor_tensor(out=g_t[:, 0, :], in0=g_t[:, 2, :], scalar=0.0, in1=g_t[:, 3, :], op0=ALU.max, op1=ALU.add))
            do(V.tensor_scalar(g_t[:, 0, :], g_t[:, 0, :], -1.0, None, ALU.mult))
            for t in range(2):
                col = slice(8 * t, 8 * t + 8)
                ins = V.tensor_tensor(g_t[:, 0, col], g_t[:, 0, col], gdn_vec[:, 2, :], ALU.mult)
                do(ins)
            tell(V.tensor_copy(note[:, :], eps_t[0:1, :]), sem("gd_decays"))
            n.tp += 12
            dve.wait_ge(tp_evacuated, n.tp)
            qn = [gtok[:, t, 0:8, :] for t in range(2)]
            kn = [gtok[:, t, 8:16, :] for t in range(2)]
            vn = [gtok[:, t, 16:24, :] for t in range(2)]

            def per_head(ap2):
                return ap2.rearrange("p (h o) -> p h o", o=1).broadcast_to([P, ap2.shape[1], P])

            for t in range(2):
                for i, xin in enumerate((qn[t], kn[t])):
                    do(V.tensor_tensor(g_sq, xin, xin, ALU.mult))
                    do(V.tensor_reduce(stat[:, i, :], g_sq, AX_X, ALU.add))
                tell(V.tensor_scalar(stat[:, 0:2, :], stat[:, 0:2, :], EPS, None, ALU.add), sem("gd_ms"))
                dve.wait_ge(sem("gd_rms"), t + 1)
                do(V.reciprocal(stat[:, 2:4, :], stat[:, 0:2, :]))
                do(V.tensor_scalar(stat[:, 2, :], stat[:, 2, :], float(P) ** -0.5, None, ALU.mult))
                do(V.tensor_tensor(qn[t], qn[t], per_head(stat[:, 2, :]), ALU.mult))
                do(V.tensor_tensor(kn[t], kn[t], per_head(stat[:, 3, :]), ALU.mult))
                do(V.tensor_tensor(vn[t], vn[t], per_head(g_t[:, 1, 8 * t:8 * t + 8]), ALU.mult))
                do(V.tensor_tensor(gkb[:, t], kn[t], per_head(g_t[:, 1, 8 * t:8 * t + 8]), ALU.mult))
            tell(V.tensor_copy(note[:, :], eps_t[0:1, :]), sem("gd_norm"))
            dve.wait_ge(sem("gd_sums"), 1)
            do(V.tensor_copy(g_t[:, 4, :], ps[:, 2, 0:16]))
            do(V.tensor_copy(g_t[:, 8, :], ps[:, 3, 0:16]))
            tell(V.tensor_tensor(g_t[:, 5, :], g_t[:, 8, :], g_t[:, 4, :], ALU.subtract), sem("gd_exparg"))
            dve.wait_ge(sem("gd_exp"), 1)
            n.tp += 12
            dve.wait_ge(tp_full, n.tp)
            do(V.tensor_tensor(g_kdec, kn[0], per_head(g_t[:, 7, 0:8]), ALU.mult))
            do(V.tensor_tensor(gkb[:, 1], gkb[:, 1], per_head(g_t[:, 6, 8:16]), ALU.mult))
            tell(V.tensor_tensor(qn[1], qn[1], per_head(g_t[:, 6, 8:16]), ALU.mult), sem("gd_qe"))
            n.tp += 2
            b4 = lambda bank: ps[:, bank, :].rearrange("p (a b) -> p a b", a=4)
            all4 = lambda m: m.rearrange("p (o b) -> p o b", o=1).broadcast_to([P, 4, P])
            for g in range(2):
                heads = slice(4 * g, 4 * g + 4)
                for t in range(2):
                    hs = slice(8 * t + 4 * g, 8 * t + 4 * g + 4)
                    tell(V.tensor_copy(TT[t], per_head(g_t[:, 0, hs])), sem("gd_gb"))
                for t in range(2):
                    hs = slice(8 * t + 4 * g, 8 * t + 4 * g + 4)
                    dve.wait_ge(sem("gd_scores"), 2 * g + t + 1)
                    do(V.tensor_tensor(LM[t], b4(0), per_head(g_t[:, 4, hs]), ALU.subtract))
                    tell(V.tensor_scalar(LM[t], LM[t], 0.0, None, ALU.min), sem("gd_gap"))
                    V.tensor_copy(DD[t], all4(ident[:, :])).then_inc(step, 1)
                    V.tensor_copy(DT_[t], all4(ident[:, :])).then_inc(step, 1)
                    tell.told[step.name] += 2
                    dve.wait_ge(sem("gd_dec"), 2 * g + t + 1)
                    do(V.tensor_tensor(LT[t], b4(1), LM[t], ALU.mult))
                    tell(V.tensor_tensor(AT[t], b4(2), LM[t], ALU.mult), sem("gd_scores_read"))
                    do(V.tensor_tensor(AT[t], AT[t], all4(s_le_t[:, :]), ALU.mult))
                for t in range(2):
                    V.tensor_tensor(LM[t], LT[t], all4(lv[:, 0, :]), ALU.mult).then_inc(sem("gd_lm"), 1)
                for lvl in range(LEVELS):
                    for t in range(2):
                        s0 = 2 * (LEVELS * g + lvl) + t
                        if lvl + 1 < LEVELS:
                            dve.wait_ge(sem("gd_t"), s0 + 1)
                            ins = V.tensor_tensor(LM[t], LT[t], all4(lv[:, lvl + 1, :]), ALU.mult)
                            do(ins)
                        dve.wait_ge(sem("gd_step"), s0 + 1)
                        V.tensor_tensor(DD[t], DD[t], b4(3 * t + 1), ALU.subtract).then_inc(step, 1)
                        tell.told[step.name] += 1
                        tell(V.tensor_tensor(DT_[t], DT_[t], b4(3 * t + 2), ALU.subtract), sem("gd_inverse"))
                        dve.wait_ge(step, tell.told[step.name])
                        if lvl + 1 < LEVELS:
                            V.tensor_copy(note[:, :], eps_t[0:1, :]).then_inc(sem("gd_lm"), 1)
                            dve.wait_ge(sem("gd_lm"), 2 * (LEVELS * g + lvl + 1) + t + 1)
                dve.wait_ge(sem("gd_u"), g + 1)
                tell(V.tensor_copy(U, b4(0)), sem("gd_u_read"))
                dve.wait_ge(sem("gd_w"), g + 1)
                do(V.tensor_copy(WT[:, 0:512], ps[:, 1, :]))
                dve.wait_ge(sem("gd_o"), 2 * g + 1)
                do(V.tensor_copy(g_o0[:, heads, :], b4(2)))
                tell(V.tensor_copy(gS, b4(3)), sem("gd_batch"))
                do(V.tensor_copy(U, b4(4)))
                dve.wait_ge(sem("gd_ws"), g + 1)
                tell(V.tensor_tensor(U, U, b4(5), ALU.subtract), sem("gd_vnew"))
                dve.wait_ge(sem("gd_o"), 2 * g + 2)
                tell(V.tensor_copy(g_o1[:, heads, :], b4(3)), sem("gd_batch"))
            for t, ot in enumerate((g_o0, g_o1)):
                do(V.tensor_tensor(g_sq, ot, ot, ALU.mult))
                do(V.tensor_reduce(stat[:, 0, :], g_sq, AX_X, ALU.add))
                tell(V.tensor_scalar(stat[:, 0, :], stat[:, 0, :], 1.0 / P, EPS, ALU.mult, ALU.add), sem("gd_oms"))
                dve.wait_ge(sem("gd_orms"), t + 1)
                do(V.reciprocal(stat[:, 1, :], stat[:, 0, :]))
                do(V.tensor_tensor(ot, ot, per_head(stat[:, 1, :]), ALU.mult))
                do(V.tensor_tensor(ot, ot, g_norm.rearrange("p (o b) -> p o b", o=1).broadcast_to([P, 8, P]), ALU.mult))
                tell(V.tensor_tensor(g_o[:, t, :], ot.rearrange("p a b -> p (a b)"), g_z[:, t, :], ALU.mult), h_ready)
                n.h += 1
                n.tp += 2
            n.block += 2
            update_and_norm()
            moe(1)
            update_tiles(LAT)


def kernel(**inputs):
    import numpy as _np
    import concourse.bacc as _bacc
    from concourse import mybir as _mybir
    from concourse.bass_utils import run_bass_kernel_spmd as _run

    nc = _bacc.Bacc("TRN2", target_bir_lowering=False, num_devices=1)
    arrays, args = {}, {}
    inputs = dict(inputs)
    lb = _np.asarray(inputs["hgrn_lb"])
    inputs["hgrn_lb"] = lb.reshape(2, 3, 4, P).transpose(3, 1, 0, 2)
    for name in ("ab_conv", "conv_w_2", "gdn_conv_w_2"):
        w = _np.asarray(inputs[name])[0]
        inputs[name] = w.reshape(w.shape[0], -1, P).transpose(2, 1, 0)
    for name, a in list(inputs.items()) + list(shape_constants().items()):
        a = _np.ascontiguousarray(a)
        arrays[f"in_{name}"] = a
        args[name] = nc.dram_tensor(f"in_{name}", a.shape, _mybir.dt.from_np(a.dtype), kind="ExternalInput").ap()
    out = nc.dram_tensor("out_0", (1, SEQ, D), F32, kind="ExternalOutput").ap()
    build(nc, args, out)
    r = _run(nc, [arrays], core_ids=[0])
    return r.results[0]["out_0"]
```
